# Optimizing a Trainium2 kernel written in Bass

```python
import math
import jax, jax.numpy as jnp
from jax import lax
import numpy as np

D_MODEL = 1024
BATCH = 1
SEQ = 512
DEPTH = 2

MIX_WIDTH = 2 * D_MODEL
RET_WIDTH = MIX_WIDTH // 4
SSD_WIDTH = MIX_WIDTH // 2
FOX_WIDTH = MIX_WIDTH // 4
RET_HEAD_DIM = 128
RET_HEADS = RET_WIDTH // RET_HEAD_DIM
SSD_HEAD_DIM = 64
SSD_HEADS = SSD_WIDTH // SSD_HEAD_DIM
SSD_GROUPS = 2
SSD_STATE = 128
CONV_K = 4
CONV_DIM = SSD_WIDTH + 2 * SSD_GROUPS * SSD_STATE
FOX_HEAD_DIM = 64
FOX_HEADS = FOX_WIDTH // FOX_HEAD_DIM
CHUNK = 128
Q_BLOCK = 128
ROPE_BASE = 10000.0
EPS = 1e-6

IN_SIZES = (RET_WIDTH, RET_WIDTH, RET_WIDTH, RET_WIDTH,
            CONV_DIM, SSD_HEADS, SSD_WIDTH,
            FOX_WIDTH, FOX_WIDTH, FOX_WIDTH, FOX_WIDTH,
            FOX_HEADS)
N_IN = sum(IN_SIZES)
IN_OFFSETS = tuple(int(v) for v in np.cumsum(IN_SIZES)[:-1])


def _rmsnorm(t, gain=None):
    t32 = t.astype(jnp.float32)
    t32 = t32 * lax.rsqrt(jnp.mean(t32 * t32, axis=-1, keepdims=True) + EPS)
    if gain is not None:
        t32 = t32 * gain.astype(jnp.float32)
    return t32.astype(t.dtype)

def _rotary(t, positions):
    half = t.shape[-1] // 2
    freq = ROPE_BASE ** (-jnp.arange(half, dtype=jnp.float32) / half)
    ang = positions.astype(jnp.float32)[..., None] * freq
    cos = jnp.cos(ang)[:, :, None, :]
    sin = jnp.sin(ang)[:, :, None, :]
    t1 = t[..., :half].astype(jnp.float32)
    t2 = t[..., half:].astype(jnp.float32)
    return jnp.concatenate([t1 * cos - t2 * sin, t1 * sin + t2 * cos], axis=-1).astype(t.dtype)

def _retention(q, k, v, positions):
    b, L, H, dh = q.shape
    n = L // CHUNK
    q = _rotary(q, positions)
    k = _rotary(k, positions) * (dh ** -0.5)
    log_g = jnp.log(1.0 - 2.0 ** (-5.0 - jnp.arange(H, dtype=jnp.float32)))
    idx = jnp.arange(CHUNK, dtype=jnp.float32)
    diff = idx[:, None] - idx[None, :]
    decay_intra = jnp.where(diff >= 0, jnp.exp(log_g[:, None, None] * jnp.maximum(diff, 0.0)), 0.0)
    decay_q = jnp.exp(log_g[:, None] * (idx + 1.0))
    decay_k = jnp.exp(log_g[:, None] * (CHUNK - 1.0 - idx))
    decay_chunk = jnp.exp(log_g * CHUNK)

    def to_chunks(t):
        return t.reshape(b, n, CHUNK, H, dh).transpose(1, 0, 3, 2, 4)

    def step(S, inp):
        qc, kc, vc = inp
        s = jnp.einsum('bhid,bhjd->bhij', qc, kc) * decay_intra
        o = (jnp.einsum('bhij,bhjd->bhid', s, vc)
             + jnp.einsum('bhid,bhde->bhie', qc, S) * decay_q[:, :, None])
        S = S * decay_chunk[:, None, None] + jnp.einsum('bhjd,hj,bhje->bhde', kc, decay_k, vc)
        return S, o

    S0 = jnp.zeros((b, H, dh, dh), jnp.float32)
    _, o = lax.scan(step, S0, (to_chunks(q), to_chunks(k), to_chunks(v)))
    o = o.transpose(1, 0, 3, 2, 4).reshape(b, L, H, dh)
    return _rmsnorm(o).astype(v.dtype)

def _ssd(xs, dt, A, Bm, Cm):
    b, L, H, P = xs.shape
    G, N = Bm.shape[2], Bm.shape[3]
    hpg = H // G
    n = L // CHUNK
    a = (dt * A).astype(jnp.float32)
    xdt = xs * dt[..., None]
    xc_all = xdt.reshape(b, n, CHUNK, G, hpg, P).transpose(1, 0, 2, 3, 4, 5)
    a_all = a.reshape(b, n, CHUNK, G, hpg).transpose(1, 0, 3, 4, 2)
    b_all = Bm.reshape(b, n, CHUNK, G, N).transpose(1, 0, 2, 3, 4)
    c_all = Cm.reshape(b, n, CHUNK, G, N).transpose(1, 0, 2, 3, 4)
    causal = jnp.tril(jnp.ones((CHUNK, CHUNK), dtype=bool))

    def step(S, inp):
        xc, ac, bc, cc = inp
        acum = jnp.cumsum(ac, axis=-1)
        seg = acum[..., :, None] - acum[..., None, :]
        Lm = jnp.exp(jnp.where(causal, seg, -jnp.inf))
        cb = jnp.einsum('bign,bjgn->bgij', cc, bc)
        y = jnp.einsum('bgij,bghij,bjghp->bighp', cb, Lm, xc)
        y = y + jnp.einsum('bign,bghpn,bghi->bighp', cc, S, jnp.exp(acum))
        last = acum[..., -1:]
        S = (S * jnp.exp(last)[..., None]
             + jnp.einsum('bjgn,bghj,bjghp->bghpn', bc, jnp.exp(last - acum), xc))
        return S, y

    S0 = jnp.zeros((b, G, hpg, P, N), jnp.float32)
    _, y = lax.scan(step, S0, (xc_all, a_all, b_all, c_all))
    return y.transpose(1, 0, 2, 3, 4, 5).reshape(b, L, H, P)

def _causal_dwconv(u, w, bias):
    out = lax.conv_general_dilated(
        u, w[:, None, :].astype(u.dtype), window_strides=(1,), padding=[(CONV_K - 1, 0)],
        dimension_numbers=('NWC', 'WIO', 'NWC'), feature_group_count=u.shape[-1])
    return out + bias

def _forgetting_attention(q, k, v, log_f):
    b, L, H, dh = q.shape
    nb = L // Q_BLOCK
    Ft = jnp.cumsum(log_f.astype(jnp.float32), axis=1).transpose(0, 2, 1)
    q_blocks = q.reshape(b, nb, Q_BLOCK, H, dh).transpose(1, 0, 2, 3, 4)
    f_blocks = Ft.reshape(b, H, nb, Q_BLOCK).transpose(2, 0, 1, 3)
    kpos = jnp.arange(L)
    scale = dh ** -0.5

    def block(inp):
        qi, fi, i = inp
        s = jnp.einsum('bqhd,bkhd->bhqk', qi, k).astype(jnp.float32) * scale
        s = s + fi[..., None] - Ft[:, :, None, :]
        qpos = i * Q_BLOCK + jnp.arange(Q_BLOCK)
        s = jnp.where(qpos[:, None] >= kpos[None, :], s, -jnp.inf)
        p = jax.nn.softmax(s, axis=-1)
        return jnp.einsum('bhqk,bkhd->bqhd', p.astype(v.dtype), v)

    o = lax.map(block, (q_blocks, f_blocks, jnp.arange(nb)))
    return o.transpose(1, 0, 2, 3, 4).reshape(b, L, H, dh)

def _layer(x, c, positions, norm_g, w_ada, b_ada, w_in, conv_w, conv_b,
           dt_bias, a_log, d_skip, ssd_norm_g, b_forget, w_out):
    b, L, _ = x.shape
    mod = jax.nn.silu(c) @ w_ada + b_ada
    shift, scale, gate = jnp.split(mod, 3, axis=-1)
    h = _rmsnorm(x, norm_g) * (1.0 + scale[:, None, :]) + shift[:, None, :]

    proj = h @ w_in
    (rq, rk, rv, rg, xbc, dt_raw, z, fq, fk, fv, fg, f_raw) = jnp.split(proj, IN_OFFSETS, axis=-1)

    ret = _retention(rq.reshape(b, L, RET_HEADS, RET_HEAD_DIM),
                     rk.reshape(b, L, RET_HEADS, RET_HEAD_DIM),
                     rv.reshape(b, L, RET_HEADS, RET_HEAD_DIM), positions)
    ret = ret.reshape(b, L, RET_WIDTH) * jax.nn.silu(rg)

    xbc = jax.nn.silu(_causal_dwconv(xbc, conv_w, conv_b))
    xs, Bm, Cm = jnp.split(xbc, (SSD_WIDTH, SSD_WIDTH + SSD_GROUPS * SSD_STATE), axis=-1)
    xs = xs.reshape(b, L, SSD_HEADS, SSD_HEAD_DIM)
    Bm = Bm.reshape(b, L, SSD_GROUPS, SSD_STATE)
    Cm = Cm.reshape(b, L, SSD_GROUPS, SSD_STATE)
    dt = jax.nn.softplus(dt_raw + dt_bias)
    A = -jnp.exp(a_log.astype(jnp.float32))
    y = _ssd(xs, dt, A, Bm, Cm) + d_skip[:, None] * xs
    ssd = _rmsnorm(y.reshape(b, L, SSD_WIDTH).astype(x.dtype) * jax.nn.silu(z), ssd_norm_g)

    log_f = jax.nn.log_sigmoid((f_raw + b_forget).astype(jnp.float32))
    fox = _forgetting_attention(fq.reshape(b, L, FOX_HEADS, FOX_HEAD_DIM),
                                fk.reshape(b, L, FOX_HEADS, FOX_HEAD_DIM),
                                fv.reshape(b, L, FOX_HEADS, FOX_HEAD_DIM), log_f)
    fox = fox.reshape(b, L, FOX_WIDTH) * jax.nn.silu(fg)

    mixed = jnp.concatenate([ret.astype(x.dtype), ssd.astype(x.dtype), fox.astype(x.dtype)], axis=-1)
    out = mixed @ w_out
    return x + gate[:, None, :] * out

def first_inputs(seed: int = 0) -> dict:
    key = jax.random.key(seed)
    ks = jax.random.split(key, 16)
    f32 = jnp.float32
    x = jax.random.normal(ks[0], (BATCH, SEQ, D_MODEL), f32)
    c = jax.random.normal(ks[1], (BATCH, D_MODEL), f32)
    offsets = jax.random.randint(ks[2], (BATCH, 1), 0, 4096, dtype=jnp.int32)
    positions = (jnp.arange(SEQ, dtype=jnp.int32)[None, :] + offsets).astype(jnp.int32)
    norm_g = 1.0 + 0.02 * jax.random.normal(ks[3], (DEPTH, D_MODEL), f32)
    w_ada = 0.5 * D_MODEL ** -0.5 * jax.random.normal(ks[4], (DEPTH, D_MODEL, 3 * D_MODEL), f32)
    b_ada = 0.02 * jax.random.normal(ks[5], (DEPTH, 3 * D_MODEL), f32)
    w_in = D_MODEL ** -0.5 * jax.random.normal(ks[6], (DEPTH, D_MODEL, N_IN), f32)
    conv_w = CONV_K ** -0.5 * jax.random.normal(ks[7], (DEPTH, CONV_K, CONV_DIM), f32)
    conv_b = 0.02 * jax.random.normal(ks[8], (DEPTH, CONV_DIM), f32)
    dt0 = jnp.exp(jax.random.uniform(ks[9], (DEPTH, SSD_HEADS), f32, math.log(1e-3), math.log(1e-1)))
    dt_bias = dt0 + jnp.log(-jnp.expm1(-dt0))
    a_log = jnp.log(jax.random.uniform(ks[10], (DEPTH, SSD_HEADS), f32, 1.0, 16.0))
    d_skip = 1.0 + 0.1 * jax.random.normal(ks[11], (DEPTH, SSD_HEADS), f32)
    ssd_norm_g = 1.0 + 0.02 * jax.random.normal(ks[12], (DEPTH, SSD_WIDTH), f32)
    b_forget = jax.random.uniform(ks[13], (DEPTH, FOX_HEADS), f32, 2.0, 5.0)
    w_out = MIX_WIDTH ** -0.5 * jax.random.normal(ks[14], (DEPTH, MIX_WIDTH, D_MODEL), f32)
    final_g = 1.0 + 0.02 * jax.random.normal(ks[15], (D_MODEL,), f32)
    return {"x": x, "c": c, "positions": positions, "norm_g": norm_g, "w_ada": w_ada,
            "b_ada": b_ada, "w_in": w_in, "conv_w": conv_w, "conv_b": conv_b,
            "dt_bias": dt_bias, "a_log": a_log, "d_skip": d_skip, "ssd_norm_g": ssd_norm_g,
            "b_forget": b_forget, "w_out": w_out, "final_g": final_g}

def first_block(x, c, positions, norm_g, w_ada, b_ada, w_in, conv_w, conv_b,
              dt_bias, a_log, d_skip, ssd_norm_g, b_forget, w_out, final_g):
    for layer in range(DEPTH):
        x = _layer(x, c, positions, norm_g[layer], w_ada[layer], b_ada[layer], w_in[layer],
                   conv_w[layer], conv_b[layer], dt_bias[layer], a_log[layer], d_skip[layer],
                   ssd_norm_g[layer], b_forget[layer], w_out[layer])
    return _rmsnorm(x, final_g)


D_MIX = D_MODEL
D_FF = 2816
NSA_HEADS = 8
NSA_KV_GROUPS = 2
NSA_HEAD_DIM = 64
NSA_GROUP_SIZE = NSA_HEADS // NSA_KV_GROUPS
NSA_OUT = NSA_HEADS * NSA_HEAD_DIM
NSA_KV_DIM = NSA_KV_GROUPS * NSA_HEAD_DIM
CMP_BLOCK = 32
CMP_STRIDE = 16
SLC_BLOCK = 64
SLC_TOPK = 8
WINDOW = 512
POOL_WINDOWS = (2, 4, 8, 16)
POOL_GROUPS = 4
POOL_GROUP_DIM = 64
POOL_DIM = POOL_GROUPS * POOL_GROUP_DIM
GLA_HEADS = 4
GLA_KEY_DIM = 32
GLA_VAL_DIM = 64
GLA_GATE_RANK = 16
GLA_TAU = 16.0
GLA_CHUNK = 64
GLA_QK = GLA_HEADS * GLA_KEY_DIM
GLA_OUT = GLA_HEADS * GLA_VAL_DIM
IN_SPLITS = (NSA_OUT, NSA_KV_DIM, NSA_KV_DIM, NSA_KV_DIM, NSA_KV_DIM, NSA_KV_DIM, NSA_KV_DIM,
             3 * NSA_HEADS, POOL_DIM, GLA_QK, GLA_QK, GLA_OUT, GLA_GATE_RANK, GLA_OUT)
D_IN = NSA_OUT + 6 * NSA_KV_DIM + 3 * NSA_HEADS + POOL_DIM + 2 * GLA_QK + 2 * GLA_OUT + GLA_GATE_RANK
ALPHA = (2.0 * DEPTH) ** 0.25
BETA = (8.0 * DEPTH) ** -0.25
LN_EPS = 1e-5
RMS_EPS = 1e-6


def layer_norm(x, g, b):
    xf = x.astype(jnp.float32)
    mu = jnp.mean(xf, axis=-1, keepdims=True)
    var = jnp.mean(jnp.square(xf - mu), axis=-1, keepdims=True)
    y = (xf - mu) * lax.rsqrt(var + LN_EPS)
    return (y * g + b).astype(x.dtype)

def swiglu(x, wg, wu, wd):
    return (jax.nn.silu(x @ wg) * (x @ wu)) @ wd

def masked_softmax(s, mask):
    s = jnp.where(mask, s.astype(jnp.float32), -jnp.inf)
    m = jnp.max(s, axis=-1, keepdims=True)
    m = jnp.where(jnp.isfinite(m), m, 0.0)
    e = jnp.exp(s - m)
    d = jnp.sum(e, axis=-1, keepdims=True)
    return e / jnp.where(d > 0, d, 1.0)

def compress_tokens(z, pe, w1, w2):
    B, S, G, D = z.shape
    chunks = z.reshape(B, S // CMP_STRIDE, CMP_STRIDE, G, D)
    blocks = jnp.concatenate([chunks[:, :-1], chunks[:, 1:]], axis=2)
    blocks = blocks + pe[None, None, :, None, :]
    flat = jnp.transpose(blocks, (0, 1, 3, 2, 4)).reshape(B, -1, G, CMP_BLOCK * D)
    return jax.nn.gelu(flat @ w1) @ w2

def nsa_mixer(q, kc_raw, vc_raw, ks, vs, kw, vw, gates, pe_k, w1_k, w2_k, pe_v, w1_v, w2_v):
    B, S = q.shape[:2]
    G, R, HD = NSA_KV_GROUPS, NSA_GROUP_SIZE, NSA_HEAD_DIM
    q = q.reshape(B, S, G, R, HD) * (HD ** -0.5)
    kc = compress_tokens(kc_raw, pe_k, w1_k, w2_k)
    vc = compress_tokens(vc_raw, pe_v, w1_v, w2_v)
    n_cmp = kc.shape[1]
    cmp_end = jnp.arange(n_cmp) * CMP_STRIDE + CMP_BLOCK - 1
    n_slc = S // SLC_BLOCK
    topk = min(SLC_TOPK, n_slc)
    c_start = jnp.arange(n_cmp)[:, None] * CMP_STRIDE
    s_start = jnp.arange(n_slc)[None, :] * SLC_BLOCK
    overlap = ((c_start <= s_start + SLC_BLOCK - 1) & (c_start + CMP_BLOCK - 1 >= s_start)).astype(jnp.float32)
    ks_blk = jnp.transpose(ks.reshape(B, n_slc, SLC_BLOCK, G, HD), (0, 3, 1, 2, 4))
    vs_blk = jnp.transpose(vs.reshape(B, n_slc, SLC_BLOCK, G, HD), (0, 3, 1, 2, 4))
    pad = ((0, 0), (WINDOW, 0), (0, 0), (0, 0))
    kw_pad = jnp.pad(kw, pad)
    vw_pad = jnp.pad(vw, pad)
    n_qb = S // Q_BLOCK
    q_blocks = jnp.swapaxes(q.reshape(B, n_qb, Q_BLOCK, G, R, HD), 0, 1)
    g_blocks = jnp.swapaxes(gates.reshape(B, n_qb, Q_BLOCK, G, R, 3), 0, 1)
    blk_ids = jnp.arange(n_slc)
    gather = jax.vmap(jax.vmap(lambda kb, ix: kb[ix]))

    def one_block(args):
        qi, qb, gb = args
        t = qi * Q_BLOCK + jnp.arange(Q_BLOCK)
        s_c = jnp.einsum('bqgrd,bngd->bgrqn', qb, kc)
        p_c = masked_softmax(s_c, cmp_end[None, :] <= t[:, None])
        o_c = jnp.einsum('bgrqn,bngd->bqgrd', p_c.astype(vc.dtype), vc)
        imp = jnp.einsum('bgrqn,nm->bgqm', p_c, overlap)
        cur = (t // SLC_BLOCK)[:, None]
        forced = (blk_ids == 0) | (blk_ids == cur) | (blk_ids == cur - 1)
        future = blk_ids[None, :] * SLC_BLOCK > t[:, None]
        imp = jnp.where(forced, jnp.inf, jnp.where(future, -jnp.inf, imp))
        _, sel = lax.top_k(imp, topk)
        k_sel = gather(ks_blk, sel).reshape(B, G, Q_BLOCK, topk * SLC_BLOCK, HD)
        v_sel = gather(vs_blk, sel).reshape(B, G, Q_BLOCK, topk * SLC_BLOCK, HD)
        kpos = (sel[..., None] * SLC_BLOCK + jnp.arange(SLC_BLOCK)).reshape(B, G, Q_BLOCK, topk * SLC_BLOCK)
        s_s = jnp.einsum('bqgrd,bgqkd->bgrqk', qb, k_sel)
        p_s = masked_softmax(s_s, (kpos <= t[:, None])[:, :, None])
        o_s = jnp.einsum('bgrqk,bgqkd->bqgrd', p_s.astype(v_sel.dtype), v_sel)
        start = qi * Q_BLOCK
        k_win = lax.dynamic_slice_in_dim(kw_pad, start, Q_BLOCK + WINDOW, axis=1)
        v_win = lax.dynamic_slice_in_dim(vw_pad, start, Q_BLOCK + WINDOW, axis=1)
        kp = start - WINDOW + jnp.arange(Q_BLOCK + WINDOW)
        mask_w = (kp[None, :] <= t[:, None]) & (kp[None, :] > t[:, None] - WINDOW) & (kp[None, :] >= 0)
        s_w = jnp.einsum('bqgrd,bkgd->bgrqk', qb, k_win)
        p_w = masked_softmax(s_w, mask_w)
        o_w = jnp.einsum('bgrqk,bkgd->bqgrd', p_w.astype(v_win.dtype), v_win)
        o = gb[..., 0:1] * o_c + gb[..., 1:2] * o_s + gb[..., 2:3] * o_w
        return o.reshape(B, Q_BLOCK, G * R * HD)

    out = lax.map(one_block, (jnp.arange(n_qb), q_blocks, g_blocks))
    return jnp.swapaxes(out, 0, 1).reshape(B, S, NSA_OUT)

def pool_mixer(u, pool_w, pool_scale):
    B, S, _ = u.shape
    uf = u.astype(jnp.float32).reshape(B, S, POOL_GROUPS, POOL_GROUP_DIM)
    c = jnp.pad(jnp.cumsum(uf, axis=1), ((0, 0), (1, 0), (0, 0), (0, 0)))
    t = jnp.arange(S)
    means = []
    for gi, w in enumerate(POOL_WINDOWS):
        cg = c[:, :, gi]
        lower = jnp.pad(cg, ((0, 0), (w, 0), (0, 0)))[:, 1:S + 1]
        cnt = jnp.minimum(w, t + 1).astype(jnp.float32)[None, :, None]
        means.append((cg[:, 1:] - lower) / cnt)
    pooled = (jnp.stack(means, axis=2) - uf).astype(u.dtype)
    y = jnp.einsum('bsgc,gcd->bsgd', pooled, pool_w).reshape(B, S, POOL_DIM)
    return y * pool_scale

def gla_mixer(q, k, v, a_lr, r, wa2, ba, norm_g):
    B, S = q.shape[:2]
    H, DK, DV, C = GLA_HEADS, GLA_KEY_DIM, GLA_VAL_DIM, GLA_CHUNK
    nc = S // C
    log_a = jax.nn.log_sigmoid((a_lr @ wa2 + ba).astype(jnp.float32)) / GLA_TAU
    qf = q.astype(jnp.float32).reshape(B, nc, C, H, DK) * (DK ** -0.5)
    kf = k.astype(jnp.float32).reshape(B, nc, C, H, DK)
    vf = v.astype(jnp.float32).reshape(B, nc, C, H, DV)
    b = jnp.cumsum(log_a.reshape(B, nc, C, H, DK), axis=2)
    b_last = b[:, :, -1:]
    q_t = qf * jnp.exp(b)
    k_t = kf * jnp.exp(-b)
    causal = jnp.tril(jnp.ones((C, C), dtype=bool))
    A = jnp.where(causal, jnp.einsum('bnihk,bnjhk->bnhij', q_t, k_t), 0.0)
    o_intra = jnp.einsum('bnhij,bnjhv->bnihv', A, vf)
    dS = jnp.einsum('bnjhk,bnjhv->nbhkv', kf * jnp.exp(b_last - b), vf)
    decay = jnp.swapaxes(jnp.exp(b_last[:, :, 0]), 0, 1)

    def step(state, inp):
        d, ds = inp
        return d[..., None] * state + ds, state

    _, s_in = lax.scan(step, jnp.zeros((B, H, DK, DV), jnp.float32), (decay, dS))
    o_inter = jnp.einsum('bnihk,nbhkv->bnihv', q_t, s_in)
    o = (o_intra + o_inter).reshape(B, S, H, DV)
    o = o * lax.rsqrt(jnp.mean(jnp.square(o), axis=-1, keepdims=True) + RMS_EPS)
    o = o.reshape(B, S, GLA_OUT) * norm_g
    return (o * jax.nn.silu(r.astype(jnp.float32))).astype(q.dtype)

def token_mix(x, w_in, w_out, cmp_pe, cmp_w1, cmp_w2, pool_w, pool_scale, gla_wa2, gla_ba, gla_norm_g):
    B, S, _ = x.shape
    h = x @ w_in
    split_pts = np.cumsum(IN_SPLITS)[:-1].tolist()
    (nq, kc, vc, ks, vs, kw, vw, gl, u, gq, gk, gv, ga, gr) = jnp.split(h, split_pts, axis=-1)
    kv = lambda z: z.reshape(B, S, NSA_KV_GROUPS, NSA_HEAD_DIM)
    gates = jax.nn.sigmoid(gl).reshape(B, S, NSA_HEADS, 3)
    o_a = nsa_mixer(nq, kv(kc), kv(vc), kv(ks), kv(vs), kv(kw), kv(vw), gates,
                    cmp_pe[0], cmp_w1[0], cmp_w2[0], cmp_pe[1], cmp_w1[1], cmp_w2[1])
    o_b = pool_mixer(u, pool_w, pool_scale)
    o_c = gla_mixer(gq, gk, gv, ga, gr, gla_wa2, gla_ba, gla_norm_g)
    return jnp.concatenate([o_a, o_b, o_c], axis=-1) @ w_out

def second_inputs(seed: int = 0) -> dict:
    key = jax.random.key(seed)
    ks = jax.random.split(key, 16)
    nrm = lambda k, shape, s: jax.random.normal(k, shape, jnp.float32) * s
    L = DEPTH
    return {
        "x": nrm(ks[0], (BATCH, SEQ, D_MODEL), 1.0),
        "ln_g": 1.0 + nrm(ks[1], (L, 3, D_MODEL), 0.05),
        "ln_b": nrm(ks[2], (L, 3, D_MODEL), 0.01),
        "ffn_wg": nrm(ks[3], (L, 2, D_MODEL, D_FF), D_MODEL ** -0.5),
        "ffn_wu": nrm(ks[4], (L, 2, D_MODEL, D_FF), D_MODEL ** -0.5),
        "ffn_wd": nrm(ks[5], (L, 2, D_FF, D_MODEL), BETA * D_FF ** -0.5),
        "w_in": nrm(ks[6], (L, D_MODEL, D_IN), D_MODEL ** -0.5),
        "w_out": nrm(ks[7], (L, D_MIX, D_MODEL), BETA * D_MIX ** -0.5),
        "cmp_pe": nrm(ks[8], (L, 2, CMP_BLOCK, NSA_HEAD_DIM), 0.1),
        "cmp_w1": nrm(ks[9], (L, 2, CMP_BLOCK * NSA_HEAD_DIM, NSA_HEAD_DIM), (CMP_BLOCK * NSA_HEAD_DIM) ** -0.5),
        "cmp_w2": nrm(ks[10], (L, 2, NSA_HEAD_DIM, NSA_HEAD_DIM), NSA_HEAD_DIM ** -0.5),
        "pool_w": nrm(ks[11], (L, POOL_GROUPS, POOL_GROUP_DIM, POOL_GROUP_DIM), POOL_GROUP_DIM ** -0.5),
        "pool_scale": 1.0 + nrm(ks[12], (L, POOL_DIM), 0.1),
        "gla_wa2": nrm(ks[13], (L, GLA_GATE_RANK, GLA_QK), GLA_GATE_RANK ** -0.5),
        "gla_ba": nrm(ks[14], (L, GLA_QK), 0.1),
        "gla_norm_g": 1.0 + nrm(ks[15], (L, GLA_OUT), 0.05),
    }

def second_block(x, ln_g, ln_b, ffn_wg, ffn_wu, ffn_wd, w_in, w_out, cmp_pe, cmp_w1, cmp_w2,
              pool_w, pool_scale, gla_wa2, gla_ba, gla_norm_g):
    for l in range(DEPTH):
        x = layer_norm(ALPHA * x + 0.5 * swiglu(x, ffn_wg[l, 0], ffn_wu[l, 0], ffn_wd[l, 0]), ln_g[l, 0], ln_b[l, 0])
        m = token_mix(x, w_in[l], w_out[l], cmp_pe[l], cmp_w1[l], cmp_w2[l], pool_w[l], pool_scale[l],
                      gla_wa2[l], gla_ba[l], gla_norm_g[l])
        x = layer_norm(ALPHA * x + m, ln_g[l, 1], ln_b[l, 1])
        x = layer_norm(ALPHA * x + 0.5 * swiglu(x, ffn_wg[l, 1], ffn_wu[l, 1], ffn_wd[l, 1]), ln_g[l, 2], ln_b[l, 2])
    return x


def setup_inputs(seed=0):
    out = dict(first_inputs(seed))
    for name, value in second_inputs(seed + 1).items():
        if name != "x":
            out[name + "_2"] = value
    return out


def reference(
    x, c, positions, norm_g, w_ada, b_ada, w_in, conv_w, conv_b, dt_bias, a_log, d_skip,
    ssd_norm_g, b_forget, w_out, final_g, ln_g_2, ln_b_2, ffn_wg_2, ffn_wu_2, ffn_wd_2, w_in_2,
    w_out_2, cmp_pe_2, cmp_w1_2, cmp_w2_2, pool_w_2, pool_scale_2, gla_wa2_2, gla_ba_2,
    gla_norm_g_2,
):
    x = first_block(
        x, c, positions, norm_g, w_ada, b_ada, w_in, conv_w, conv_b, dt_bias, a_log, d_skip,
        ssd_norm_g, b_forget, w_out, final_g,
    )
    return second_block(
        x, ln_g_2, ln_b_2, ffn_wg_2, ffn_wu_2, ffn_wd_2, w_in_2, w_out_2, cmp_pe_2, cmp_w1_2,
        cmp_w2_2, pool_w_2, pool_scale_2, gla_wa2_2, gla_ba_2, gla_norm_g_2,
    )


_drawn_inputs = setup_inputs


def setup_inputs(seed=0):
    import zlib

    import numpy as np

    out = dict(_drawn_inputs(seed))
    spreads = {}
    factors = {'norm_g': 5.457,
     'conv_b': 6.82,
     'd_skip': 114.6,
     'ssd_norm_g': 8.0,
     'b_forget': 3.563,
     'final_g': 2.686,
     'cmp_pe_2': 5.096,
     'gla_wa2_2': 3.189,
     'gla_ba_2': 8.0,
     'gla_norm_g_2': 7.535}
    for name, (base, spread) in spreads.items():
        noise = np.random.default_rng([zlib.crc32(name.encode()), seed]).standard_normal(out[name].shape)
        drawn = base * np.exp(spread * noise) if base else spread * noise
        out[name] = __import__('jax').numpy.asarray(drawn.astype(out[name].dtype))
    for name, factor in factors.items():
        out[name] = (out[name] * factor).astype(out[name].dtype)
    return out
```

```python
from contextlib import ExitStack

import numpy as np

import concourse.bass as bass
from concourse import mybir
from concourse.alu_op_type import AluOpType as ALU

F32 = mybir.dt.float32
I32 = mybir.dt.int32
ACT = mybir.ActivationFunctionType
AX = mybir.AxisListType

P = 128
T = 512
NT = T // P
D = 1024
KD = D // P
DEPTH = 2
UC = 256
UNIT = KD * UC
SLOTS = 4
BIG = 1.0e30
ARENA = 24340
EPS = 1e-6
LN_EPS = 1e-5

RH = 4
SH, SP, SG, SN = 16, 64, 2, 128
HG = SH // SG
CONV_K = 4
FH, FD = 8, 64
MIX1 = 2048
FF = 2816
KF = FF // P
NH, NG, HD = 8, 2, 64
CB, CS = 32, 16
NCMP = T // CS - 1
GH, GK, GV, GC = 4, 32, 64, 64
NGC = T // GC
ALPHA = (2.0 * DEPTH) ** 0.25

P1 = dict(norm_g=(0, 8), b_ada=(8, 32), conv_w=(32, 80), conv_b=(80, 92), ssd_g=(92, 100),
          dtf_b=(100, 124), a_log=(124, 140), d_skip=(140, 156))
P1N = 156
P2 = dict(ln_g=(0, 24), ln_b=(24, 48), pool_s=(48, 50), gla_ba=(50, 51), gla_g=(51, 53))
P2N = 53
C0 = dict(ident=(0, 128), ones=(128, 256), triu=(256, 384), causal=(384, 896), freq=(896, 897),
          sign=(897, 898), zero=(898, 899))
C0N = 899
C1 = dict(decayT=(0, 512), decq=(512, 1024), deck=(1024, 1028))
C1N = 1028
C2 = dict(reset=(0, 512), invcnt=(512, 1536), cmpadd=(1536, 1664), cmpmul=(1664, 1792),
          gmask=(1792, 2048))
C2N = 2048
CN = 2052


def split3(ap, a):
    return ap.rearrange("p (a b) -> p a b", a=a)


def spread(ap, n):
    return ap.unsqueeze(2).broadcast_to([ap.shape[0], ap.shape[1], n])


def repeat(ap, n):
    return ap.unsqueeze(1).broadcast_to([ap.shape[0], n, ap.shape[1]])


class Stream:

    def __init__(self, loaded):
        self.loaded = loaded
        self.units = []
        self.sent = 0

    def add(self, source, n, sem, value):
        self.units.append((source, n, sem, value))
        return len(self.units) - 1

    def send(self, sp, w, upto):
        while self.sent < min(upto, len(self.units)):
            u = self.sent
            source, n, _, _ = self.units[u]
            if u >= SLOTS:
                _, _, sem, value = self.units[u - SLOTS]
                sp.wait_ge(sem, value)
            sp.dma_start(w[:, u % SLOTS, 0:n], source).then_inc(self.loaded[u % SLOTS], 16)
            self.sent += 1

    def await_unit(self, pe, u):
        pe.wait_ge(self.loaded[u % SLOTS], 16 * (u // SLOTS + 1))


def build(nc, dr, out):
    ctx = ExitStack()
    with ctx:
        def sb(name, n):
            return ctx.enter_context(nc.sbuf_tensor(name, [P, n], F32))

        scope = []
        holder = [ctx]

        def sem(name):
            s = holder[0].enter_context(nc.semaphore(name))
            scope.append(s)
            return s

        def layers(body):
            scope.clear()
            with ExitStack() as own:
                holder[0] = own
                with nc.Fori(0, DEPTH) as l:
                    body(l)
                    clear_semaphores(list(scope))
            holder[0] = ctx
            scope.clear()

        PS = ctx.enter_context(nc.psum_tensor("PS", [P, 8, 512], F32))
        x_all = sb("x_all", KD * T)
        h_all = sb("h_all", KD * T)
        w_all = sb("w_all", SLOTS * UNIT)
        m_all = sb("m_all", 16 * T)
        AR = sb("arena", ARENA)
        cst = sb("cst", C0N)
        spec = sb("spec", CN)
        par = sb("par", P1N)
        mod = sb("mod", 40)
        F8 = sb("F8", T)
        small = sb("small", 500)
        X = split3(x_all[:, :], KD)
        H = split3(h_all[:, :], KD)
        W = split3(w_all[:, :], SLOTS)
        M = split3(m_all[:, :], 16)
        ident = cst[:, 0:128]
        ones = cst[:, 128:256]
        triu = cst[:, 256:384]

        def const(name, table=C0, tile=None):
            a, b = table[name]
            return (cst if tile is None else tile)[:, a:b]

        def p1(name):
            return par[:, P1[name][0]:P1[name][1]]

        def p2(name):
            return par[:, P2[name][0]:P2[name][1]]

        class Arena:

            def __init__(self, at=0):
                self.at = at

            def take(self, n):
                assert self.at + n <= ARENA, self.at + n
                self.at += n
                return AR[:, self.at - n:self.at]

        def clear_semaphores(sems):
            with nc.Block() as block:
                @block.sync
                def _(sp):
                    for s in sems:
                        sp.sem_clear(s)

        def chain(eng, s):
            n = [0]

            def link(ins):
                n[0] += 1
                ins.then_inc(s, 1)
                eng.wait_ge(s, n[0])
            return link

        s_in = sem("inputs_loaded")
        s_vc = sem("setup_vector_step")
        s_red = sem("angles_reduced")
        s_sin = sem("sines_ready")
        COS, SIN = spec[:, C1N:C1N + T], spec[:, C1N + T:C1N + 2 * T]
        silu_c = mod[:, 32:40]
        with nc.Block() as block:
            ar = Arena()
            posi = ar.take(T).bitcast(I32)
            ang, k, r, r2, g = (ar.take(T) for _ in range(5))

            @block.sync
            def _(sp):
                sp.dma_start(cst[:, :], dr["c0"]).then_inc(s_in, 16)
                sp.dma_start(posi, dr["pos"]).then_inc(s_in, 16)
                sp.dma_start(silu_c, dr["c"]).then_inc(s_in, 16)
                sp.dma_start(spec[:, 0:C1N], dr["c1"]).then_inc(s_in, 16)
                sp.dma_start(x_all[:, :], dr["x"]).then_inc(s_in, 16)

            @block.vector
            def _(dve):
                link = chain(dve, s_vc)
                dve.wait_ge(s_in, 80)
                link(dve.tensor_copy(ang, posi))
                link(dve.tensor_scalar(ang, ang, const("freq"), None, ALU.mult))
                link(dve.tensor_scalar(k, ang, float(1 / (2 * np.pi)), 12582912.0, ALU.mult, ALU.add))
                link(dve.tensor_scalar(k, k, 12582912.0, None, ALU.subtract))
                c1 = 6.28125
                c2 = float(np.round((2 * np.pi - c1) * 2 ** 20) / 2 ** 20)
                c3 = float(2 * np.pi - c1 - c2)
                link(dve.scalar_tensor_tensor(r, k, -c1, ang, ALU.mult, ALU.add))
                link(dve.scalar_tensor_tensor(r, k, -c2, r, ALU.mult, ALU.add))
                link(dve.scalar_tensor_tensor(r, k, -c3, r, ALU.mult, ALU.add))
                link(dve.tensor_scalar(g, r, float(np.pi / 2), float(-2 * np.pi), ALU.is_gt, ALU.mult))
                link(dve.scalar_tensor_tensor(r2, r, float(np.pi / 2), g, ALU.add, ALU.add))
                pi = float(np.nextafter(np.float32(np.pi), np.float32(0)))
                link(dve.tensor_scalar(r, r, pi, -pi, ALU.min, ALU.max))
                dve.tensor_scalar(r2, r2, pi, -pi, ALU.min, ALU.max).then_inc(s_red, 1)
                dve.wait_ge(s_sin, 2)
                link(dve.tensor_scalar(SIN, SIN, const("sign"), None, ALU.mult))

            @block.scalar
            def _(act):
                act.wait_ge(s_red, 1)
                act.activation(SIN, r, ACT.Sin).then_inc(s_sin, 1)
                act.activation(COS, r2, ACT.Sin).then_inc(s_sin, 1)
                act.activation(silu_c, silu_c, ACT.Silu).then_inc(s_sin, 1)


        def column_sum(pe, bank, tiles, ready, base=0):
            for n, t in enumerate(tiles):
                pe.wait_ge(ready, base + n + 1)
                last = pe.matmul(PS[:, bank, :], ones, t, start=(n == 0), stop=(n == len(tiles) - 1))
            return last

        class Project:

            def __init__(self, stream, projected, evacuated):
                self.stream, self.projected, self.evacuated = stream, projected, evacuated
                self.jobs = []

            def feature_major(self, source, ncols, tiles, ktiles=KD, src=None):
                u = self.stream.add(source, ktiles * ncols, self.projected, len(self.jobs) + len(tiles))
                first = len(self.jobs)
                for c, m in tiles:
                    self.jobs.append((u, "f", c, m, ncols, ktiles, src))
                return first

            def token_major(self, source, ncols):
                u = self.stream.add(source, KD * ncols, self.projected, len(self.jobs) + NT)
                first = len(self.jobs)
                for t in range(NT):
                    self.jobs.append((u, "t", t, ncols, ncols, KD, None))
                return first

            def run(self, pe, j, source):
                u, kind, c, m, ncols, kt, _ = self.jobs[j]
                self.stream.await_unit(pe, u)
                if j >= 4:
                    pe.wait_ge(self.evacuated, j - 3)
                w = W[:, u % SLOTS, 0:kt * ncols].rearrange("p (k n) -> p k n", k=kt)
                for k in range(kt):
                    if kind == "f":
                        last = pe.matmul(PS[0:m, j % 4, :], w[:, k, c:c + m], source[:, k, :],
                                         start=(k == 0), stop=(k == kt - 1))
                    else:
                        last = pe.matmul(PS[:, j % 4, 0:m], source[:, k, c * P:(c + 1) * P], w[:, k, :],
                                         start=(k == 0), stop=(k == kt - 1))
                last.then_inc(self.projected, 1)

        class Attention:

            def __init__(self, name, heads, q, kf, vf, rows, buf):
                self.heads, self.q, self.kf, self.vf, self.rows = heads, q, kf, vf, rows
                self.steps = NT * heads
                (self.scored, self.smax, self.prob, self.turned, self.copied, self.weighted,
                 self.taken) = (sem(f"{name}_{x}") for x in (
                     "scored", "max_taken", "probabilities", "turned", "turned_copied", "weighted",
                     "output_taken"))
                self.sm, self.p, self.pt, self.nm, self.rs = buf

            def score(self, pe, s):
                i, h = divmod(s, self.heads)
                n = (i + 1) * P
                if s >= 2:
                    pe.wait_ge(self.smax, s - 1)
                pe.matmul(PS[:, 4 + s % 2, 0:n], self.q[0:self.rows, h, i * P:(i + 1) * P],
                          self.kf(h)[0:self.rows, 0:n], start=True, stop=True).then_inc(self.scored, 1)

            def turn(self, pe, s):
                i = s // self.heads
                pe.wait_ge(self.prob, s + 1)
                if s >= 2:
                    pe.wait_ge(self.copied, s - 1)
                for t in range(i + 1):
                    last = pe.transpose(PS[:, 6 + s % 2, t * P:(t + 1) * P],
                                        self.p[:, s % 2, t * P:(t + 1) * P], ident)
                last.then_inc(self.turned, 1)

            def weigh(self, pe, s):
                i, h = divmod(s, self.heads)
                pe.wait_ge(self.copied, s + 1)
                if h == 0 and i >= 2:
                    pe.wait_ge(self.taken, i - 1)
                for t in range(i + 1):
                    last = pe.matmul(PS[:, i % 2, h * FD:(h + 1) * FD], self.pt[:, s % 2, t * P:(t + 1) * P],
                                     self.vf(h, t), start=(t == 0), stop=(t == i))
                last.then_inc(self.weighted, 1)

            def tensor(self, pe):
                self.score(pe, 0)
                self.score(pe, 1)
                for s in range(self.steps):
                    self.turn(pe, s)
                    if s + 2 < self.steps:
                        self.score(pe, s + 2)
                    if s >= 1:
                        self.weigh(pe, s - 1)
                self.weigh(pe, self.steps - 1)

            def scalar(self, act):
                for s in range(self.steps):
                    n = (s // self.heads + 1) * P
                    act.wait_ge(self.smax, s + 1)
                    if s >= 2:
                        act.wait_ge(self.turned, s - 1)
                    act.activation(self.p[:, s % 2, 0:n], self.sm[:, s % 2, 0:n], ACT.Exp,
                                   bias=self.nm[:, s:s + 1], scale=-1.0,
                                   accum_out=self.rs[:, s:s + 1]).then_inc(self.prob, 1)

            def vector(self, dve, finish):
                def maximum(s):
                    n = (s // self.heads + 1) * P
                    dve.wait_ge(self.scored, s + 1)
                    if s >= 2:
                        dve.wait_ge(self.prob, s - 1)
                    dve.tensor_tensor_reduce(self.sm[:, s % 2, 0:n], PS[:, 4 + s % 2, 0:n],
                                             const("causal")[:, T - n:T], -(FD ** -0.5), 3.0e38,
                                             ALU.add, ALU.min, self.nm[:, s:s + 1]).then_inc(self.smax, 1)

                def copy(s):
                    n = (s // self.heads + 1) * P
                    dve.wait_ge(self.turned, s + 1)
                    if s >= 2:
                        dve.wait_ge(self.weighted, s - 1)
                    dve.tensor_copy(self.pt[:, s % 2, 0:n], PS[:, 6 + s % 2, 0:n]).then_inc(self.copied, 1)

                maximum(0)
                for s in range(self.steps):
                    if s + 1 < self.steps:
                        maximum(s + 1)
                    copy(s)
                    if s % self.heads == 1 and s > self.heads:
                        finish(s // self.heads - 1)
                finish(NT - 1)

        def first_layer(l):
            stream = Stream([sem(f"weights_loaded_{i}") for i in range(SLOTS)])
            projected, evacuated = sem("projected"), sem("evacuated")
            mod_used = sem("modulation_unit_used")
            proj = Project(stream, projected, evacuated)

            def drl(name, *ix):
                t = dr[name][bass.ds(l, 1)]
                for i in ix:
                    t = t[:, i]
                return t.rearrange("a p n -> (a p) n")

            NADA = 12
            for u in range(NADA):
                stream.add(drl("w_ada", u), UNIT, mod_used, u + 1)
            two = [(0, P), (P, P)]
            wu = lambda i: drl("w_in", i)
            J = {}
            J["rq"] = [proj.feature_major(wu(i), UC, two) for i in (0, 1)][0]
            J["rk"] = [proj.feature_major(wu(i), UC, two) for i in (2, 3)][0]
            J["rg"] = [proj.feature_major(wu(i), UC, two) for i in (4, 5)][0]
            J["rv"] = [proj.token_major(wu(i), UC) for i in (6, 7)][0]
            end_r = len(stream.units)
            J["dtf"] = proj.token_major(drl("w_dtf"), 24)
            J["bc"] = [proj.feature_major(wu(i), UC, two) for i in (8, 9)][0]
            J["xs"] = [proj.feature_major(wu(i), UC, two) for i in range(10, 14)][0]
            J["z"] = [proj.token_major(wu(i), UC) for i in range(14, 18)][0]
            end_s = len(stream.units)
            J["fq"] = [proj.feature_major(wu(i), UC, two) for i in (18, 19)][0]
            J["fk"] = [proj.feature_major(wu(i), UC, two) for i in (20, 21)][0]
            J["fv"] = [proj.token_major(wu(i), UC) for i in (22, 23)][0]
            J["fg"] = [proj.token_major(wu(i), UC) for i in (24, 25)][0]
            end_f = len(stream.units)
            J["out"] = [proj.feature_major(drl("w_out", i), P, [(0, P)], ktiles=16) for i in range(8)][0]

            s_par = sem("parameters_loaded")
            s_sq = sem("x_squared")
            s_ss = sem("x_square_sum")
            s_rms = sem("x_rms")
            s_mod = sem("modulation_done")
            s_hs = sem("h_scaled")
            s_dv = sem("mod_vector_step")
            s_h = sem("h_ready")
            with nc.Block() as block:
                ar = Arena()
                sq = split3(ar.take(KD * T), KD)
                rms, rstd = ar.take(T), ar.take(T)
                msb, amul = mod[:, 0:24], mod[:, 24:32]

                @block.sync
                def _(sp):
                    sp.dma_start(par[:, 0:P1N], drl("par1")).then_inc(s_par, 16)
                    stream.send(sp, W, NADA + SLOTS)

                @block.tensor
                def _(pe):
                    column_sum(pe, 0, [sq[:, k, :] for k in range(KD)], s_sq).then_inc(s_ss, 1)
                    for u in range(NADA):
                        stream.await_unit(pe, u)
                        w = split3(W[:, u % SLOTS, :], KD)
                        for j in range(2):
                            c = 2 * u + j
                            for k in range(KD):
                                last = pe.matmul(PS[:, 7, c:c + 1], w[:, k, j * P:(j + 1) * P],
                                                 silu_c[:, k:k + 1], start=(k == 0), stop=(k == KD - 1))
                        last.then_inc(mod_used, 1)

                @block.scalar
                def _(act):
                    for k in range(KD):
                        act.activation(sq[:, k, :], X[:, k, :], ACT.Square).then_inc(s_sq, 1)
                    act.wait_ge(s_ss, 1)
                    act.activation(rms, PS[:, 0, :], ACT.Sqrt, bias=EPS, scale=1.0 / D).then_inc(s_rms, 1)
                    for k in range(KD):
                        act.wait_ge(s_hs, k + 1)
                        act.activation(H[:, k, :], H[:, k, :], ACT.Identity,
                                       bias=msb[:, k:k + 1]).then_inc(s_h, 1)

                @block.vector
                def _(dve):
                    link = chain(dve, s_dv)
                    dve.wait_ge(s_rms, 1)
                    link(dve.reciprocal(rstd, rms))
                    dve.wait_ge(s_par, 16)
                    dve.wait_ge(mod_used, NADA)
                    link(dve.tensor_tensor(msb, PS[:, 7, 0:24], p1("b_ada"), ALU.add))
                    link(dve.scalar_tensor_tensor(amul, msb[:, 8:16], 1.0, p1("norm_g"), ALU.add, ALU.mult))
                    for k in range(KD):
                        dve.scalar_tensor_tensor(H[:, k, :], X[:, k, :], amul[:, k:k + 1], rstd,
                                                 ALU.mult, ALU.mult).then_inc(s_hs, 1)

            s_rot = sem("rotated")
            s_qd = sem("q_decayed")
            s_kt = sem("k_turned")
            s_kd = sem("k_decayed")
            s_rs = sem("ret_scored")
            s_rd = sem("ret_scores_decayed")
            s_ds = sem("ret_state_products")
            s_st = sem("ret_state_ready")
            s_ro = sem("ret_output")
            s_rq = sem("ret_squared")
            s_rn = sem("ret_square_sum")
            s_rr = sem("ret_rms")
            s_rv = sem("ret_vector_step")
            decay_chunk = [float((1.0 - 2.0 ** (-5.0 - h)) ** P) for h in range(RH)]
            decayT = spec[:, 0:512]
            decq = spec[:, 512:1024]
            deck = spec[:, 1024:1028]
            with nc.Block() as block:
                ar = Arena()
                q4, k4, qd4 = (split3(ar.take(4 * T), 4) for _ in range(3))
                v4 = split3(ar.take(4 * T), 4)
                kd4 = ar.take(4 * 384).rearrange("p (h c d) -> p h c d", h=4, c=3)
                sT = split3(ar.take(4 * T), 4)
                S = split3(ar.take(3 * T), 3)
                raw = split3(ar.take(2 * T), 2)
                swp = split3(ar.take(2 * T), 2)
                sq = split3(ar.take(4 * T), 4)
                rr = split3(ar.take(4 * T), 4)
                jq, jg, jv = J["rq"], J["rg"], J["rv"]
                nj = J["dtf"]

                @block.sync
                def _(sp):
                    stream.send(sp, W, end_r + SLOTS)

                @block.tensor
                def _(pe):
                    for j in range(nj):
                        proj.run(pe, j, H)
                    for h in range(RH):
                        pe.wait_ge(s_rot, 4 + h + 1)
                        if h >= 2:
                            pe.wait_ge(s_kd, h - 1)
                        for c in range(3):
                            last = pe.transpose(PS[:, 4 + h % 2, c * P:(c + 1) * P],
                                                k4[:, h, c * P:(c + 1) * P], ident)
                        last.then_inc(s_kt, 1)
                    for c in range(NT):
                        if c >= 2:
                            pe.wait_ge(s_rd, c - 1)
                        for h in range(RH):
                            last = pe.matmul(PS[:, 6 + c % 2, h * P:(h + 1) * P], k4[:, h, c * P:(c + 1) * P],
                                             q4[:, h, c * P:(c + 1) * P], start=True, stop=True)
                        last.then_inc(s_rs, 1)
                    pe.wait_ge(evacuated, nj)
                    for c in range(NT - 1):
                        if c == 0:
                            pe.wait_ge(s_kd, RH)
                        if c >= 2:
                            pe.wait_ge(s_st, c - 1)
                        for h in range(RH):
                            last = pe.matmul(PS[:, 4 + c % 2, h * P:(h + 1) * P], kd4[:, h, c, :],
                                             v4[:, c, h * P:(h + 1) * P], start=True, stop=True)
                        last.then_inc(s_ds, 1)
                    pe.wait_ge(s_qd, RH)
                    for c in range(NT):
                        pe.wait_ge(s_rd, c + 1)
                        if c:
                            pe.wait_ge(s_st, c)
                        for h in range(RH):
                            o = PS[:, c, h * P:(h + 1) * P]
                            last = pe.matmul(o, v4[:, c, h * P:(h + 1) * P], sT[:, c, h * P:(h + 1) * P],
                                             start=True, stop=(c == 0))
                            if c:
                                last = pe.matmul(o, S[:, c - 1, h * P:(h + 1) * P],
                                                 qd4[:, h, c * P:(c + 1) * P], start=False, stop=True)
                        last.then_inc(s_ro, 1)
                    pe.wait_ge(s_rq, NT)
                    for h in range(RH):
                        if h == 0:
                            pe.wait_ge(s_st, 3)
                        pe.matmul(PS[:, 4 + h, :], ones, sq[:, h, :], start=True, stop=True).then_inc(s_rn, 1)

                @block.scalar
                def _(act):
                    for j in range(nj):
                        act.wait_ge(projected, j + 1)
                        b = PS[:, j % 4, :]
                        if j < jg:
                            if j >= 2:
                                act.wait_ge(s_rot, j - 1)
                            act.copy(raw[:, j % 2, :], b)
                            act.copy(swp[0:64, j % 2, :], b[64:128, :])
                            act.copy(swp[64:128, j % 2, :], b[0:64, :]).then_inc(evacuated, 1)
                        elif j < jv:
                            act.activation(M[:, j - jg, :], b, ACT.Silu).then_inc(evacuated, 1)
                        else:
                            u, t = divmod(j - jv, NT)
                            act.copy(v4[:, t, u * UC:(u + 1) * UC], b[:, 0:UC]).then_inc(evacuated, 1)
                    for c in range(NT):
                        act.wait_ge(s_ro, c + 1)
                        act.activation(sq[:, :, c * P:(c + 1) * P], split3(PS[:, c, :], 4),
                                       ACT.Square).then_inc(s_rq, 1)
                    for h in range(RH):
                        act.wait_ge(s_rn, h + 1)
                        act.activation(rr[:, h, :], PS[:, 4 + h, :], ACT.Sqrt, bias=EPS,
                                       scale=1.0 / P).then_inc(s_rr, 1)

                @block.vector
                def _(dve):
                    link = chain(dve, s_rv)
                    for j in range(8):
                        dve.wait_ge(evacuated, j + 1)
                        link(dve.tensor_tensor(raw[:, j % 2, :], raw[:, j % 2, :], COS, ALU.mult))
                        link(dve.tensor_tensor(swp[:, j % 2, :], swp[:, j % 2, :], SIN, ALU.mult))
                        dst = (q4 if j < 4 else k4)[:, j % 4, :]
                        dve.tensor_tensor(dst, raw[:, j % 2, :], swp[:, j % 2, :], ALU.add).then_inc(s_rot, 1)
                        if j < 4:
                            dve.wait_ge(s_rot, j + 1)
                            dve.tensor_tensor(split3(qd4[:, j, :], 4), split3(q4[:, j, :], 4),
                                              repeat(decq[:, j * P:(j + 1) * P], 4), ALU.mult).then_inc(s_qd, 1)
                    for h in range(RH):
                        dve.wait_ge(s_kt, h + 1)
                        dve.tensor_scalar(kd4[:, h, :, :], split3(PS[:, 4 + h % 2, 0:384], 3), deck[:, h:h + 1],
                                          None, ALU.mult).then_inc(s_kd, 1)
                    for c in range(NT):
                        dve.wait_ge(s_rs, c + 1)
                        dve.tensor_tensor(sT[:, c, :], PS[:, 6 + c % 2, :], decayT, ALU.mult).then_inc(s_rd, 1)
                    for c in range(NT - 1):
                        dve.wait_ge(s_ds, c + 1)
                        if c == 0:
                            dve.tensor_copy(S[:, 0, :], PS[:, 4, :]).then_inc(s_st, 1)
                            continue
                        dve.wait_ge(s_st, c)
                        for h in range(RH):
                            last = dve.scalar_tensor_tensor(
                                S[:, c, h * P:(h + 1) * P], S[:, c - 1, h * P:(h + 1) * P], decay_chunk[h],
                                PS[:, 4 + c % 2, h * P:(h + 1) * P], ALU.mult, ALU.add)
                        last.then_inc(s_st, 1)
                    for c in range(NT):
                        dve.wait_ge(s_rq, c + 1)
                        g = M[:, 0:4, c * P:(c + 1) * P]
                        link(dve.tensor_tensor(g, split3(PS[:, c, :], 4), g, ALU.mult))
                    for h in range(RH):
                        dve.wait_ge(s_rr, h + 1)
                        link(dve.reciprocal(rr[:, h, :], rr[:, h, :]))
                        link(dve.tensor_tensor(M[:, h, :], M[:, h, :], rr[:, h, :], ALU.mult))

            nb = lambda n: sem("ssd_" + n)
            s_sel, s_sv, s_ab, s_ex, s_w1, s_ln = (nb(x) for x in (
                "selectors_loaded", "vector_step", "gate_magnitudes", "gate_exp", "gate_one_plus", "gate_log"))
            s_a, s_lf, s_sm, s_smt, s_ea = (nb(x) for x in (
                "steps_ready", "log_forget_ready", "cumulative_sums", "cumulative_sums_taken", "decays_ready"))
            s_al, s_cv, s_si, s_bt, s_btc = (nb(x) for x in (
                "a_exp", "convolved", "conv_activated", "b_turned", "b_turned_copied"))
            s_cb, s_cbm, s_xt, s_xtc, s_xd = (nb(x) for x in (
                "cb_products", "cb_masked", "x_turned", "x_turned_copied", "x_scaled"))
            s_bc, s_sg, s_le, s_we, s_y, s_yt = (nb(x) for x in (
                "log_decay_spread", "log_decay_ready", "decay_ready", "weights_ready", "y_products", "y_taken"))
            s_sd, s_ss2, s_xdd, s_q2, s_r2, s_yn = (nb(x) for x in (
                "state_products", "state_ready", "x_state_scaled", "y_squared", "y_rms", "y_normed"))
            s_tr, s_ev, s_nf = (nb(x) for x in ("y_turned", "y_turned_copied", "negated_copied"))
            s_pad = nb("conv_padding_zeroed")
            dtf = split3(small[:, 0:96], 4)
            mag = split3(small[:, 96:192], 4)
            ex = split3(small[:, 192:288], 4)
            w1 = split3(small[:, 288:384], 4)
            lg = split3(small[:, 384:480], 4)
            with nc.Block() as block:
                ar = Arena()
                pre = split3(ar.take(2 * 515), 2)
                acc = split3(ar.take(2 * T), 2)
                xf = split3(ar.take(2 * T), 2)
                bcf = split3(ar.take(4 * T), 4)
                xt = split3(ar.take(NT * D), NT)
                xdt = split3(ar.take(NT * D), NT)
                xdd = ar.take(D)
                z = split3(ar.take(NT * D), NT)
                bt = ar.take(768).rearrange("p (g c n) -> p g c n", g=2, c=3)
                cb = ar.take(1024).rearrange("p (g c i) -> p g c i", g=2, c=4)
                St = split3(ar.take(2 * T), 2)
                yt = split3(ar.take(2 * T), 2)
                sel = ar.take(SH * P)
                seg = split3(m_all[:, 12 * T:16 * T], 2)
                afm = M[0:SH, 7, :]
                sums = M[:, 4, 0:512]
                acum, tot = split3(sums[:, 0:64], 4), split3(sums[:, 64:128], 4)
                eac, edl, eto = (split3(sums[:, 128 + 64 * i:192 + 64 * i], 4) for i in range(3))
                nac = split3(sums[:, 320:384], 4)
                aa = split3(sums[:, 384:448], 4)
                amat = sums[:, 448:464]
                Ft = F8[0:FH, :]
                ssq, rst = M[:, 6, 0:4], M[:, 6, 4:8]
                jd, jb, jx, jz, je = J["dtf"], J["bc"], J["xs"], J["z"], J["fq"]
                steps = [(c, g) for c in range(NT) for g in range(SG)]

                @block.sync
                def _(sp):
                    sp.dma_start(sel[0:SH, :], dr["sel"]).then_inc(s_sel, 16)
                    stream.send(sp, W, end_s + SLOTS)

                @block.gpsimd
                def _(pool):
                    pool.memset(pre[:, :, 0:3], 0.0).then_inc(s_pad, 1)

                @block.tensor
                def _(pe):
                    for j in range(jd, jx):
                        proj.run(pe, j, H)
                    pe.wait_ge(s_a, 1)
                    for c in range(NT):
                        pe.matmul(PS[:, 4, c * SH:(c + 1) * SH], triu, aa[:, c, :], start=True, stop=True)
                        pe.matmul(PS[:, 4, 64 + c * SH:64 + (c + 1) * SH], ones, aa[:, c, :], start=True, stop=True)
                    for c in range(NT):
                        last = pe.matmul(PS[0:SH, 5, c * P:(c + 1) * P], aa[:, c, :], triu, start=True, stop=True)
                    last.then_inc(s_sm, 1)
                    pe.wait_ge(s_lf, 1)
                    for c in range(NT):
                        for b in range(c + 1):
                            last = pe.matmul(PS[0:FH, 6, c * P:(c + 1) * P], lg[:, b, 16:24],
                                             triu if b == c else ones, start=(b == 0), stop=(b == c))
                    last.then_inc(s_sm, 1)
                    pe.wait_ge(s_si, 4)
                    pe.wait_ge(s_smt, 3)
                    for g in range(SG):
                        for c in range(NT - 1):
                            last = pe.transpose(PS[:, 4 + g, c * P:(c + 1) * P], bcf[:, g, c * P:(c + 1) * P], ident)
                        last.then_inc(s_bt, 1)
                    for g in range(SG):
                        for c in range(NT):
                            last = pe.matmul(PS[:, 6 + g, c * P:(c + 1) * P], bcf[:, g, c * P:(c + 1) * P],
                                             bcf[:, 2 + g, c * P:(c + 1) * P], start=True, stop=True)
                        last.then_inc(s_cb, 1)

                    def turn_x(n):
                        pe.wait_ge(s_si, 4 + n + 1)
                        if n < 2:
                            pe.wait_ge(s_btc, n + 1)
                        else:
                            pe.wait_ge(s_xtc, n - 1)
                        for c in range(NT):
                            last = pe.transpose(PS[:, 4 + n % 2, c * P:(c + 1) * P],
                                                xf[:, n % 2, c * P:(c + 1) * P], ident)
                        last.then_inc(s_xt, 1)

                    for j in range(jx, je):
                        proj.run(pe, j, H)
                        if 2 <= j - jx < 10:
                            turn_x(j - jx - 2)

                    def spread_decay(s):
                        c, g = steps[s]
                        if s == 0:
                            pe.wait_ge(s_sel, 16)
                            pe.wait_ge(s_xtc, 8)
                            pe.wait_ge(s_smt, 3)
                        else:
                            pe.wait_ge(s_sg, s)
                        for h in range(HG):
                            hh = g * HG + h
                            last = pe.matmul(PS[:, 4 + h // 4, (h % 4) * P:(h % 4 + 1) * P],
                                             sel[0:SH, hh * P:(hh + 1) * P], afm[:, c * P:(c + 1) * P],
                                             start=True, stop=True)
                        last.then_inc(s_bc, 1)

                    def outputs(s):
                        c, g = steps[s]
                        pe.wait_ge(s_we, s + 1)
                        if s == 0:
                            pe.wait_ge(s_cbm, 2)
                            pe.wait_ge(s_xd, NT)
                        else:
                            pe.wait_ge(s_yt, s)
                        for h in range(HG):
                            last = pe.matmul(PS[:, 6, h * SP:(h + 1) * SP], seg[:, s % 2, h * P:(h + 1) * P],
                                             xdt[:, c, (g * HG + h) * SP:(g * HG + h + 1) * SP],
                                             start=True, stop=True)
                        if c:
                            pe.wait_ge(s_ss2, (c - 1) * 2 + g + 1)
                            last = pe.matmul(PS[:, 7, :], bcf[:, 2 + g, c * P:(c + 1) * P], St[:, g, :],
                                             start=True, stop=True)
                        last.then_inc(s_y, 1)
                        if c < NT - 1:
                            n = 2 * c + g
                            if n == 0:
                                pe.wait_ge(evacuated, je)
                                pe.wait_ge(s_btc, 2)
                            if c:
                                pe.wait_ge(s_ss2, n - 1)
                            pe.wait_ge(s_xdd, c + 1)
                            pe.matmul(PS[:, g, :], bt[:, g, c, :], xdd[:, g * T:(g + 1) * T],
                                      start=True, stop=True).then_inc(s_sd, 1)

                    spread_decay(0)
                    for s in range(8):
                        if s + 1 < 8:
                            spread_decay(s + 1)
                        outputs(s)
                    for f in range(8):
                        b = 2 + f % 2
                        if f == 0:
                            pe.wait_ge(s_yn, NT)
                        if f >= 2:
                            pe.wait_ge(s_ev, f - 1)
                        for c in range(NT):
                            last = pe.transpose(PS[:, b, c * P:(c + 1) * P], z[:, c, f * P:(f + 1) * P], ident)
                        last.then_inc(s_tr, 1)

                @block.scalar
                def _(act):
                    def evacuate(j):
                        act.wait_ge(projected, j + 1)
                        b = PS[:, j % 4, :]
                        if j < jb:
                            act.copy(dtf[:, j - jd, :], b[:, 0:24]).then_inc(evacuated, 1)
                        elif j < jz:
                            n = j - jb
                            if n == 0:
                                act.wait_ge(s_pad, 1)
                            if n >= 2:
                                act.wait_ge(s_cv, n - 1)
                            act.copy(pre[:, n % 2, 3:515], b).then_inc(evacuated, 1)
                        else:
                            u, t = divmod(j - jz, NT)
                            act.activation(z[:, t, u * UC:(u + 1) * UC], b[:, 0:UC],
                                           ACT.Silu).then_inc(evacuated, 1)

                    def activate(n):
                        act.wait_ge(s_cv, n + 1)
                        if n >= 6:
                            act.wait_ge(s_xt, n - 5)
                        dst = bcf[:, n, :] if n < 4 else xf[:, n % 2, :]
                        act.activation(dst, acc[:, n % 2, :], ACT.Silu).then_inc(s_si, 1)

                    def copy_x(n):
                        act.wait_ge(s_xt, n + 1)
                        act.copy(xt[:, :, n * P:(n + 1) * P], split3(PS[:, 4 + n % 2, :], 4)).then_inc(s_xtc, 1)

                    for j in range(jd, jb):
                        evacuate(j)
                    act.activation(amat, p1("a_log"), ACT.Exp).then_inc(s_al, 1)
                    act.wait_ge(s_ab, 1)
                    act.activation(ex, mag, ACT.Exp, scale=-1.0).then_inc(s_ex, 1)
                    act.wait_ge(s_w1, 1)
                    act.activation(lg, w1, ACT.Ln).then_inc(s_ln, 1)
                    for j in range(jb, jx):
                        evacuate(j)
                        if j > jb:
                            activate(j - jb - 1)
                    activate(3)
                    act.wait_ge(s_sm, 1)
                    act.copy(afm, PS[0:SH, 5, :]).then_inc(s_smt, 1)
                    act.wait_ge(s_sm, 2)
                    act.copy(Ft, PS[0:FH, 6, :]).then_inc(s_smt, 1)
                    act.wait_ge(s_smt, 3)
                    act.wait_ge(s_nf, 1)
                    act.activation(eac, acum, ACT.Exp)
                    act.activation(eto, tot, ACT.Exp)
                    act.activation(edl, edl, ACT.Exp).then_inc(s_ea, 1)
                    for g in range(SG):
                        act.wait_ge(s_bt, g + 1)
                        act.copy(bt[:, g, :, :], split3(PS[:, 4 + g, 0:384], 3)).then_inc(s_btc, 1)
                    for j in range(jx, je):
                        evacuate(j)
                        if 1 <= j - jx < 9:
                            activate(4 + j - jx - 1)
                        if 4 <= j - jx < 12:
                            copy_x(j - jx - 4)
                    for s in range(8):
                        act.wait_ge(s_sg, s + 1)
                        act.activation(seg[:, s % 2, :], seg[:, s % 2, :], ACT.Exp).then_inc(s_le, 1)
                    for c in range(NT):
                        act.wait_ge(s_yt, 2 * c + 2)
                        act.activation(xt[:, c, :], z[:, c, :], ACT.Square,
                                       accum_out=ssq[:, c:c + 1]).then_inc(s_q2, 1)
                        act.wait_ge(s_q2, c + 1)
                    act.activation(rst, ssq, ACT.Sqrt, bias=EPS, scale=1.0 / D).then_inc(s_r2, 1)
                    for f in range(8):
                        act.wait_ge(s_tr, f + 1)
                        act.activation(M[:, 4 + f, :], PS[:, 2 + f % 2, :], ACT.Copy,
                                       scale=p1("ssd_g")[:, f:f + 1]).then_inc(s_ev, 1)

                @block.vector
                def _(dve):
                    link = chain(dve, s_sv)
                    dve.wait_ge(evacuated, jb)
                    link(dve.tensor_tensor(dtf, dtf, repeat(p1("dtf_b"), NT), ALU.add))
                    dve.scalar_tensor_tensor(mag, dtf, -1.0, dtf, ALU.mult, ALU.max).then_inc(s_ab, 1)
                    dve.wait_ge(s_ex, 1)
                    dve.tensor_scalar(w1, ex, 1.0, None, ALU.add).then_inc(s_w1, 1)
                    dve.wait_ge(s_w1, 1)
                    link(dve.scalar_tensor_tensor(mag, w1, 1.0, ex, ALU.subtract, ALU.subtract))
                    dve.wait_ge(s_ln, 1)
                    link(dve.reciprocal(w1, w1))
                    link(dve.tensor_tensor(mag, mag, w1, ALU.mult))
                    link(dve.tensor_tensor(lg, lg, mag, ALU.subtract))
                    link(dve.scalar_tensor_tensor(dtf[:, :, 0:16], dtf[:, :, 0:16], 0.0, lg[:, :, 0:16],
                                                  ALU.max, ALU.add))
                    dve.scalar_tensor_tensor(lg[:, :, 16:24], dtf[:, :, 16:24], 0.0, lg[:, :, 16:24],
                                             ALU.min, ALU.subtract).then_inc(s_lf, 1)
                    dve.wait_ge(s_al, 1)
                    dve.scalar_tensor_tensor(aa, dtf[:, :, 0:16], -1.0, repeat(amat, NT),
                                             ALU.mult, ALU.mult).then_inc(s_a, 1)

                    def convolve(n):
                        dve.wait_ge(evacuated, jb + n + 1)
                        if n >= 2:
                            dve.wait_ge(s_si, n - 1)
                        t = (n + 8) % 12
                        a, p = acc[:, n % 2, :], pre[:, n % 2, :]
                        wk = lambda k: p1("conv_w")[:, k * 12 + t:k * 12 + t + 1]
                        link(dve.tensor_scalar(a, p[:, 0:512], wk(0), p1("conv_b")[:, t:t + 1], ALU.mult, ALU.add))
                        for k in (1, 2):
                            link(dve.scalar_tensor_tensor(a, p[:, k:k + 512], wk(k), a, ALU.mult, ALU.add))
                        dve.scalar_tensor_tensor(a, p[:, 3:515], wk(3), a, ALU.mult, ALU.add).then_inc(s_cv, 1)

                    for n in range(4):
                        convolve(n)
                    dve.wait_ge(s_sm, 1)
                    dve.tensor_copy(sums[:, 0:128], PS[:, 4, 0:128]).then_inc(s_smt, 1)
                    dve.wait_ge(s_smt, 3)
                    link(dve.tensor_scalar(nac, acum, -1.0, None, ALU.mult))
                    dve.tensor_tensor(edl, tot, acum, ALU.subtract).then_inc(s_nf, 1)
                    dve.wait_ge(s_ea, 1)
                    link(dve.tensor_tensor(edl, edl, dtf[:, :, 0:16], ALU.mult))
                    for g in range(SG):
                        dve.wait_ge(s_cb, g + 1)
                        dve.tensor_tensor(cb[:, g, :, :], split3(PS[:, 6 + g, :], 4), repeat(triu, 4),
                                          ALU.mult).then_inc(s_cbm, 1)
                    for n in range(4, 12):
                        convolve(n)
                    dve.wait_ge(s_xtc, 8)
                    for c in range(NT):
                        dve.tensor_tensor(split3(xdt[:, c, :], SH), split3(xt[:, c, :], SH),
                                          spread(dtf[:, c, 0:16], SP), ALU.mult).then_inc(s_xd, 1)

                    def log_decays(s):
                        c, g = steps[s]
                        dve.wait_ge(s_bc, s + 1)
                        if s >= 2:
                            dve.wait_ge(s_y, s - 1)
                        for h in range(HG):
                            last = dve.tensor_scalar(seg[:, s % 2, h * P:(h + 1) * P],
                                                     PS[:, 4 + h // 4, (h % 4) * P:(h % 4 + 1) * P],
                                                     nac[:, c, g * HG + h:g * HG + h + 1], 0.0,
                                                     ALU.add, ALU.min)
                        last.then_inc(s_sg, 1)

                    def weigh(s):
                        c, g = steps[s]
                        dve.wait_ge(s_cbm, 2)
                        dve.wait_ge(s_le, s + 1)
                        v = split3(seg[:, s % 2, :], HG)
                        dve.tensor_tensor(v, v, repeat(cb[:, g, c, :], HG), ALU.mult).then_inc(s_we, 1)

                    def state_input(c):
                        if c >= 1:
                            dve.wait_ge(s_sd, 2 * c)
                        dve.tensor_tensor(split3(xdd, SH), split3(xt[:, c, :], SH), spread(edl[:, c, :], SP),
                                          ALU.mult).then_inc(s_xdd, 1)

                    def combine(s):
                        c, g = steps[s]
                        hs = slice(g * HG, (g + 1) * HG)
                        y0, y1 = (split3(yt[:, i, :], HG) for i in range(2))
                        xs_ = split3(xt[:, c, g * T:(g + 1) * T], HG)
                        link(dve.tensor_tensor(y0, xs_, spread(p1("d_skip")[:, hs], SP), ALU.mult))
                        dve.wait_ge(s_y, s + 1)
                        if c:
                            link(dve.tensor_tensor(y1, split3(PS[:, 7, :], HG), spread(eac[:, c, hs], SP), ALU.mult))
                            link(dve.tensor_tensor(y0, y0, y1, ALU.add))
                        link(dve.tensor_tensor(y0, y0, split3(PS[:, 6, :], HG), ALU.add))
                        zz = split3(z[:, c, g * T:(g + 1) * T], HG)
                        dve.tensor_tensor(zz, y0, zz, ALU.mult).then_inc(s_yt, 1)
                        dve.wait_ge(s_yt, s + 1)
                        if c < NT - 1:
                            n = 2 * c + g
                            dve.wait_ge(s_sd, n + 1)
                            if c == 0:
                                dve.tensor_copy(St[:, g, :], PS[:, g, :]).then_inc(s_ss2, 1)
                            else:
                                sv = split3(St[:, g, :], HG)
                                link(dve.tensor_tensor(sv, sv, spread(eto[:, c, hs], SP), ALU.mult))
                                dve.tensor_tensor(St[:, g, :], St[:, g, :], PS[:, g, :], ALU.add).then_inc(s_ss2, 1)
                            dve.wait_ge(s_ss2, n + 1)

                    log_decays(0)
                    for s in range(8):
                        if s + 1 < 8:
                            log_decays(s + 1)
                        c, g = steps[s]
                        if g == 0 and c < NT - 1:
                            state_input(c)
                        weigh(s)
                        if s == 0:
                            dve.wait_ge(evacuated, je)
                        combine(s)
                    dve.wait_ge(s_r2, 1)
                    link(dve.reciprocal(rst, rst))
                    for c in range(NT):
                        dve.tensor_scalar(z[:, c, :], z[:, c, :], rst[:, c:c + 1], None, ALU.mult).then_inc(s_yn, 1)

            s_aug = sem("fox_bias_rows_loaded")
            s_fb = sem("fox_bias_rows_ready")
            s_fv = sem("fox_vector_step")
            s_fx = sem("fox_tile_ready")
            s_ft = sem("fox_output_turned")
            s_fe = sem("fox_output_copied")
            with nc.Block() as block:
                ar = Arena()
                q, k = split3(ar.take(FH * T), FH), split3(ar.take(FH * T), FH)
                v, fg = split3(ar.take(4 * T), 4), split3(ar.take(4 * T), 4)
                rinv = ar.take(FH)
                buf = (split3(ar.take(2 * T), 2), split3(ar.take(2 * T), 2), split3(ar.take(2 * T), 2),
                       ar.take(32), ar.take(32))
                att = Attention("fox", FH, q, lambda h: k[:, h, :],
                                lambda h, t: v[:, t, h * FD:(h + 1) * FD], 104, buf)
                jq, jk, jv, jg, je = J["fq"], J["fk"], J["fv"], J["fg"], J["out"]

                @block.sync
                def _(sp):
                    sp.dma_start(q[64:104, :, :], dr["aug_q"].rearrange("p (h t) -> p h t", h=FH)).then_inc(s_aug, 16)
                    sp.dma_start(k[64:104, :, :], dr["aug_k"].rearrange("p (h t) -> p h t", h=FH)).then_inc(s_aug, 16)
                    stream.send(sp, W, end_f + SLOTS)

                @block.tensor
                def _(pe):
                    for j in range(jq, je):
                        proj.run(pe, j, H)
                    pe.wait_ge(evacuated, je)
                    pe.wait_ge(s_fb, 2)
                    att.tensor(pe)
                    for f in range(NT):
                        if f == 0:
                            pe.wait_ge(s_fx, NT)
                        if f >= 2:
                            pe.wait_ge(s_fe, f - 1)
                        for i in range(NT):
                            last = pe.transpose(PS[:, 2 + f % 2, i * P:(i + 1) * P], fg[:, i, f * P:(f + 1) * P], ident)
                        last.then_inc(s_ft, 1)

                @block.scalar
                def _(act):
                    for j in range(jq, je):
                        act.wait_ge(projected, j + 1)
                        b = PS[:, j % 4, :]
                        if j < jv:
                            dst, h = (q, j - jq) if j < jk else (k, j - jk)
                            act.copy(dst[0:64, 2 * h, :], b[0:64, :])
                            act.copy(dst[0:64, 2 * h + 1, :], b[64:128, :]).then_inc(evacuated, 1)
                        elif j < jg:
                            u, t = divmod(j - jv, NT)
                            act.copy(v[:, t, u * UC:(u + 1) * UC], b[:, 0:UC]).then_inc(evacuated, 1)
                        else:
                            u, t = divmod(j - jg, NT)
                            act.activation(fg[:, t, u * UC:(u + 1) * UC], b[:, 0:UC], ACT.Silu).then_inc(evacuated, 1)
                    att.scalar(act)
                    for f in range(NT):
                        act.wait_ge(s_ft, f + 1)
                        act.copy(M[:, 12 + f, :], PS[:, 2 + f % 2, :]).then_inc(s_fe, 1)

                @block.vector
                def _(dve):
                    link = chain(dve, s_fv)
                    dve.wait_ge(s_aug, 32)
                    dve.tensor_scalar(q[96:104, :, :], repeat(F8[0:FH, :], FH), FD ** 0.5, None,
                                      ALU.mult).then_inc(s_fb, 1)
                    dve.tensor_copy(k[64:72, :, :], repeat(F8[0:FH, :], FH)).then_inc(s_fb, 1)

                    def finish(i):
                        dve.wait_ge(att.weighted, FH * (i + 1))
                        dve.wait_ge(att.prob, FH * (i + 1))
                        link(dve.reciprocal(rinv, att.rs[:, FH * i:FH * (i + 1)]))
                        g = split3(fg[:, i, :], FH)
                        link(dve.tensor_tensor(g, g, spread(rinv, FD), ALU.mult))
                        dve.tensor_tensor(g, g, split3(PS[:, i % 2, :], FH), ALU.mult).then_inc(att.taken, 1)
                        dve.wait_ge(att.taken, i + 1)

                    att.vector(dve, finish)
                    dve.sem_inc(s_fx, NT)

            s_xn = evacuated
            with nc.Block() as block:
                @block.sync
                def _(sp):
                    stream.send(sp, W, len(stream.units))

                @block.tensor
                def _(pe):
                    for j in range(J["out"], J["out"] + KD):
                        proj.run(pe, j, M)

                @block.vector
                def _(dve):
                    for m in range(KD):
                        j = J["out"] + m
                        dve.wait_ge(projected, j + 1)
                        dve.scalar_tensor_tensor(X[:, m, :], PS[:, j % 4, :], mod[:, 16 + m:17 + m], X[:, m, :],
                                                 ALU.mult, ALU.add).then_inc(evacuated, 1)

        layers(first_layer)

        s_g, s_sq, s_ss, s_rms, s_rc, s_xn = (sem(f"final_{x}") for x in (
            "gain_loaded", "squared", "square_sum", "rms", "reciprocal", "normed"))
        with nc.Block() as block:
            ar = Arena()
            sq = split3(ar.take(KD * T), KD)
            rms = ar.take(T)
            gain = ar.take(KD)

            @block.sync
            def _(sp):
                sp.dma_start(gain, dr["final_g"]).then_inc(s_g, 16)
                sp.dma_start(spec[:, 0:C2N], dr["c2"]).then_inc(s_g, 16)

            @block.tensor
            def _(pe):
                column_sum(pe, 0, [sq[:, k, :] for k in range(KD)], s_sq).then_inc(s_ss, 1)

            @block.scalar
            def _(act):
                for k in range(KD):
                    act.activation(sq[:, k, :], X[:, k, :], ACT.Square).then_inc(s_sq, 1)
                act.wait_ge(s_ss, 1)
                act.activation(rms, PS[:, 0, :], ACT.Sqrt, bias=EPS, scale=1.0 / D).then_inc(s_rms, 1)

            @block.vector
            def _(dve):
                dve.wait_ge(s_rms, 1)
                dve.reciprocal(rms, rms).then_inc(s_rc, 1)
                dve.wait_ge(s_rc, 1)
                dve.wait_ge(s_g, 32)
                for k in range(KD):
                    dve.scalar_tensor_tensor(X[:, k, :], X[:, k, :], gain[:, k:k + 1], rms,
                                             ALU.mult, ALU.mult).then_inc(s_xn, 1)

        class LayerNorm:

            def __init__(self, name, R, sq, rstd, ready, base, gain, bias):
                self.R, self.sq, self.rstd, self.ready, self.base = R, sq, rstd, ready, base
                self.gain, self.bias = gain, bias
                (self.sum, self.centred, self.squared, self.sqsum, self.std, self.inv, self.scaled,
                 self.done) = (sem(f"{name}_{x}") for x in (
                     "sum", "centred", "squared", "square_sum", "deviation", "inverse", "scaled", "normed"))

            def tensor(self, pe):
                column_sum(pe, 6, [self.R[:, k, :] for k in range(KD)], self.ready, self.base).then_inc(self.sum, 1)
                column_sum(pe, 7, [self.sq[:, k, :] for k in range(KD)], self.squared).then_inc(self.sqsum, 1)

            def scalar(self, act):
                for k in range(KD):
                    act.wait_ge(self.centred, k + 1)
                    act.activation(self.sq[:, k, :], self.R[:, k, :], ACT.Square).then_inc(self.squared, 1)
                act.wait_ge(self.sqsum, 1)
                act.activation(self.rstd, PS[:, 7, :], ACT.Sqrt, bias=LN_EPS, scale=1.0 / D).then_inc(self.std, 1)
                for k in range(KD):
                    act.wait_ge(self.scaled, k + 1)
                    act.activation(X[:, k, :], self.R[:, k, :], ACT.Identity,
                                   bias=self.bias[:, k:k + 1]).then_inc(self.done, 1)

            def vector(self, dve):
                dve.wait_ge(self.sum, 1)
                for k in range(KD):
                    dve.scalar_tensor_tensor(self.R[:, k, :], PS[:, 6, :], -1.0 / D, self.R[:, k, :],
                                             ALU.mult, ALU.add).then_inc(self.centred, 1)
                dve.wait_ge(self.std, 1)
                dve.reciprocal(self.rstd, self.rstd).then_inc(self.inv, 1)
                dve.wait_ge(self.inv, 1)
                dve.wait_ge(self.squared, KD)
                for k in range(KD):
                    dve.scalar_tensor_tensor(self.R[:, k, :], self.R[:, k, :], self.gain[:, k:k + 1], self.rstd,
                                             ALU.mult, ALU.mult).then_inc(self.scaled, 1)

        def feed_forward(l, half, s_par):
            nm = lambda x: sem(f"ffn{half}_{x}")
            s_wl = [nm("gate_up_loaded_0"), nm("gate_up_loaded_1")]
            s_dl = [nm("down_loaded_0"), nm("down_loaded_1")]
            s_g, s_u, s_si, s_h, s_o, s_hf, s_r = (nm(x) for x in (
                "gate_product", "up_product", "gate_activated", "hidden_ready", "down_product",
                "down_halved", "residual_added"))
            ar = Arena()
            hid = split3(ar.take(KF * T), KF)
            wd = split3(ar.take(2 * KF * P), 2)
            R = split3(ar.take(KD * T), KD)
            gs, hf = split3(ar.take(2 * T), 2), split3(ar.take(2 * T), 2)
            ln_i = 0 if half == 0 else 2
            ln = LayerNorm(f"ffn{half}_norm", R, hid[:, 0:KD, :], hid[:, KD, :], s_r, 2,
                           p2("ln_g")[:, ln_i * 8:ln_i * 8 + 8], p2("ln_b")[:, ln_i * 8:ln_i * 8 + 8])
            gu, dn = dr["w_gu"][bass.ds(l, 1)], dr["w_d"][bass.ds(l, 1)]
            with nc.Block() as block:
                @block.sync
                def _(sp):
                    if half == 0:
                        sp.dma_start(par[:, 0:P2N], dr["par2"][bass.ds(l, 1)].rearrange("a p n -> (a p) n")).then_inc(s_par, 16)
                    sp.sem_inc(s_u, 2)
                    sp.sem_inc(s_o, 2)
                    with sp.Fori(0, KF // 2) as i:
                        for b in range(2):
                            sp.wait_ge(s_u, i * 2 + (b + 1))
                            sp.dma_start(W[:, b, :], gu[:, half, bass.ds(i * 2 + b, 1)]
                                         .rearrange("a c p n -> (a c p) n")).then_inc(s_wl[b], 16)
                    with sp.Fori(0, KD // 2) as i:
                        for b in range(2):
                            sp.wait_ge(s_o, i * 2 + (b + 1))
                            sp.dma_start(wd[:, b, :], dn[:, half, bass.ds(i * 2 + b, 1)]
                                         .rearrange("a c p n -> (a c p) n")).then_inc(s_dl[b], 16)

                @block.tensor
                def _(pe):
                    with pe.Fori(0, KF // 2) as i:
                        for b in range(2):
                            w = W[:, b, :].rearrange("p (g k n) -> p g k n", g=2, k=KD)
                            pe.wait_ge(s_wl[b], i * 16 + 16)
                            pe.wait_ge(s_h, i * 2 + (b + 1))
                            for g, s in ((0, s_g), (1, s_u)):
                                for k in range(KD):
                                    last = pe.matmul(PS[:, 2 * b + g, :], w[:, g, k, :], X[:, k, :],
                                                     start=(k == 0), stop=(k == KD - 1))
                                last.then_inc(s, 1)
                    pe.wait_ge(s_h, KF + 2)
                    with pe.Fori(0, KD // 2) as i:
                        for b in range(2):
                            pe.wait_ge(s_dl[b], i * 16 + 16)
                            pe.wait_ge(s_hf, i * 2 + (b + 1))
                            for k in range(KF):
                                last = pe.matmul(PS[:, 4 + b, :], wd[:, b, k * P:(k + 1) * P], hid[:, k, :],
                                                 start=(k == 0), stop=(k == KF - 1))
                            last.then_inc(s_o, 1)
                    ln.tensor(pe)

                @block.scalar
                def _(act):
                    act.sem_inc(s_hf, 2)
                    with act.Fori(0, KF // 2) as i:
                        for b in range(2):
                            act.wait_ge(s_g, i * 2 + (b + 1))
                            act.wait_ge(s_h, i * 2 + (b + 1))
                            act.activation(gs[:, b, :], PS[:, 2 * b, :], ACT.Silu).then_inc(s_si, 1)
                    with act.Fori(0, KD // 2) as i:
                        for b in range(2):
                            act.wait_ge(s_o, i * 2 + (b + 3))
                            act.wait_ge(s_r, i * 2 + (b + 1))
                            act.activation(hf[:, b, :], PS[:, 4 + b, :], ACT.Copy, scale=0.5).then_inc(s_hf, 1)
                    ln.scalar(act)

                @block.vector
                def _(dve):
                    dve.sem_inc(s_h, 2)
                    dve.sem_inc(s_r, 2)
                    with dve.Fori(0, KF // 2) as i:
                        for b in range(2):
                            dve.wait_ge(s_si, i * 2 + (b + 1))
                            dve.wait_ge(s_u, i * 2 + (b + 3))
                            dve.tensor_tensor(hid[:, bass.ds(i * 2 + b, 1), :].rearrange("p a t -> p (a t)"),
                                              PS[:, 2 * b + 1, :], gs[:, b, :], ALU.mult).then_inc(s_h, 1)
                    with dve.Fori(0, KD // 2) as i:
                        for b in range(2):
                            dve.wait_ge(s_hf, i * 2 + (b + 3))
                            m = bass.ds(i * 2 + b, 1)
                            dve.scalar_tensor_tensor(R[:, m, :].rearrange("p a t -> p (a t)"),
                                                     X[:, m, :].rearrange("p a t -> p (a t)"), ALPHA,
                                                     hf[:, b, :], ALU.mult, ALU.add).then_inc(s_r, 1)
                    dve.wait_ge(s_par, 16)
                    ln.vector(dve)

        def mix_tokens(l):
            stream = Stream([sem(f"mix_weights_loaded_{i}") for i in range(SLOTS)])
            projected, evacuated = sem("mix_projected"), sem("mix_evacuated")
            proj = Project(stream, projected, evacuated)

            def drl(name, *ix):
                t = dr[name][bass.ds(l, 1)]
                for i in ix:
                    t = t[:, i]
                return t.rearrange("a p n -> (a p) n")

            two = [(0, P), (P, P)]
            wu = lambda i: drl("w_in2", i)
            J = {}
            J["ga"] = proj.feature_major(drl("w_ga"), 16, [(0, 16)])
            J["g"] = proj.feature_major(wu(5), UC, two)
            J["gv"] = proj.token_major(wu(8), UC)
            J["kc"] = proj.feature_major(wu(2), UC, two)
            J["u"] = proj.feature_major(wu(4), UC, two)
            J["gr"] = proj.feature_major(wu(6), UC, two)
            end_1 = len(stream.units)
            J["gl"] = proj.token_major(drl("w_gl"), 24)
            J["nq"] = [proj.feature_major(wu(i), UC, two) for i in (0, 1)][0]
            J["k"] = proj.feature_major(wu(3), UC, two)
            J["v"] = proj.token_major(wu(7), UC)
            end_2 = len(stream.units)
            J["out"] = [proj.feature_major(drl("w_out2", i), UC, two) for i in range(4)][0]

            otok = split3(h_all[:, 0:4 * T], 4)
            vbd = split3(h_all[:, 2048:2560], 2)
            kc = split3(h_all[0:64, 2560:2624], 2)

            nb = lambda n: sem("gla_" + n)
            s_mw = nb("small_weights_loaded")
            s_z, s_lg, s_x, s_mg, s_ex, s_w1, s_ln = (nb(x) for x in (
                "buffers_zeroed", "gate_logits", "gate_biased", "gate_magnitude", "gate_exp", "gate_one_plus",
                "gate_log"))
            s_v, s_b, s_e, s_qt, s_bd, s_kt, s_kk, s_kkc = (nb(x) for x in (
                "vector_step", "log_decay", "decays_ready", "q_ready", "q_spread", "k_ready", "k_turned",
                "k_turned_copied"))
            s_at, s_am, s_ds, s_st, s_o, s_oc = (nb(x) for x in (
                "scores", "scores_masked", "state_products", "state_ready", "output", "output_copied"))
            s_s2, s_r, s_n, s_t = (nb(x) for x in ("square_sums", "rms", "normed", "turned"))
            s_pp, s_pd, s_pm, s_pw = (sem("pool_" + x) for x in ("step", "pooled", "product", "scaled"))
            s_pe, s_c1, s_cg, s_c2, s_cc = (sem("cmp_" + x) for x in (
                "position_added", "first_product", "activated", "second_product", "copied"))
            s_fin = nb("tile_done")
            with nc.Block() as block:
                ar = Arena()
                w1 = ar.take(4096).rearrange("p (v l e) -> p v l e", v=2, l=CB)
                zr = ar.take(2048).rearrange("p (v g t) -> p v g t", v=2, g=2)
                zflat = ar.take(4096)
                zp = zflat.rearrange("p (v a g t) -> p v a g t", v=2, a=2, g=2)
                sw = ar.take(128 + 64 + 256 + 128)
                gq, gk, b, e1, e2, kt, kd, xg = (ar.take(T) for _ in range(8))
                qbd = ar.take(2048).rearrange("p (c h i) -> p c h i", c=NGC, h=GH)
                AT = split3(ar.take(512), 2)
                Sb = ar.take(256)
                kdt = split3(ar.take(NGC * P), NGC)
                gaT = h_all[:, 2624:2624 + T]
                up = split3(ar.take(2 * 528), 2)
                pa, pb = ar.take(528), ar.take(528)
                pooled = split3(ar.take(2 * T), 2)
                act_g = ar.take(128).rearrange("p (v g n) -> p v g n", v=2, g=2)
                dcy = ar.take(NGC)
                ss = ar.take(32)
                mag, one, lgt, qt = (ar.take(T) for _ in range(4))
                gv = split3(m_all[0:64, 8 * T:12 * T], NGC)
                oa = split3(m_all[0:64, 12 * T:16 * T], NGC)
                osq = split3(zflat[0:64, 0:2048], NGC)
                jg, jv, jc, ju, jr, je = J["g"], J["gv"], J["kc"], J["u"], J["gr"], J["gl"]

                @block.sync
                def _(sp):
                    sp.dma_start(w1[0:64].rearrange("p v l e -> p (v l e)"), drl("w_c1")).then_inc(s_mw, 16)
                    sp.dma_start(sw, drl("w_small")).then_inc(s_mw, 16)
                    stream.send(sp, W, end_1 + SLOTS)

                @block.gpsimd
                def _(pool):
                    pool.memset(qbd, 0.0).then_inc(s_z, 1)
                    pool.memset(AT, 0.0).then_inc(s_z, 1)
                    pool.memset(Sb, 0.0).then_inc(s_z, 1)
                    pool.memset(vbd, 0.0).then_inc(s_z, 1)
                    pool.memset(h_all[0:64, 2560:2624], 0.0).then_inc(s_z, 1)
                    pool.memset(up[:, :, 0:16], 0.0).then_inc(s_z, 1)
                    pool.memset(pa[:, 0:16], 0.0).then_inc(s_z, 1)
                    pool.memset(pb[:, 0:16], 0.0).then_inc(s_z, 1)
                    pool.wait_ge(s_mw, 32)
                    pool.wait_ge(evacuated, jc + 2)
                    for v in range(2):
                        for a in range(2):
                            z3 = lambda t: t.rearrange("p g (n l) -> p (g n) l", l=CS)
                            pool.tensor_tensor(z3(zp[0:64, v, a]), z3(zr[0:64, v]),
                                               repeat(sw[0:64, 128 + 32 * v + CS * a:128 + 32 * v + CS * (a + 1)], 64),
                                               ALU.add).then_inc(s_pe, 1)
                    link = chain(pool, s_pp)
                    pool.wait_ge(s_z, 8)
                    for t in range(2):
                        pool.wait_ge(evacuated, ju + t + 1)
                        src, w, bufs = up[:, t, :], 1, [pa, pb]
                        for n in range(2 + 2 * t):
                            dst = bufs[n % 2]
                            link(pool.tensor_tensor(dst[:, 16:528], src[:, 16:528], src[:, 16 - w:528 - w], ALU.add))
                            src, w = dst, 2 * w
                            half = {(0, 0): 0, (0, 1): 1, (1, 2): 0, (1, 3): 1}.get((t, n))
                            if half is not None:
                                r = slice(64 * half, 64 * half + 64)
                                inv = spec[r, C2["invcnt"][0] + t * T:C2["invcnt"][0] + (t + 1) * T]
                                link(pool.tensor_tensor(pooled[r, t, :], dst[r, 16:528], inv, ALU.mult))
                        pool.tensor_tensor(pooled[:, t, :], pooled[:, t, :], up[:, t, 16:528],
                                           ALU.subtract).then_inc(s_pd, 1)

                @block.tensor
                def _(pe):
                    for j in range(0, jc):
                        proj.run(pe, j, X)
                    pe.wait_ge(s_mw, 32)
                    pe.matmul(PS[:, 4, :], sw[0:16, 448:576], gaT[0:16, :], start=True, stop=True).then_inc(s_lg, 1)
                    for j in range(jc, je):
                        proj.run(pe, j, X)
                    pe.wait_ge(s_kt, 2)
                    pe.wait_ge(s_x, 1)
                    for c in range(NGC):
                        last = pe.transpose(PS[0:64, 4 + c // 4, (c % 4) * P:(c % 4 + 1) * P],
                                            kd[:, c * GC:(c + 1) * GC], ident)
                        if c % 4 == 3:
                            last.then_inc(s_kk, 1)
                    pe.wait_ge(s_kkc, 2)
                    pe.wait_ge(s_bd, 4)
                    pe.wait_ge(s_qt, 1)
                    pe.wait_ge(evacuated, je)

                    def scores(c):
                        if c >= 2:
                            pe.wait_ge(s_am, c - 1)
                        pe.matmul(PS[0:64, 4 + c % 2, 0:256], kt[:, c * GC:(c + 1) * GC],
                                  qbd[:, c, :, :], start=True, stop=True).then_inc(s_at, 1)

                    scores(0)
                    for c in range(NGC):
                        if c + 1 < NGC:
                            scores(c + 1)
                        if c >= 2:
                            pe.wait_ge(s_oc, c - 1)
                        if c < NGC - 1:
                            if c >= 2:
                                pe.wait_ge(s_st, c - 1)
                            pe.matmul(PS[:, c % 2, 0:256], kdt[0:64, c, :], gv[:, c, :],
                                      start=True, stop=True).then_inc(s_ds, 1)
                        if c:
                            pe.wait_ge(s_st, c)
                            pe.matmul(PS[0:64, 6 + c % 2, 0:256], qt[:, c * GC:(c + 1) * GC], Sb,
                                      start=True, stop=False, skip_group_check=True)
                        pe.wait_ge(s_am, c + 1)
                        for h in range(GH):
                            last = pe.matmul(PS[0:64, 6 + c % 2, h * GV:(h + 1) * GV],
                                             AT[0:64, c % 2, h * GC:(h + 1) * GC], gv[:, c, h * GV:(h + 1) * GV],
                                             start=(c == 0), stop=True, skip_group_check=True)
                        last.then_inc(s_o, 1)
                    pe.wait_ge(s_pe, 4)
                    for v in range(2):
                        for l_ in range(CB):
                            a, r = divmod(l_, CS)
                            rhs = zp[0:64, v, a].rearrange("p g (n l) -> p g n l", l=CS)[:, :, a:a + NCMP, r]
                            last = pe.matmul(PS[0:64, 2 + v, 0:2 * NCMP], w1[0:64, v, l_, :], rhs,
                                             start=(l_ == 0), stop=(l_ == CB - 1))
                        last.then_inc(s_c1, 1)
                    for t in range(2):
                        pe.wait_ge(s_pd, t + 1)
                        pe.wait_ge(s_am, NGC)
                        pe.matmul(PS[:, 4 + t, :], sw[:, 192 + t * P:192 + (t + 1) * P], pooled[:, t, :],
                                  start=True, stop=True).then_inc(s_pm, 1)
                    pe.wait_ge(s_cg, 2)
                    pe.wait_ge(s_st, NGC - 1)
                    pe.matmul(PS[0:64, 0, 0:2 * NCMP], sw[0:64, 0:64],
                              act_g[0:64, 0].rearrange("p g n -> p (g n)")[:, 0:2 * NCMP],
                              start=True, stop=True).then_inc(s_c2, 1)
                    for g in range(NG):
                        last = pe.matmul(PS[0:NCMP, 1, g * HD:(g + 1) * HD],
                                         act_g[0:64, 1].rearrange("p g n -> p (g n)")[:, g * NCMP:(g + 1) * NCMP],
                                         sw[0:64, 64:128], start=True, stop=True)
                    last.then_inc(s_c2, 1)
                    pe.wait_ge(s_n, 1)
                    for t in range(2):
                        pe.wait_ge(s_oc, NGC)
                        for c in range(NGC):
                            last = pe.transpose(PS[:, 6 + t, c * GC:(c + 1) * GC], oa[:, c, t * P:(t + 1) * P],
                                                ident[0:64, 0:64])
                        last.then_inc(s_t, 1)

                @block.scalar
                def _(act):
                    def evacuate(j):
                        act.wait_ge(projected, j + 1)
                        bk = PS[:, j % 4, :]
                        if j < jg:
                            ins = act.copy(gaT[0:16, :], bk[0:16, :])
                        elif j < jv:
                            ins = act.copy(gq if j == jg else gk, bk)
                        elif j < jc:
                            t = j - jv
                            act.copy(gv[:, 2 * t, :], bk[0:64, 0:256])
                            ins = act.copy(gv[:, 2 * t + 1, :], bk[64:128, 0:256])
                        elif j < ju:
                            act.copy(zr[0:64, j - jc, 0, :], bk[0:64, :])
                            ins = act.copy(zr[0:64, j - jc, 1, :], bk[64:128, :])
                        elif j < jr:
                            ins = act.copy(up[:, j - ju, 16:528], bk)
                        else:
                            ins = act.activation(M[:, 6 + j - jr, :], bk, ACT.Silu)
                        ins.then_inc(evacuated, 1)

                    for j in range(0, jc):
                        evacuate(j)
                    act.wait_ge(s_lg, 1)
                    act.activation(xg, PS[:, 4, :], ACT.Identity, bias=p2("gla_ba")).then_inc(s_x, 1)
                    for j in range(jc, je):
                        evacuate(j)
                    act.wait_ge(s_mg, 1)
                    act.activation(e1, mag, ACT.Exp, scale=-1.0).then_inc(s_ex, 1)
                    act.wait_ge(s_w1, 1)
                    act.activation(lgt, one, ACT.Ln).then_inc(s_ln, 1)
                    act.wait_ge(s_b, 1)
                    act.activation(e1, b, ACT.Exp).then_inc(s_e, 1)
                    act.activation(e2, b, ACT.Exp, scale=-1.0).then_inc(s_e, 1)
                    act.activation(dcy, b.rearrange("p (c i) -> p c i", c=NGC)[:, :, GC - 1], ACT.Exp).then_inc(s_e, 1)
                    act.wait_ge(s_b, 2)
                    act.activation(mag, mag, ACT.Exp).then_inc(s_e, 1)
                    act.wait_ge(s_z, 1)
                    act.wait_ge(s_qt, 1)
                    for h in range(GH):
                        r = slice(GK * h, GK * (h + 1))
                        act.copy(qbd[r, :, h, :], split3(qt[r, :], NGC)).then_inc(s_bd, 1)
                    for n in range(2):
                        act.wait_ge(s_kk, n + 1)
                        act.copy(kdt[0:64, 4 * n:4 * n + 4, :], split3(PS[0:64, 4 + n, :], 4)).then_inc(s_kkc, 1)
                    for c in range(NGC):
                        act.wait_ge(s_o, c + 1)
                        act.copy(oa[:, c, :], PS[0:64, 6 + c % 2, 0:256]).then_inc(s_oc, 1)
                    for v in range(2):
                        act.wait_ge(s_c1, v + 1)
                        act.activation(act_g[0:64, v].rearrange("p g n -> p (g n)")[:, 0:2 * NCMP],
                                       PS[0:64, 2 + v, 0:2 * NCMP], ACT.Gelu_apprx_tanh).then_inc(s_cg, 1)
                    for t in range(2):
                        act.wait_ge(s_pm, t + 1)
                        act.activation(M[:, 4 + t, :], PS[:, 4 + t, :], ACT.Copy,
                                       scale=p2("pool_s")[:, t:t + 1]).then_inc(s_pw, 1)
                    act.wait_ge(s_z, 5)
                    act.wait_ge(s_c2, 1)
                    act.copy(kc[:, :, 0:NCMP], PS[0:64, 0, 0:2 * NCMP].rearrange("p (g n) -> p g n", g=2)).then_inc(s_cc, 1)
                    act.wait_ge(s_c2, 2)
                    for g in range(NG):
                        for r in range(4):
                            act.copy(vbd[32 * r:32 * r + NCMP, g, r * HD:(r + 1) * HD],
                                     PS[0:NCMP, 1, g * HD:(g + 1) * HD]).then_inc(s_cc, 1)
                    act.wait_ge(s_s2, 1)
                    act.activation(ss[0:64, :], ss[0:64, :], ACT.Sqrt, bias=EPS, scale=1.0 / GV).then_inc(s_r, 1)

                @block.vector
                def _(dve):
                    link = chain(dve, s_v)
                    dve.wait_ge(s_x, 1)
                    dve.scalar_tensor_tensor(mag, xg, -1.0, xg, ALU.mult, ALU.max).then_inc(s_mg, 1)
                    dve.wait_ge(s_ex, 1)
                    dve.tensor_scalar(one, e1, 1.0, None, ALU.add).then_inc(s_w1, 1)
                    dve.wait_ge(s_w1, 1)
                    link(dve.scalar_tensor_tensor(mag, one, 1.0, e1, ALU.subtract, ALU.subtract))
                    dve.wait_ge(s_ln, 1)
                    link(dve.reciprocal(one, one))
                    link(dve.tensor_tensor(mag, mag, one, ALU.mult))
                    link(dve.tensor_tensor(lgt, lgt, mag, ALU.subtract))
                    link(dve.scalar_tensor_tensor(xg, xg, 0.0, lgt, ALU.min, ALU.subtract))
                    link(dve.tensor_scalar(xg, xg, 1.0 / 16.0, None, ALU.mult))
                    dve.tensor_tensor_scan(b, const("reset", C2, spec), xg, 0.0, ALU.mult, ALU.add).then_inc(s_b, 1)
                    dve.wait_ge(s_b, 1)
                    b3 = b.rearrange("p (c i) -> p c i", c=NGC)
                    dve.tensor_tensor(split3(mag, NGC), spread(b3[:, :, GC - 1], GC), b3, ALU.subtract).then_inc(s_b, 1)
                    dve.wait_ge(s_e, 1)
                    dve.wait_ge(evacuated, jv)
                    dve.scalar_tensor_tensor(qt, gq, GK ** -0.5, e1, ALU.mult, ALU.mult).then_inc(s_qt, 1)
                    dve.wait_ge(s_e, 2)
                    dve.tensor_tensor(kt, gk, e2, ALU.mult).then_inc(s_kt, 1)
                    dve.wait_ge(s_e, 4)
                    dve.tensor_tensor(kd, gk, mag, ALU.mult).then_inc(s_kt, 1)
                    gm = const("gmask", C2, spec)[0:64, :].bitcast(mybir.dt.uint32)
                    dve.wait_ge(s_z, 3)

                    def mask(c):
                        dve.wait_ge(s_at, c + 1)
                        if c >= 2:
                            dve.wait_ge(s_o, c - 1)
                        dve.copy_predicated(AT[0:64, c % 2, :], gm, PS[0:64, 4 + c % 2, 0:256]).then_inc(s_am, 1)

                    mask(0)
                    for c in range(NGC):
                        if c + 1 < NGC:
                            mask(c + 1)
                            dve.wait_ge(s_ds, c + 1)
                            if c:
                                dve.wait_ge(s_o, c + 1)
                                dve.wait_ge(s_st, c)
                            for h in range(GH):
                                r = slice(GK * h, GK * (h + 1))
                                cs = slice(GV * h, GV * (h + 1))
                                last = dve.scalar_tensor_tensor(Sb[r, cs], Sb[r, cs], dcy[r, c:c + 1],
                                                                PS[r, c % 2, cs], ALU.mult, ALU.add)
                            last.then_inc(s_st, 1)
                    dve.wait_ge(s_oc, NGC)
                    dve.wait_ge(s_c1, 2)
                    link(dve.tensor_tensor(osq, oa, oa, ALU.mult))
                    dve.tensor_reduce(ss[0:64, :], osq.rearrange("p c (h v) -> p (c h) v", h=GH), AX.X,
                                      ALU.add).then_inc(s_s2, 1)
                    dve.wait_ge(s_r, 1)
                    link(dve.reciprocal(ss[0:64, :], ss[0:64, :]))
                    o3 = oa.rearrange("p c (h v) -> p (c h) v", h=GH)
                    dve.tensor_tensor(o3, o3, spread(ss[0:64, :], GV), ALU.mult).then_inc(s_n, 1)
                    for t in range(2):
                        dve.wait_ge(s_t, t + 1)
                        dve.scalar_tensor_tensor(M[:, 6 + t, :], PS[:, 6 + t, :], p2("gla_g")[:, t:t + 1],
                                                 M[:, 6 + t, :], ALU.mult, ALU.mult).then_inc(s_fin, 1)

            s_cs, s_cd, s_ce, s_cn, s_cv, s_ct, s_ctc, s_co, s_cf = (sem("cmpatt_" + x) for x in (
                "scored", "shifted", "exp", "normed", "vector_step", "turned", "turned_copied", "weighted", "added"))
            s_os, s_ot, s_oe = (sem("nsa_" + x) for x in ("output_done", "output_turned", "output_copied"))
            with nc.Block() as block:
                ar = Arena()
                q = split3(ar.take(NH * T), NH)
                kk = ar.take(4 * T).rearrange("p (w g t) -> p w g t", w=2, g=2)
                v = split3(ar.take(4 * 256), 4)
                gl = split3(ar.take(96), 4)
                buf = (split3(ar.take(2 * T), 2), split3(ar.take(2 * T), 2), split3(ar.take(2 * T), 2),
                       ar.take(32), ar.take(32))
                pc = split3(ar.take(4 * 256), 4)
                pct = split3(ar.take(2 * 256), 2)
                mx, den, coef = ar.take(8), ar.take(8), ar.take(8)
                tmp = ar.take(T)
                att = [Attention(n, NH, q, (lambda w: lambda h: kk[:, w, h // 4, :])(w),
                                 (lambda w: lambda h, t: v[:, t, w * P + (h // 4) * HD:w * P + (h // 4 + 1) * HD])(w),
                                 64, buf) for w, n in enumerate(("selected", "window"))]
                jl, jq, jk, jv, je = J["gl"], J["nq"], J["k"], J["v"], J["out"]

                @block.sync
                def _(sp):
                    stream.send(sp, W, end_2 + SLOTS)

                @block.tensor
                def _(pe):
                    for j in range(jl, je):
                        proj.run(pe, j, X)
                    pe.wait_ge(evacuated, je)
                    for i in range(NT):
                        if i >= 2:
                            pe.wait_ge(s_cd, i - 1)
                        for h in range(NH):
                            last = pe.matmul(PS[:, 4 + i % 2, h * 32:(h + 1) * 32], q[0:64, h, i * P:(i + 1) * P],
                                             kc[:, h // 4, :], start=True, stop=True)
                        last.then_inc(s_cs, 1)
                    for i in range(NT):
                        pe.wait_ge(s_cn, i + 1)
                        if i >= 2:
                            pe.wait_ge(s_ctc, i - 1)
                        for g in range(NG):
                            last = pe.transpose(PS[:, 6 + i % 2, g * P:(g + 1) * P], pc[:, i, g * P:(g + 1) * P], ident)
                        last.then_inc(s_ct, 1)
                        pe.wait_ge(s_ctc, i + 1)
                        if i >= 2:
                            pe.wait_ge(s_cf, i - 1)
                        for g in range(NG):
                            last = pe.matmul(PS[:, i % 2, g * 256:(g + 1) * 256], pct[:, i % 2, g * P:(g + 1) * P],
                                             vbd[:, g, :], start=True, stop=True)
                        last.then_inc(s_co, 1)
                    pe.wait_ge(s_cf, NT)
                    for a in att:
                        a.tensor(pe)
                    for f in range(NT):
                        if f == 0:
                            pe.wait_ge(s_os, 1)
                        if f >= 2:
                            pe.wait_ge(s_oe, f - 1)
                        for i in range(NT):
                            last = pe.transpose(PS[:, 2 + f % 2, i * P:(i + 1) * P], otok[:, i, f * P:(f + 1) * P], ident)
                        last.then_inc(s_ot, 1)

                @block.scalar
                def _(act):
                    for j in range(jl, je):
                        act.wait_ge(projected, j + 1)
                        bk = PS[:, j % 4, :]
                        if j < jq:
                            ins = act.activation(gl[:, j - jl, :], bk[:, 0:24], ACT.Sigmoid)
                        elif j < jv:
                            d = (lambda h: q[0:64, 2 * (j - jq) + h, :]) if j < jk else (lambda h: kk[0:64, j - jk, h, :])
                            act.copy(d(0), bk[0:64, :])
                            ins = act.copy(d(1), bk[64:128, :])
                        else:
                            ins = act.copy(v[:, j - jv, :], bk[:, 0:256])
                        ins.then_inc(evacuated, 1)
                    for i in range(NT):
                        act.wait_ge(s_cd, i + 1)
                        act.activation(pc[:, i, :], pc[:, i, :], ACT.Exp, scale=HD ** -0.5).then_inc(s_ce, 1)
                    for i in range(NT):
                        act.wait_ge(s_ct, i + 1)
                        if i >= 2:
                            act.wait_ge(s_co, i - 1)
                        act.copy(pct[:, i % 2, :], PS[:, 6 + i % 2, 0:256]).then_inc(s_ctc, 1)
                    for a in att:
                        a.scalar(act)
                    for f in range(NT):
                        act.wait_ge(s_ot, f + 1)
                        act.copy(M[:, f, :], PS[:, 2 + f % 2, :]).then_inc(s_oe, 1)

                @block.vector
                def _(dve):
                    link = chain(dve, s_cv)
                    gates = gl.rearrange("p i (h w) -> p i h w", w=3)
                    add = split3(const("cmpadd", C2, spec), 4)
                    keep = split3(const("cmpmul", C2, spec), 4)
                    for i in range(NT):
                        dve.wait_ge(s_cs, i + 1)
                        p3 = split3(pc[:, i, :], NH)
                        link(dve.tensor_tensor(p3, split3(PS[:, 4 + i % 2, 0:256], NH), repeat(add[:, i, :], NH), ALU.add))
                        link(dve.tensor_reduce(mx, p3, AX.X, ALU.max))
                        dve.tensor_tensor(p3, p3, spread(mx, 32), ALU.subtract).then_inc(s_cd, 1)
                        dve.wait_ge(s_cd, i + 1)
                    for i in range(NT):
                        dve.wait_ge(s_ce, i + 1)
                        p3 = split3(pc[:, i, :], NH)
                        link(dve.tensor_tensor(p3, p3, repeat(keep[:, i, :], NH), ALU.mult))
                        link(dve.tensor_reduce(den, p3, AX.X, ALU.add))
                        link(dve.tensor_scalar(den, den, 1e-30, None, ALU.max))
                        link(dve.reciprocal(den, den))
                        dve.tensor_tensor(p3, p3, spread(den, 32), ALU.mult).then_inc(s_cn, 1)
                        dve.wait_ge(s_cn, i + 1)
                    for i in range(NT):
                        dve.wait_ge(s_co, i + 1)
                        dve.tensor_tensor(split3(otok[:, i, :], NH), split3(PS[:, i % 2, :], NH),
                                          spread(gates[:, i, :, 0], HD), ALU.mult).then_inc(s_cf, 1)

                    def finish_of(w):
                        a = att[w]

                        def finish(i):
                            dve.wait_ge(a.weighted, NH * (i + 1))
                            dve.wait_ge(a.prob, NH * (i + 1))
                            link(dve.reciprocal(coef, a.rs[:, NH * i:NH * (i + 1)]))
                            link(dve.tensor_tensor(coef, coef, gates[:, i, :, w + 1], ALU.mult))
                            dve.tensor_tensor(split3(tmp, NH), split3(PS[:, i % 2, :], NH), spread(coef, HD),
                                              ALU.mult).then_inc(a.taken, 1)
                            dve.wait_ge(a.taken, i + 1)
                            link(dve.tensor_tensor(otok[:, i, :], otok[:, i, :], tmp, ALU.add))
                        return finish

                    dve.wait_ge(s_cf, NT)
                    for w in range(2):
                        att[w].vector(dve, finish_of(w))
                    dve.sem_inc(s_os, 1)

            s_hr = sem("mix_residual_added")
            with nc.Block() as block:
                ar = Arena()
                R = split3(ar.take(KD * T), KD)
                sq = split3(ar.take(KD * T), KD)
                rstd = ar.take(T)
                ln = LayerNorm("mix_norm", R, sq, rstd, evacuated, J["out"],
                               p2("ln_g")[:, 8:16], p2("ln_b")[:, 8:16])

                @block.sync
                def _(sp):
                    stream.send(sp, W, len(stream.units))

                @block.tensor
                def _(pe):
                    for j in range(J["out"], J["out"] + KD):
                        proj.run(pe, j, M)
                    ln.tensor(pe)

                @block.scalar
                def _(act):
                    ln.scalar(act)

                @block.vector
                def _(dve):
                    for m in range(KD):
                        j = J["out"] + m
                        dve.wait_ge(projected, j + 1)
                        dve.scalar_tensor_tensor(R[:, m, :], X[:, m, :], ALPHA, PS[:, j % 4, :],
                                                 ALU.mult, ALU.add).then_inc(evacuated, 1)
                    dve.wait_ge(evacuated, J["out"] + KD)
                    ln.vector(dve)

        def second_layer(l):
            s_par = sem("parameters2_loaded")
            feed_forward(l, 0, s_par)
            mix_tokens(l)
            feed_forward(l, 1, s_par)

        layers(second_layer)

        s_out = sem("output_stored")
        with nc.Block() as block:
            @block.sync
            def _(sp):
                sp.dma_start(out, x_all[:, :]).then_inc(s_out, 16)
                sp.wait_ge(s_out, 16)


def constants():
    f = np.float32
    i = np.arange(P)
    c0 = np.zeros((P, C0N), f)
    c0[:, 0:128] = np.eye(P)
    c0[:, 128:256] = 1.0
    c0[:, 256:384] = i[:, None] <= i[None, :]
    c0[:, 768:896] = np.where(i[None, :] > i[:, None], -BIG, 0.0)
    c0[:, 896] = (10000.0 ** (-(i % 64) / 64.0)).astype(f)
    c0[:, 897] = np.where(i < 64, -1.0, 1.0)
    c1 = np.zeros((P, C1N), f)
    lg = np.log(1.0 - 2.0 ** (-5.0 - np.arange(RH)))
    diff = i[None, :] - i[:, None]
    for h in range(RH):
        c1[:, h * P:(h + 1) * P] = np.where(diff >= 0, np.exp(lg[h] * np.maximum(diff, 0)), 0.0) * P ** -0.5
        c1[:, 512 + h * P:512 + (h + 1) * P] = np.exp(lg[h] * (i + 1.0))[None, :]
        c1[:, 1024 + h] = np.exp(lg[h] * (P - 1.0 - i)) * P ** -0.5
    c2 = np.zeros((P, C2N), f)
    t = np.arange(T)
    c2[:, 0:512] = (t % GC != 0)
    for n, w in enumerate((2, 4, 8, 16)):
        a, r = divmod(n, 2)
        c2[64 * r:64 * r + 64, 512 + a * T:512 + (a + 1) * T] = 1.0 / np.minimum(w, t + 1)
    for q in range(NT):
        ok = (np.arange(32)[None, :] * CS + CB - 1 <= (q * P + i)[:, None]) & (np.arange(32) < NCMP)[None, :]
        c2[:, 1536 + 32 * q:1568 + 32 * q] = np.where(ok, 0.0, -BIG)
        c2[:, 1664 + 32 * q:1696 + 32 * q] = ok
    c2[:, 1792:2048] = np.tile((np.arange(GC)[None, :] >= i[:, None]), (1, 4))
    sel = np.zeros((SH, SH * P), f)
    for h in range(SH):
        sel[h, h * P:(h + 1) * P] = 1.0
    aug_q, aug_k = np.zeros((40, FH, T), f), np.zeros((40, FH, T), f)
    for h in range(FH):
        aug_q[h, h] = -(FD ** 0.5)
        aug_k[32 + h, h] = 1.0
    return dict(c0=c0, c1=c1, c2=c2, sel=sel, aug_q=aug_q.reshape(40, -1), aug_k=aug_k.reshape(40, -1))


def layout(a):
    def units(w, cols, n):
        L, K, _ = w.shape
        w = w[:, :, cols].reshape(L, K // P, P, len(cols) // n, n)
        return np.ascontiguousarray(w.transpose(0, 3, 2, 1, 4)).reshape(L, len(cols) // n, P, -1)

    def column(v):
        return np.moveaxis(v.reshape(v.shape[:-1] + (-1, P)), -1, -2)

    def rows(v):
        return np.broadcast_to(v[:, None, :], (DEPTH, P, v.shape[-1]))

    r = lambda o, n: np.arange(o, o + n)
    off = np.cumsum([0, 512, 512, 512, 512, 1536, 16, 1024, 512, 512, 512, 512, 8])
    rq, rk, rv, rg, xbc, dt, z, fq, fk, fv, fg, fr = off[:12]
    cols = np.concatenate([r(rq, 512), r(rk, 512), r(rg, 512), r(rv, 512), r(xbc + 1024, 512), r(xbc, 1024),
                           r(z, 1024), r(fq, 512), r(fk, 512), r(fv, 512), r(fg, 512)])
    d = dict(w_ada=units(a["w_ada"], r(0, 3072), UC), w_in=units(a["w_in"], cols, UC),
             w_dtf=units(a["w_in"], np.concatenate([r(dt, 16), r(fr, 8)]), 24)[:, 0],
             w_out=units(a["w_out"], r(0, D), P))
    conv = np.concatenate([column(a["conv_w"][:, k]) for k in range(CONV_K)], axis=2)
    d["par1"] = np.concatenate([column(a["norm_g"]), column(a["b_ada"]), conv, column(a["conv_b"]),
                                column(a["ssd_norm_g"]), rows(a["dt_bias"]), rows(a["b_forget"]),
                                rows(a["a_log"]), rows(a["d_skip"])], axis=2)
    d["final_g"] = column(a["final_g"])
    d["c"] = column(a["c"])[0]
    d["pos"] = np.broadcast_to(a["positions"], (P, T))
    d["x"] = a["x"][0].T.reshape(KD, P, T).transpose(1, 0, 2).reshape(P, KD * T)
    off = np.cumsum([0, 512, 128, 128, 128, 128, 128, 128, 24, 256, 128, 128, 256, 16, 256])
    nq, kc, vc, ks, vs, kw, vw, gl, u, gq, gk, gv, ga, gr = off[:14]
    cols = np.concatenate([r(nq, 512), r(kc, 256), r(ks, 128), r(kw, 128), r(u, 256), r(gq, 256), r(gr, 256),
                           r(vs, 128), r(vw, 128), r(gv, 256)])
    w = a["w_in_2"]
    d["w_in2"] = units(w, cols, UC)
    d["w_ga"] = units(w, r(ga, 16), 16)[:, 0]
    d["w_gl"] = units(w, r(gl, 24), 24)[:, 0]
    d["w_out2"] = units(a["w_out_2"], r(0, D), UC)
    wg, wu = (a[n].reshape(2 * DEPTH, D, FF) for n in ("ffn_wg_2", "ffn_wu_2"))
    gu = np.stack([units(wg, r(0, FF), P), units(wu, r(0, FF), P)], axis=3)
    d["w_gu"] = gu.reshape(DEPTH, 2, KF, P, 2 * D)
    d["w_d"] = units(a["ffn_wd_2"].reshape(2 * DEPTH, FF, D), r(0, D), P).reshape(DEPTH, 2, KD, P, FF)
    d["w_c1"] = a["cmp_w1_2"].reshape(DEPTH, 2, CB, HD, HD).transpose(0, 3, 1, 2, 4).reshape(DEPTH, HD, -1)
    s = np.zeros((DEPTH, P, 576), np.float32)
    s[:, 0:64, 0:128] = a["cmp_w2_2"].transpose(0, 2, 1, 3).reshape(DEPTH, 64, 128)
    s[:, 0:64, 128:192] = a["cmp_pe_2"].transpose(0, 3, 1, 2).reshape(DEPTH, 64, 64)
    for n in range(4):
        t, q = divmod(n, 2)
        s[:, 64 * q:64 * q + 64, 192 + P * t + 64 * q:192 + P * t + 64 * q + 64] = a["pool_w_2"][:, n]
    s[:, 0:16, 448:576] = a["gla_wa2_2"]
    d["w_small"] = s
    ln_g, ln_b = (column(a[n]).transpose(0, 2, 1, 3).reshape(DEPTH, P, 24) for n in ("ln_g_2", "ln_b_2"))
    d["par2"] = np.concatenate([ln_g, ln_b, column(a["pool_scale_2"]), column(a["gla_ba_2"]),
                                column(a["gla_norm_g_2"])], axis=2)
    return {k: np.ascontiguousarray(v) for k, v in d.items()}


def kernel(**inputs):
    import concourse.bacc as bacc
    from concourse.bass_utils import run_bass_kernel_spmd

    arrays = layout({k: np.asarray(v) for k, v in inputs.items()})
    arrays.update(constants())
    nc = bacc.Bacc("TRN2", target_bir_lowering=False, num_devices=1)
    dr = {k: nc.dram_tensor(f"in_{k}", v.shape, mybir.dt.from_np(v.dtype), kind="ExternalInput").ap()
          for k, v in arrays.items()}
    out = nc.dram_tensor("out", (P, KD * T), F32, kind="ExternalOutput").ap()
    build(nc, dr, out)
    r = run_bass_kernel_spmd(nc, [{f"in_{k}": v for k, v in arrays.items()}], core_ids=[0])
    o = r.results[0]["out"].reshape(P, KD, T).transpose(2, 1, 0).reshape(1, T, D)
    return np.ascontiguousarray(o)
```

```python
from contextlib import ExitStack

import numpy as np

import concourse.bass as bass
from concourse import mybir
from concourse.alu_op_type import AluOpType as ALU

F32 = mybir.dt.float32
F32R = mybir.dt.float32r
I32 = mybir.dt.int32
ACT = mybir.ActivationFunctionType
AX = mybir.AxisListType

P = 128
T = 512
NT = T // P
D = 1024
KD = D // P
DEPTH = 2
UC = 256
UNIT = KD * UC
SLOTS = 2
BIG = 1.0e30
EPS = 1e-6
LN_EPS = 1e-5

RH = 4
SH, SP, SG, SN = 16, 64, 2, 128
HG = SH // SG
CONV_K = 4
FH, FD = 8, 64
MIX1 = 2048
FF = 2816
KF = FF // P
NH, NG, HD = 8, 2, 64
CB, CS = 32, 16
NCMP = T // CS - 1
GH, GK, GV, GC = 4, 32, 64, 64
NGC = T // GC
ALPHA = (2.0 * DEPTH) ** 0.25

P1 = dict(norm_g=(0, 8), b_ada=(8, 32), conv_w=(32, 80), conv_b=(80, 92), ssd_g=(92, 100),
          dtf_b=(100, 124), a_log=(124, 140), d_skip=(140, 156))
P1N = 156
P2 = dict(ln_g=(0, 24), ln_b=(24, 48), pool_s=(48, 50), gla_ba=(50, 51), gla_g=(51, 53))
P2N = 53
C0 = dict(ident=(0, 128), ones=(128, 256), triu=(256, 384), causal=(384, 896), freq=(896, 897),
          sign=(897, 898), zero=(898, 899))
C0N = 899
C1 = dict(decayT=(0, 512), decq=(512, 1024), deck=(1024, 1028))
C1N = 1028
C2 = dict(reset=(0, 512), invcnt=(512, 1536), cmpadd=(1536, 1664), cmpmul=(1664, 1792),
          gmask=(1792, 2048))
C2N = 2048
CN = 2052


def split3(ap, a):
    return ap.rearrange("p (a b) -> p a b", a=a)


def spread(ap, n):
    return ap.unsqueeze(2).broadcast_to([ap.shape[0], ap.shape[1], n])


def repeat(ap, n):
    return ap.unsqueeze(1).broadcast_to([ap.shape[0], n, ap.shape[1]])


class Stream:

    def __init__(self, loaded, high, low):
        self.loaded, self.high, self.low = loaded, high, low
        self.units, self.freed = [], []
        self.sent = self.rounded = self.lowered = 0

    def add(self, source, n, sem, value):
        self.units.append((source, n))
        self.freed.append((sem, value))
        return len(self.units) - 1

    def send(self, sp, raw, upto):
        while self.sent < min(upto, len(self.units)):
            u = self.sent
            source, n = self.units[u]
            if u >= SLOTS:
                sp.wait_ge(self.low, u - SLOTS + 1)
            sp.dma_start(raw[:, u % SLOTS, 0:n], source).then_inc(self.loaded[u % SLOTS], 16)
            self.sent += 1

    def round(self, eng, op, raw, parts, upto):
        while self.rounded < min(upto, len(self.units)):
            u = self.rounded
            n = self.units[u][1]
            eng.wait_ge(self.loaded[u % SLOTS], 16 * (u // SLOTS + 1))
            if u >= SLOTS:
                eng.wait_ge(*self.freed[u - SLOTS])
            op(parts[:, u % SLOTS, 0, 0:n], raw[:, u % SLOTS, 0:n]).then_inc(self.high, 1)
            self.rounded += 1

    def lower(self, pool, raw, parts, upto):
        while self.lowered < min(upto, len(self.units)):
            u = self.lowered
            n = self.units[u][1]
            pool.wait_ge(self.high, u + 1)
            pool.tensor_tensor(parts[:, u % SLOTS, 1, 0:n], raw[:, u % SLOTS, 0:n],
                               parts[:, u % SLOTS, 0, 0:n].bitcast(F32), ALU.subtract).then_inc(self.low, 1)
            self.lowered += 1


def build(nc, dr, out):
    ctx = ExitStack()
    with ctx:
        def sb(name, n, dt=F32, stack=None):
            return (stack or ctx).enter_context(nc.sbuf_tensor(name, [P, n], dt))

        scope = []
        holder = [ctx]

        def sem(name):
            s = holder[0].enter_context(nc.semaphore(name))
            scope.append(s)
            return s

        def layers(body):
            scope.clear()
            with ExitStack() as own:
                holder[0] = own
                with nc.Fori(0, DEPTH) as l:
                    body(l)
                    clear_semaphores(list(scope))
            holder[0] = ctx
            scope.clear()

        PS = ctx.enter_context(nc.psum_tensor("PS", [P, 8, 512], F32))
        x_all = sb("x_all", KD * T)
        xs_all = sb("x_parts", 2 * KD * T, F32R)
        w_raw = sb("w_raw", SLOTS * UNIT)
        w_parts = sb("w_parts", 2 * SLOTS * UNIT, F32R)
        cst = sb("cst", C0N)
        spec = sb("spec", CN)
        par = sb("par", P1N)
        X = split3(x_all[:, :], KD)
        XS = xs_all[:, :].rearrange("p (a k t) -> p a k t", a=2, k=KD)
        RAW = split3(w_raw[:, :], SLOTS)
        WP = w_parts[:, :].rearrange("p (s a n) -> p s a n", s=SLOTS, a=2)
        ident = cst[:, 0:128]
        ones = cst[:, 128:256]
        triu = cst[:, 256:384]

        def const(name, table=C0, tile=None):
            a, b = table[name]
            return (cst if tile is None else tile)[:, a:b]

        def p1(name):
            return par[:, P1[name][0]:P1[name][1]]

        def p2(name):
            return par[:, P2[name][0]:P2[name][1]]

        phase = [ExitStack()]

        class Arena:

            def __init__(self, name, n):
                phase[0].close()
                phase[0] = ExitStack()
                self.n, self.at = n, 0
                self.t = sb(f"{name}_buffers", n, stack=phase[0])

            def take(self, n):
                assert self.at + n <= self.n, self.at + n
                self.at += n
                return self.t[:, self.at - n:self.at]

            def parts(self, name, n):
                return sb(name, n, F32R, stack=phase[0])

        def clear_semaphores(sems):
            with nc.Block() as block:
                @block.sync
                def _(sp):
                    for s in sems:
                        sp.sem_clear(s)

        def begin_phase():
            scope.clear()
            holder[0] = ExitStack()

        def end_phase():
            clear_semaphores(list(scope))
            holder[0].close()
            holder[0] = ctx
            scope.clear()

        def chain(eng, s):
            n = [0]

            def link(ins):
                n[0] += 1
                ins.then_inc(s, 1)
                eng.wait_ge(s, n[0])
            return link

        begin_phase()
        s_in, s_x = sem("inputs_loaded"), sem("x_loaded")
        s_vc = sem("setup_vector_step")
        s_red = sem("angles_reduced")
        s_sin = sem("sines_ready")
        COS, SIN = spec[:, C1N:C1N + T], spec[:, C1N + T:C1N + 2 * T]
        first = ExitStack()
        m_all = sb("m_all", 16 * T, stack=first)
        mod = sb("mod", 40, stack=first)
        silu_c = mod[:, 32:40]
        F8 = sb("F8", T, stack=first)
        small = sb("small", 516, stack=first)
        M = split3(m_all[:, :], 16)
        raw_mod = small[:, 500:516]
        NADA, NEARLY = 12, 8
        ada = split3(m_all[:, :], 4)

        def modulation(pe, u, w):
            for j in range(2):
                c = 2 * u + j
                for k in range(KD):
                    last = pe.matmul(PS[:, 7, c:c + 1], w[:, k, j * P:(j + 1) * P],
                                     silu_c[:, k:k + 1], start=(k == 0), stop=(k == KD - 1))
            return last

        class ShiftAndScale:

            def __init__(self, name, source):
                self.source = source
                self.loaded = [sem(f"{name}_loaded_{i}") for i in range(4)]
                self.used, self.taken = sem(f"{name}_used"), sem(f"{name}_taken")

            def load(self, eng, units):
                for u in units:
                    if u >= 4:
                        eng.wait_ge(self.used, u - 3)
                    eng.dma_start(ada[:, u % 4, :], self.source(u)).then_inc(self.loaded[u % 4], 16)

            def tensor(self, pe, u):
                pe.wait_ge(self.loaded[u % 4], 16 * (u // 4 + 1))
                modulation(pe, u, split3(ada[:, u % 4, :], KD)).then_inc(self.used, 1)

            def vector(self, dve):
                dve.wait_ge(self.used, NEARLY)
                dve.tensor_copy(raw_mod, PS[:, 7, 0:16]).then_inc(self.taken, 1)

        ss = ShiftAndScale("first_ada", lambda u: dr["w_ada"][u])
        ar = Arena("setup", 6 * T)
        with nc.Block() as block:
            posi = ar.take(T).bitcast(I32)
            ang, k, r, r2, g = (ar.take(T) for _ in range(5))

            @block.sync
            def _(sp):
                sp.dma_start(cst[:, :], dr["c0"]).then_inc(s_in, 16)
                sp.dma_start(posi, dr["pos"]).then_inc(s_in, 16)
                sp.dma_start(silu_c, dr["c"]).then_inc(s_in, 16)
                sp.dma_start(spec[:, 0:C1N], dr["c1"]).then_inc(s_in, 16)
                ss.load(sp, range(0, NEARLY, 2))
                sp.dma_start(x_all[:, :], dr["x"]).then_inc(s_x, 16)
                sp.wait_ge(s_x, 16)

            @block.tensor
            def _(pe):
                pe.wait_ge(s_sin, 1)
                for u in range(NEARLY):
                    ss.tensor(pe, u)

            @block.vector
            def _(dve):
                link = chain(dve, s_vc)
                dve.wait_ge(s_in, 64)
                link(dve.tensor_copy(ang, posi))
                link(dve.tensor_scalar(ang, ang, const("freq"), None, ALU.mult))
                link(dve.tensor_scalar(k, ang, float(1 / (2 * np.pi)), 12582912.0, ALU.mult, ALU.add))
                link(dve.tensor_scalar(k, k, 12582912.0, None, ALU.subtract))
                c1 = 6.28125
                c2 = float(np.round((2 * np.pi - c1) * 2 ** 20) / 2 ** 20)
                c3 = float(2 * np.pi - c1 - c2)
                link(dve.scalar_tensor_tensor(r, k, -c1, ang, ALU.mult, ALU.add))
                link(dve.scalar_tensor_tensor(r, k, -c2, r, ALU.mult, ALU.add))
                link(dve.scalar_tensor_tensor(r, k, -c3, r, ALU.mult, ALU.add))
                link(dve.tensor_scalar(g, r, float(np.pi / 2), float(-2 * np.pi), ALU.is_gt, ALU.mult))
                link(dve.scalar_tensor_tensor(r2, r, float(np.pi / 2), g, ALU.add, ALU.add))
                pi = float(np.nextafter(np.float32(np.pi), np.float32(0)))
                link(dve.tensor_scalar(r, r, pi, -pi, ALU.min, ALU.max))
                dve.tensor_scalar(r2, r2, pi, -pi, ALU.min, ALU.max).then_inc(s_red, 1)
                dve.wait_ge(s_sin, 3)
                link(dve.tensor_scalar(SIN, SIN, const("sign"), None, ALU.mult))
                ss.vector(dve)

            @block.scalar
            def _(act):
                ss.load(act, (1, 3))
                act.wait_ge(s_in, 64)
                act.activation(silu_c, silu_c, ACT.Silu).then_inc(s_sin, 1)
                act.wait_ge(s_red, 1)
                act.activation(SIN, r, ACT.Sin).then_inc(s_sin, 1)
                act.activation(COS, r2, ACT.Sin).then_inc(s_sin, 1)
                ss.load(act, (5, 7))


        end_phase()

        def of_layer(name, l, *ix):
            t = dr[name][bass.ds(l, 1)]
            for i in ix:
                t = t[:, i]
            return t.rearrange("a p n -> (a p) n")

        def column_sum(pe, bank, tiles, ready, base=0):
            for n, t in enumerate(tiles):
                pe.wait_ge(ready, base + n + 1)
                last = pe.matmul(PS[:, bank, :], ones, t, start=(n == 0), stop=(n == len(tiles) - 1))
            return last

        class Project:

            def __init__(self, stream, projected, evacuated):
                self.stream, self.projected, self.evacuated = stream, projected, evacuated
                self.jobs = []

            def feature_major(self, source, ncols, tiles, ktiles=KD):
                u = self.stream.add(source, ktiles * ncols, self.projected, len(self.jobs) + len(tiles))
                first = len(self.jobs)
                for c, m in tiles:
                    self.jobs.append((u, "f", c, m, ncols, ktiles))
                return first

            def token_major(self, source, ncols):
                u = self.stream.add(source, KD * ncols, self.projected, len(self.jobs) + NT)
                first = len(self.jobs)
                for t in range(NT):
                    self.jobs.append((u, "t", t, ncols, ncols, KD))
                return first

            def run(self, pe, j, part, ready=None):
                u, kind, c, m, ncols, kt = self.jobs[j]
                pe.wait_ge(self.stream.low, u + 1)
                if j >= 2:
                    pe.wait_ge(self.evacuated, j - 1)
                w = [WP[:, u % SLOTS, a, 0:kt * ncols].rearrange("p (k n) -> p k n", k=kt) for a in range(2)]
                for k in range(kt):
                    if ready is not None:
                        pe.wait_ge(ready, k + 1)
                    for n, (a, b) in enumerate(((0, 0), (0, 1), (1, 0))):
                        start, stop = k == 0 and n == 0, k == kt - 1 and n == 2
                        if kind == "f":
                            last = pe.matmul(PS[0:m, j % 2, :], w[a][:, k, c:c + m], part(b, k),
                                             start=start, stop=stop)
                        else:
                            last = pe.matmul(PS[:, j % 2, 0:m], part(a, k)[:, c * P:(c + 1) * P], w[b][:, k, :],
                                             start=start, stop=stop)
                last.then_inc(self.projected, 1)

            def after(self, j, act):
                u = self.jobs[j][0] if j >= 0 else -1
                if j + 1 == len(self.jobs) or self.jobs[j + 1][0] != u:
                    self.stream.round(act, act.copy, RAW, WP, u + 1 + SLOTS)

        tokens = lambda a, k: XS[:, a, k, :]

        class Attention:

            def __init__(self, name, heads, q, kf, vf, rows, buf):
                self.heads, self.q, self.kf, self.vf, self.rows = heads, q, kf, vf, rows
                self.steps = NT * heads
                (self.scored, self.smax, self.prob, self.turned, self.copied, self.weighted,
                 self.taken) = (sem(f"{name}_{x}") for x in (
                     "scored", "max_taken", "probabilities", "turned", "turned_copied", "weighted",
                     "output_taken"))
                self.sm, self.p, self.pt, self.nm, self.rs = buf

            def score(self, pe, s):
                i, h = divmod(s, self.heads)
                n = (i + 1) * P
                if s >= 2:
                    pe.wait_ge(self.smax, s - 1)
                pe.matmul(PS[:, 4 + s % 2, 0:n], self.q[0:self.rows, h, i * P:(i + 1) * P],
                          self.kf(h)[0:self.rows, 0:n], start=True, stop=True).then_inc(self.scored, 1)

            def turn(self, pe, s):
                i = s // self.heads
                pe.wait_ge(self.prob, s + 1)
                if s >= 2:
                    pe.wait_ge(self.copied, s - 1)
                for t in range(i + 1):
                    last = pe.transpose(PS[:, 6 + s % 2, t * P:(t + 1) * P],
                                        self.p[:, s % 2, t * P:(t + 1) * P], ident)
                last.then_inc(self.turned, 1)

            def weigh(self, pe, s):
                i, h = divmod(s, self.heads)
                pe.wait_ge(self.copied, s + 1)
                if h == 0 and i >= 2:
                    pe.wait_ge(self.taken, i - 1)
                for t in range(i + 1):
                    last = pe.matmul(PS[:, i % 2, h * FD:(h + 1) * FD], self.pt[:, s % 2, t * P:(t + 1) * P],
                                     self.vf(h, t), start=(t == 0), stop=(t == i))
                last.then_inc(self.weighted, 1)

            def tensor(self, pe):
                self.score(pe, 0)
                self.score(pe, 1)
                for s in range(self.steps):
                    self.turn(pe, s)
                    if s + 2 < self.steps:
                        self.score(pe, s + 2)
                    if s >= 1:
                        self.weigh(pe, s - 1)
                self.weigh(pe, self.steps - 1)

            def scalar(self, act):
                for s in range(self.steps):
                    n = (s // self.heads + 1) * P
                    act.wait_ge(self.smax, s + 1)
                    if s >= 2:
                        act.wait_ge(self.turned, s - 1)
                    act.activation(self.p[:, s % 2, 0:n], self.sm[:, s % 2, 0:n], ACT.Exp,
                                   bias=self.nm[:, s:s + 1], scale=-1.0,
                                   accum_out=self.rs[:, s:s + 1]).then_inc(self.prob, 1)

            def vector(self, dve, finish):
                def maximum(s):
                    n = (s // self.heads + 1) * P
                    dve.wait_ge(self.scored, s + 1)
                    if s >= 2:
                        dve.wait_ge(self.prob, s - 1)
                    dve.tensor_tensor_reduce(self.sm[:, s % 2, 0:n], PS[:, 4 + s % 2, 0:n],
                                             const("causal")[:, T - n:T], -(FD ** -0.5), 3.0e38,
                                             ALU.add, ALU.min, self.nm[:, s:s + 1]).then_inc(self.smax, 1)

                def copy(s):
                    n = (s // self.heads + 1) * P
                    dve.wait_ge(self.turned, s + 1)
                    if s >= 2:
                        dve.wait_ge(self.weighted, s - 1)
                    dve.tensor_copy(self.pt[:, s % 2, 0:n], PS[:, 6 + s % 2, 0:n]).then_inc(self.copied, 1)

                maximum(0)
                for s in range(self.steps):
                    if s + 1 < self.steps:
                        maximum(s + 1)
                    copy(s)
                    if s % self.heads == 1 and s > self.heads:
                        finish(s // self.heads - 1)
                finish(NT - 1)

        def first_layer(l):
            stream = Stream([sem(f"weights_loaded_{i}") for i in range(SLOTS)], sem("weights_rounded"),
                            sem("weights_lowered"))
            projected, evacuated = sem("projected"), sem("evacuated")
            proj = Project(stream, projected, evacuated)

            drl = lambda name, *ix: of_layer(name, l, *ix)

            ada_of = lambda u: dr["w_ada"][bass.ds(l * 12 + u, 1)].rearrange("a p n -> (a p) n")
            two = [(0, P), (P, P)]
            wu = lambda i: drl("w_in", i)
            J = {}
            J["rq"] = [proj.feature_major(wu(i), UC, two) for i in (0, 1)][0]
            J["rk"] = [proj.feature_major(wu(i), UC, two) for i in (2, 3)][0]
            J["rg"] = [proj.feature_major(wu(i), UC, two) for i in (4, 5)][0]
            J["rv"] = [proj.token_major(wu(i), UC) for i in (6, 7)][0]
            end_r = len(stream.units)
            J["dtf"] = proj.feature_major(drl("w_dtf"), P, [(0, P)])
            J["bc"] = [proj.feature_major(wu(i), UC, two) for i in (8, 9)][0]
            J["xs"] = [proj.feature_major(wu(i), UC, two) for i in range(10, 14)][0]
            J["z"] = [proj.token_major(wu(i), UC) for i in range(14, 18)][0]
            end_s = len(stream.units)
            J["fq"] = [proj.feature_major(wu(i), UC, two) for i in (18, 19)][0]
            J["fk"] = [proj.feature_major(wu(i), UC, two) for i in (20, 21)][0]
            J["fv"] = [proj.token_major(wu(i), UC) for i in (22, 23)][0]
            J["fg"] = [proj.token_major(wu(i), UC) for i in (24, 25)][0]
            end_f = len(stream.units)
            J["out"] = [proj.feature_major(drl("w_out", i), P, [(0, P)], ktiles=16) for i in range(8)][0]

            s_par = sem("parameters_loaded")
            s_gl = [sem(f"gate_loaded_{i}") for i in range(2)]
            s_gu = sem("gate_unit_used")
            s_sq = sem("x_squared")
            s_ss = sem("x_square_sum")
            s_rms = sem("x_rms")
            s_hs = sem("h_scaled")
            s_dv = sem("mod_vector_step")
            s_h = sem("h_ready")
            s_hh = sem("h_rounded")
            s_hl = sem("h_split")
            msb, amul = mod[:, 0:24], mod[:, 24:32]

            rstd = F8
            ar = Arena("modulate", KD * T + T)
            with nc.Block() as block:
                sq = split3(ar.take(KD * T), KD)
                rms = ar.take(T)

                @block.sync
                def _(sp):
                    sp.dma_start(par[:, 0:P1N], drl("par1")).then_inc(s_par, 16)
                    stream.send(sp, RAW, SLOTS)

                @block.gpsimd
                def _(pool):
                    stream.lower(pool, RAW, WP, SLOTS)

                @block.tensor
                def _(pe):
                    column_sum(pe, 0, [sq[:, k, :] for k in range(KD)], s_sq).then_inc(s_ss, 1)

                @block.scalar
                def _(act):
                    for k in range(KD):
                        act.activation(sq[:, k, :], X[:, k, :], ACT.Square).then_inc(s_sq, 1)
                    act.wait_ge(s_ss, 1)
                    act.activation(rms, PS[:, 0, :], ACT.Sqrt, bias=EPS, scale=1.0 / D).then_inc(s_rms, 1)
                    stream.round(act, act.copy, RAW, WP, SLOTS)

                @block.vector
                def _(dve):
                    link = chain(dve, s_dv)
                    dve.wait_ge(s_par, 16)
                    link(dve.tensor_tensor(msb[:, 0:16], raw_mod, p1("b_ada")[:, 0:16], ALU.add))
                    link(dve.scalar_tensor_tensor(amul, msb[:, 8:16], 1.0, p1("norm_g"), ALU.add, ALU.mult))
                    dve.wait_ge(s_rms, 1)
                    link(dve.reciprocal(rstd[:, :], rms))

            s_rot = sem("rotated")
            s_gt = sem("gate_taken")
            s_qd = sem("q_decayed")
            s_kt = sem("k_turned")
            s_kd = sem("k_decayed")
            s_rs = sem("ret_scored")
            s_rd = sem("ret_scores_decayed")
            s_ds = sem("ret_state_products")
            s_st = sem("ret_state_ready")
            s_ro = sem("ret_output")
            s_rq = sem("ret_squared")
            s_rn = sem("ret_square_sum")
            s_rr = sem("ret_rms")
            s_rv = sem("ret_vector_step")
            decay_chunk = [float((1.0 - 2.0 ** (-5.0 - h)) ** P) for h in range(RH)]
            decayT = spec[:, 0:512]
            decq = spec[:, 512:1024]
            deck = spec[:, 1024:1028]
            ar = Arena("retention", 15400)
            with nc.Block() as block:
                q4, k4, qd4 = (split3(ar.take(4 * T), 4) for _ in range(3))
                v4 = split3(ar.take(4 * T), 4)
                kd4 = ar.take(4 * 384).rearrange("p (h c d) -> p h c d", h=4, c=3)
                sT = split3(ar.take(4 * T), 4)
                S = split3(ar.take(3 * T), 3)
                rr_ = ar.take(4 * T)
                raw, swp = split3(rr_[:, 0:2 * T], 2), split3(rr_[:, 2 * T:4 * T], 2)
                rr = M[:, 12:16, :]
                sq = q4
                gate = split3(m_all[:, 4 * T:12 * T], 2)
                H = lambda k: M[:, (12 + k) % 16, :]
                jq, jg, jv = J["rq"], J["rg"], J["rv"]
                nj = J["dtf"]

                @block.sync
                def _(sp):
                    for n in range(2):
                        sp.dma_start(gate[:, n, 0:UNIT], ada_of(NEARLY + n)).then_inc(s_gl[n], 16)
                    stream.send(sp, RAW, 4)
                    for n in range(2, NADA - NEARLY):
                        sp.wait_ge(s_gu, n - 1)
                        sp.dma_start(gate[:, n % 2, 0:UNIT], ada_of(NEARLY + n)).then_inc(s_gl[n % 2], 16)
                        stream.send(sp, RAW, 4 + n - 1)
                    stream.send(sp, RAW, end_r + 2 * SLOTS)

                @block.gpsimd
                def _(pool):
                    stream.lower(pool, RAW, WP, end_r + SLOTS)

                @block.tensor
                def _(pe):
                    for j in range(nj):
                        proj.run(pe, j, tokens, s_hl if j == 0 else None)
                        if j in (5, 7, 11, 15):
                            n = (5, 7, 11, 15).index(j)
                            pe.wait_ge(s_gl[n % 2], 16 * (n // 2 + 1))
                            modulation(pe, NEARLY + n, split3(gate[:, n % 2, 0:UNIT], KD)).then_inc(s_gu, 1)
                    pe.wait_ge(s_gt, 1)
                    for h in range(RH):
                        pe.wait_ge(s_rot, 4 + h + 1)
                        if h >= 2:
                            pe.wait_ge(s_kd, h - 1)
                        for c in range(3):
                            last = pe.transpose(PS[:, 4 + h % 2, c * P:(c + 1) * P],
                                                k4[:, h, c * P:(c + 1) * P], ident)
                        last.then_inc(s_kt, 1)
                    for c in range(NT):
                        if c >= 2:
                            pe.wait_ge(s_rd, c - 1)
                        for h in range(RH):
                            last = pe.matmul(PS[:, 6 + c % 2, h * P:(h + 1) * P], k4[:, h, c * P:(c + 1) * P],
                                             q4[:, h, c * P:(c + 1) * P], start=True, stop=True)
                        last.then_inc(s_rs, 1)
                    pe.wait_ge(evacuated, nj)
                    for c in range(NT - 1):
                        if c == 0:
                            pe.wait_ge(s_kd, RH)
                        if c >= 2:
                            pe.wait_ge(s_st, c - 1)
                        for h in range(RH):
                            last = pe.matmul(PS[:, 4 + c % 2, h * P:(h + 1) * P], kd4[:, h, c, :],
                                             v4[:, c, h * P:(h + 1) * P], start=True, stop=True)
                        last.then_inc(s_ds, 1)
                    pe.wait_ge(s_qd, RH)
                    for c in range(NT):
                        pe.wait_ge(s_rd, c + 1)
                        if c:
                            pe.wait_ge(s_st, c)
                        for h in range(RH):
                            o = PS[:, c, h * P:(h + 1) * P]
                            last = pe.matmul(o, v4[:, c, h * P:(h + 1) * P], sT[:, c, h * P:(h + 1) * P],
                                             start=True, stop=(c == 0))
                            if c:
                                last = pe.matmul(o, S[:, c - 1, h * P:(h + 1) * P],
                                                 qd4[:, h, c * P:(c + 1) * P], start=False, stop=True)
                        last.then_inc(s_ro, 1)
                    pe.wait_ge(s_rq, NT)
                    for h in range(RH):
                        if h == 0:
                            pe.wait_ge(s_st, 3)
                        pe.matmul(PS[:, 4 + h, :], ones, sq[:, h, :], start=True, stop=True).then_inc(s_rn, 1)

                @block.scalar
                def _(act):
                    for k in range(KD):
                        act.wait_ge(s_hs, k + 1)
                        act.activation(H(k), H(k), ACT.Identity,
                                       bias=msb[:, k:k + 1]).then_inc(s_h, 1)
                        act.wait_ge(s_h, k + 1)
                        act.copy(XS[:, 0, k, :], H(k)).then_inc(s_hh, 1)
                    act.wait_ge(s_hl, KD)
                    for j in range(nj):
                        if j:
                            proj.after(j - 1, act)
                        act.wait_ge(projected, j + 1)
                        b = PS[:, j % 2, :]
                        if j < jg:
                            if j >= 2:
                                act.wait_ge(s_rot, j - 1)
                            act.copy(raw[:, j % 2, :], b)
                            act.copy(swp[0:64, j % 2, :], b[64:128, :])
                            act.copy(swp[64:128, j % 2, :], b[0:64, :]).then_inc(evacuated, 1)
                        elif j < jv:
                            act.activation(M[:, j - jg, :], b, ACT.Silu).then_inc(evacuated, 1)
                        else:
                            u, t = divmod(j - jv, NT)
                            act.copy(v4[:, t, u * UC:(u + 1) * UC], b[:, 0:UC]).then_inc(evacuated, 1)
                    proj.after(nj - 1, act)
                    for c in range(NT):
                        act.wait_ge(s_ro, c + 1)
                        act.activation(sq[:, :, c * P:(c + 1) * P], split3(PS[:, c, :], 4),
                                       ACT.Square).then_inc(s_rq, 1)
                    for h in range(RH):
                        act.wait_ge(s_rn, h + 1)
                        act.activation(rr[:, h, :], PS[:, 4 + h, :], ACT.Sqrt, bias=EPS,
                                       scale=1.0 / P).then_inc(s_rr, 1)

                @block.vector
                def _(dve):
                    link = chain(dve, s_rv)
                    for k in range(KD + 1):
                        if k < KD:
                            dve.scalar_tensor_tensor(H(k), X[:, k, :], amul[:, k:k + 1], rstd[:, :],
                                                     ALU.mult, ALU.mult).then_inc(s_hs, 1)
                        if k:
                            dve.wait_ge(s_hh, k)
                            dve.tensor_tensor(XS[:, 1, k - 1, :], H(k - 1), XS[:, 0, k - 1, :].bitcast(F32),
                                              ALU.subtract).then_inc(s_hl, 1)
                    for j in range(8):
                        dve.wait_ge(evacuated, j + 1)
                        link(dve.tensor_tensor(raw[:, j % 2, :], raw[:, j % 2, :], COS, ALU.mult))
                        link(dve.tensor_tensor(swp[:, j % 2, :], swp[:, j % 2, :], SIN, ALU.mult))
                        dst = (q4 if j < 4 else k4)[:, j % 4, :]
                        dve.tensor_tensor(dst, raw[:, j % 2, :], swp[:, j % 2, :], ALU.add).then_inc(s_rot, 1)
                        if j < 4:
                            dve.wait_ge(s_rot, j + 1)
                            dve.tensor_tensor(split3(qd4[:, j, :], 4), split3(q4[:, j, :], 4),
                                              repeat(decq[:, j * P:(j + 1) * P], 4), ALU.mult).then_inc(s_qd, 1)
                    dve.wait_ge(s_gu, NADA - NEARLY)
                    dve.tensor_tensor(msb[:, 16:24], PS[:, 7, 16:24], p1("b_ada")[:, 16:24], ALU.add).then_inc(s_gt, 1)
                    for h in range(RH):
                        dve.wait_ge(s_kt, h + 1)
                        dve.tensor_scalar(kd4[:, h, :, :], split3(PS[:, 4 + h % 2, 0:384], 3), deck[:, h:h + 1],
                                          None, ALU.mult).then_inc(s_kd, 1)
                    for c in range(NT):
                        dve.wait_ge(s_rs, c + 1)
                        dve.tensor_tensor(sT[:, c, :], PS[:, 6 + c % 2, :], decayT, ALU.mult).then_inc(s_rd, 1)
                    for c in range(NT - 1):
                        dve.wait_ge(s_ds, c + 1)
                        if c == 0:
                            dve.tensor_copy(S[:, 0, :], PS[:, 4, :]).then_inc(s_st, 1)
                            continue
                        dve.wait_ge(s_st, c)
                        for h in range(RH):
                            last = dve.scalar_tensor_tensor(
                                S[:, c, h * P:(h + 1) * P], S[:, c - 1, h * P:(h + 1) * P], decay_chunk[h],
                                PS[:, 4 + c % 2, h * P:(h + 1) * P], ALU.mult, ALU.add)
                        last.then_inc(s_st, 1)
                    for c in range(NT):
                        dve.wait_ge(s_rq, c + 1)
                        g = M[:, 0:4, c * P:(c + 1) * P]
                        link(dve.tensor_tensor(g, split3(PS[:, c, :], 4), g, ALU.mult))

            nb = lambda n: sem("ssd_" + n)
            s_sel, s_sv, s_ab, s_ex, s_w1, s_ln = (nb(x) for x in (
                "selectors_loaded", "vector_step", "gate_magnitudes", "gate_exp", "gate_one_plus", "gate_log"))
            s_a, s_lf, s_sm, s_smt, s_ea = (nb(x) for x in (
                "steps_ready", "log_forget_ready", "cumulative_sums", "cumulative_sums_taken", "decays_ready"))
            s_al, s_cv, s_si, s_bt, s_btc = (nb(x) for x in (
                "a_exp", "convolved", "conv_activated", "b_turned", "b_turned_copied"))
            s_cb, s_cbm, s_xt, s_xtc, s_xd = (nb(x) for x in (
                "cb_products", "cb_masked", "x_turned", "x_turned_copied", "x_scaled"))
            s_bc, s_sg, s_le, s_we, s_y, s_yt = (nb(x) for x in (
                "log_decay_spread", "log_decay_ready", "decay_ready", "weights_ready", "y_products", "y_taken"))
            s_sd, s_ss2, s_xdd, s_q2, s_r2, s_yn = (nb(x) for x in (
                "state_products", "state_ready", "x_state_scaled", "y_squared", "y_rms", "y_normed"))
            s_tr, s_ev, s_nf = (nb(x) for x in ("y_turned", "y_turned_copied", "negated_copied"))
            s_pad = nb("conv_padding_zeroed")
            s_dt, s_rn2 = nb("steps_turned"), nb("retention_normed")
            s_yz = nb("y_gated")
            dtf = split3(small[:, 0:96], 4)
            mag = split3(small[:, 96:192], 4)
            ex = split3(small[:, 192:288], 4)
            w1 = split3(small[:, 288:384], 4)
            lg = split3(small[:, 384:480], 4)
            ar = Arena("ssd", 16200)
            with nc.Block() as block:
                late = ar.take(3 * D + 2 * T + SH * P)
                pre = split3(late[:, 0:2 * 515], 2)
                acc = split3(late[:, 1030:1030 + 2 * T], 2)
                xf = split3(late[:, 2054:2054 + 2 * T], 2)
                xdt = split3(late[:, 0:2 * D], 2)
                St = split3(late[:, 2 * D:2 * D + 2 * T], 2)
                yt = split3(late[:, 3 * D:3 * D + 2 * T], 2)
                sel = late[:, 4 * D:4 * D + SH * P]
                bcf = split3(ar.take(4 * T), 4)
                xdd = bcf[:, 0:2, :].rearrange("p a t -> p (a t)")
                xt = split3(ar.take(NT * D), NT)
                zu = [split3(t, NT) for t in (m_all[:, 8 * T:10 * T], m_all[:, 10 * T:12 * T],
                                              ar.take(D), ar.take(D))]
                bt = ar.take(768).rearrange("p (g c n) -> p g c n", g=2, c=3)
                cb = ar.take(1024).rearrange("p (g c i) -> p g c i", g=2, c=4)
                seg = split3(m_all[:, 12 * T:16 * T], 2)
                dtfT = M[0:24, 5, :]
                afm = M[0:SH, 7, :]
                sums = M[:, 4, 0:512]
                acum, tot = split3(sums[:, 0:64], 4), split3(sums[:, 64:128], 4)
                eac, edl, eto = (split3(sums[:, 128 + 64 * i:192 + 64 * i], 4) for i in range(3))
                aa = split3(sums[:, 384:448], 4)
                amat = sums[:, 448:464]
                Ft = F8[0:FH, :]
                ssq, rst = M[:, 6, 0:4], M[:, 6, 4:8]
                jd, jb, jx, jz, je = J["dtf"], J["bc"], J["xs"], J["z"], J["fq"]
                steps = [(c, g) for c in range(NT) for g in range(SG)]

                @block.sync
                def _(sp):
                    sp.dma_start(sel[0:SH, :], dr["sel"]).then_inc(s_sel, 16)
                    stream.send(sp, RAW, end_s + 2 * SLOTS)

                @block.gpsimd
                def _(pool):
                    pool.memset(pre[:, :, 0:3], 0.0).then_inc(s_pad, 1)
                    stream.lower(pool, RAW, WP, end_s + SLOTS)

                @block.tensor
                def _(pe):
                    proj.run(pe, jd, tokens)
                    proj.run(pe, jb, tokens)
                    pe.wait_ge(evacuated, jb)
                    for c in range(NT):
                        last = pe.transpose(PS[:, 7, c * 24:(c + 1) * 24], dtfT[:, c * P:(c + 1) * P],
                                            ident[0:24, 0:24])
                    last.then_inc(s_dt, 1)
                    for j in range(jb + 1, jx):
                        proj.run(pe, j, tokens)
                    pe.wait_ge(s_a, 1)
                    for c in range(NT):
                        pe.matmul(PS[:, 4, c * SH:(c + 1) * SH], triu, aa[:, c, :], start=True, stop=True)
                        pe.matmul(PS[:, 4, 64 + c * SH:64 + (c + 1) * SH], ones, aa[:, c, :], start=True, stop=True)
                    for c in range(NT):
                        last = pe.matmul(PS[0:SH, 5, c * P:(c + 1) * P], aa[:, c, :], triu, start=True, stop=True)
                    last.then_inc(s_sm, 1)
                    pe.wait_ge(s_lf, 1)
                    for c in range(NT):
                        for b in range(c + 1):
                            last = pe.matmul(PS[0:FH, 6, c * P:(c + 1) * P], lg[:, b, 16:24],
                                             triu if b == c else ones, start=(b == 0), stop=(b == c))
                    last.then_inc(s_sm, 1)
                    pe.wait_ge(s_si, 4)
                    pe.wait_ge(s_smt, 3)
                    for g in range(SG):
                        for c in range(NT - 1):
                            last = pe.transpose(PS[:, 4 + g, c * P:(c + 1) * P], bcf[:, g, c * P:(c + 1) * P], ident)
                        last.then_inc(s_bt, 1)
                    for g in range(SG):
                        for c in range(NT):
                            last = pe.matmul(PS[:, 6 + g, c * P:(c + 1) * P], bcf[:, g, c * P:(c + 1) * P],
                                             bcf[:, 2 + g, c * P:(c + 1) * P], start=True, stop=True)
                        last.then_inc(s_cb, 1)

                    def turn_x(n):
                        pe.wait_ge(s_si, 4 + n + 1)
                        if n < 2:
                            pe.wait_ge(s_btc, n + 1)
                        else:
                            pe.wait_ge(s_xtc, n - 1)
                        for c in range(NT):
                            last = pe.transpose(PS[:, 4 + n % 2, c * P:(c + 1) * P],
                                                xf[:, n % 2, c * P:(c + 1) * P], ident)
                        last.then_inc(s_xt, 1)

                    for j in range(jx, jz + 2):
                        proj.run(pe, j, tokens)
                        if j - jx >= 2:
                            turn_x(j - jx - 2)

                    def spread_decay(s):
                        c, g = steps[s]
                        if s == 0:
                            pe.wait_ge(s_sel, 16)
                            pe.wait_ge(s_xtc, 8)
                            pe.wait_ge(s_smt, 3)
                        else:
                            pe.wait_ge(s_sg, s)
                        for h in range(HG):
                            hh = g * HG + h
                            last = pe.matmul(PS[:, 4 + h // 4, (h % 4) * P:(h % 4 + 1) * P],
                                             sel[0:SH, hh * P:(hh + 1) * P], afm[:, c * P:(c + 1) * P],
                                             start=True, stop=True)
                        last.then_inc(s_bc, 1)

                    def outputs(s):
                        c, g = steps[s]
                        pe.wait_ge(s_we, s + 1)
                        if s == 0:
                            pe.wait_ge(s_cbm, 2)
                            pe.wait_ge(s_xd, 1)
                        else:
                            pe.wait_ge(s_yt, s)
                        pe.wait_ge(s_xd, c + 1)
                        for h in range(HG):
                            last = pe.matmul(PS[:, 6, h * SP:(h + 1) * SP], seg[:, s % 2, h * P:(h + 1) * P],
                                             xdt[:, c % 2, (g * HG + h) * SP:(g * HG + h + 1) * SP],
                                             start=True, stop=True)
                        if c:
                            pe.wait_ge(s_ss2, (c - 1) * 2 + g + 1)
                            last = pe.matmul(PS[:, 7, :], bcf[:, 2 + g, c * P:(c + 1) * P], St[:, g, :],
                                             start=True, stop=True)
                        last.then_inc(s_y, 1)
                        if c < NT - 1:
                            n = 2 * c + g
                            if n == 0:
                                pe.wait_ge(s_btc, 2)
                            if c:
                                pe.wait_ge(s_ss2, n - 1)
                            pe.wait_ge(s_xdd, c + 1)
                            pe.matmul(PS[:, 2 + g, :], bt[:, g, c, :], xdd[:, g * T:(g + 1) * T],
                                      start=True, stop=True).then_inc(s_sd, 1)

                    spread_decay(0)
                    for s in range(8):
                        if s + 1 < 8:
                            spread_decay(s + 1)
                        for j in range(jz + 2 + 2 * s, min(jz + 4 + 2 * s, je)):
                            proj.run(pe, j, tokens)
                        outputs(s)
                    for f in range(8):
                        b = 2 + f % 2
                        if f == 0:
                            pe.wait_ge(s_yn, NT)
                        if f >= 2:
                            pe.wait_ge(s_ev, f - 1)
                        for c in range(NT):
                            last = pe.transpose(PS[:, b, c * P:(c + 1) * P], xt[:, c, f * P:(f + 1) * P], ident)
                        last.then_inc(s_tr, 1)

                @block.scalar
                def _(act):
                    def evacuate(j):
                        proj.after(j - 1, act)
                        act.wait_ge(projected, j + 1)
                        b = PS[:, j % 2, :]
                        if j < jb:
                            act.copy(dtfT, b[0:24, :]).then_inc(evacuated, 1)
                        elif j < jz:
                            n = j - jb
                            if n == 0:
                                act.wait_ge(s_pad, 1)
                            if n >= 2:
                                act.wait_ge(s_cv, n - 1)
                            act.copy(pre[:, n % 2, 3:515], b).then_inc(evacuated, 1)
                        else:
                            u, t = divmod(j - jz, NT)
                            act.activation(zu[u][:, t, :], b[:, 0:UC], ACT.Silu).then_inc(evacuated, 1)

                    def activate(n):
                        act.wait_ge(s_cv, n + 1)
                        if n >= 6:
                            act.wait_ge(s_xt, n - 5)
                        dst = bcf[:, n, :] if n < 4 else xf[:, n % 2, :]
                        act.activation(dst, acc[:, n % 2, :], ACT.Silu).then_inc(s_si, 1)

                    def copy_x(n):
                        act.wait_ge(s_xt, n + 1)
                        act.copy(xt[:, :, n * P:(n + 1) * P], split3(PS[:, 4 + n % 2, :], 4)).then_inc(s_xtc, 1)

                    evacuate(jd)
                    act.activation(amat, p1("a_log"), ACT.Exp).then_inc(s_al, 1)
                    act.wait_ge(s_ab, 1)
                    act.activation(ex, mag, ACT.Exp, scale=-1.0).then_inc(s_ex, 1)
                    act.wait_ge(s_w1, 1)
                    act.activation(lg, w1, ACT.Ln).then_inc(s_ln, 1)
                    for j in range(jb, jx):
                        evacuate(j)
                        if j > jb:
                            activate(j - jb - 1)
                    activate(3)
                    act.wait_ge(s_sm, 1)
                    act.copy(afm, PS[0:SH, 5, :]).then_inc(s_smt, 1)
                    act.wait_ge(s_sm, 2)
                    act.copy(Ft, PS[0:FH, 6, :]).then_inc(s_smt, 1)
                    act.wait_ge(s_smt, 3)
                    act.wait_ge(s_nf, 1)
                    act.activation(eac, acum, ACT.Exp)
                    act.activation(eto, tot, ACT.Exp)
                    act.activation(edl, edl, ACT.Exp).then_inc(s_ea, 1)
                    for g in range(SG):
                        act.wait_ge(s_bt, g + 1)
                        act.copy(bt[:, g, :, :], split3(PS[:, 4 + g, 0:384], 3)).then_inc(s_btc, 1)
                    for j in range(jx, jz + 2):
                        evacuate(j)
                        if 1 <= j - jx < 9:
                            activate(4 + j - jx - 1)
                        if j - jx >= 3:
                            copy_x(j - jx - 3)
                    copy_x(7)

                    def decays(s):
                        c, g = steps[s]
                        act.wait_ge(s_bc, s + 1)
                        if s >= 2:
                            act.wait_ge(s_y, s - 1)
                        for h in range(HG):
                            last = act.activation(seg[:, s % 2, h * P:(h + 1) * P],
                                                  PS[:, 4 + h // 4, (h % 4) * P:(h % 4 + 1) * P], ACT.Relu,
                                                  bias=acum[:, c, g * HG + h:g * HG + h + 1], scale=-1.0)
                        last.then_inc(s_sg, 1)
                        act.wait_ge(s_sg, s + 1)
                        act.activation(seg[:, s % 2, :], seg[:, s % 2, :], ACT.Exp, scale=-1.0).then_inc(s_le, 1)

                    act.wait_ge(s_rn2, 1)
                    decays(0)
                    for s in range(8):
                        if s + 1 < 8:
                            decays(s + 1)
                        for j in range(jz + 2 + 2 * s, min(jz + 4 + 2 * s, je)):
                            evacuate(j)
                    proj.after(je - 1, act)
                    for c in range(NT):
                        act.wait_ge(s_yz, c + 1)
                        act.activation(late[:, 0:D], xt[:, c, :], ACT.Square,
                                       accum_out=ssq[:, c:c + 1]).then_inc(s_q2, 1)
                        act.wait_ge(s_q2, c + 1)
                    act.activation(rst, ssq, ACT.Sqrt, bias=EPS, scale=1.0 / D).then_inc(s_r2, 1)
                    for f in range(8):
                        act.wait_ge(s_tr, f + 1)
                        act.activation(M[:, 4 + f, :], PS[:, 2 + f % 2, :], ACT.Copy,
                                       scale=p1("ssd_g")[:, f:f + 1]).then_inc(s_ev, 1)

                @block.vector
                def _(dve):
                    link = chain(dve, s_sv)
                    dve.wait_ge(s_dt, 1)
                    link(dve.tensor_tensor(dtf, split3(PS[:, 7, 0:96], NT), repeat(p1("dtf_b"), NT), ALU.add))
                    dve.scalar_tensor_tensor(mag, dtf, -1.0, dtf, ALU.mult, ALU.max).then_inc(s_ab, 1)
                    dve.wait_ge(s_ex, 1)
                    dve.tensor_scalar(w1, ex, 1.0, None, ALU.add).then_inc(s_w1, 1)
                    dve.wait_ge(s_w1, 1)
                    link(dve.scalar_tensor_tensor(mag, w1, 1.0, ex, ALU.subtract, ALU.subtract))
                    dve.wait_ge(s_ln, 1)
                    link(dve.reciprocal(w1, w1))
                    link(dve.tensor_tensor(mag, mag, w1, ALU.mult))
                    link(dve.tensor_tensor(lg, lg, mag, ALU.subtract))
                    link(dve.scalar_tensor_tensor(dtf[:, :, 0:16], dtf[:, :, 0:16], 0.0, lg[:, :, 0:16],
                                                  ALU.max, ALU.add))
                    dve.scalar_tensor_tensor(lg[:, :, 16:24], dtf[:, :, 16:24], 0.0, lg[:, :, 16:24],
                                             ALU.min, ALU.subtract).then_inc(s_lf, 1)
                    dve.wait_ge(s_al, 1)
                    dve.scalar_tensor_tensor(aa, dtf[:, :, 0:16], -1.0, repeat(amat, NT),
                                             ALU.mult, ALU.mult).then_inc(s_a, 1)

                    def convolve(n):
                        dve.wait_ge(evacuated, jb + n + 1)
                        if n >= 2:
                            dve.wait_ge(s_si, n - 1)
                        t = (n + 8) % 12
                        a, p = acc[:, n % 2, :], pre[:, n % 2, :]
                        wk = lambda k: p1("conv_w")[:, k * 12 + t:k * 12 + t + 1]
                        link(dve.tensor_scalar(a, p[:, 0:512], wk(0), p1("conv_b")[:, t:t + 1], ALU.mult, ALU.add))
                        for k in (1, 2):
                            link(dve.scalar_tensor_tensor(a, p[:, k:k + 512], wk(k), a, ALU.mult, ALU.add))
                        dve.scalar_tensor_tensor(a, p[:, 3:515], wk(3), a, ALU.mult, ALU.add).then_inc(s_cv, 1)

                    for n in range(4):
                        convolve(n)
                    dve.wait_ge(s_sm, 1)
                    dve.tensor_copy(sums[:, 0:128], PS[:, 4, 0:128]).then_inc(s_smt, 1)
                    dve.wait_ge(s_smt, 3)
                    dve.tensor_tensor(edl, tot, acum, ALU.subtract).then_inc(s_nf, 1)
                    dve.wait_ge(s_ea, 1)
                    link(dve.tensor_tensor(edl, edl, dtf[:, :, 0:16], ALU.mult))
                    for g in range(SG):
                        dve.wait_ge(s_cb, g + 1)
                        dve.tensor_tensor(cb[:, g, :, :], split3(PS[:, 6 + g, :], 4), repeat(triu, 4),
                                          ALU.mult).then_inc(s_cbm, 1)
                    for n in range(4, 12):
                        convolve(n)
                        if n < 8:
                            h = n - 4
                            link(dve.reciprocal(M[:, 12 + h, :], M[:, 12 + h, :]))
                            link(dve.tensor_tensor(M[:, h, :], M[:, h, :], M[:, 12 + h, :], ALU.mult))
                    dve.sem_inc(s_rn2, 1)
                    dve.wait_ge(s_xtc, 8)

                    def scale_x(c):
                        if c >= 2:
                            dve.wait_ge(s_y, 2 * c - 2)
                        dve.tensor_tensor(split3(xdt[:, c % 2, :], SH), split3(xt[:, c, :], SH),
                                          spread(dtf[:, c, 0:16], SP), ALU.mult).then_inc(s_xd, 1)

                    def weigh(s):
                        c, g = steps[s]
                        dve.wait_ge(s_cbm, 2)
                        dve.wait_ge(s_le, s + 1)
                        v = split3(seg[:, s % 2, :], HG)
                        dve.tensor_tensor(v, v, repeat(cb[:, g, c, :], HG), ALU.mult).then_inc(s_we, 1)

                    def state_input(c):
                        if c >= 1:
                            dve.wait_ge(s_sd, 2 * c)
                        else:
                            dve.wait_ge(s_btc, 2)
                        dve.tensor_tensor(split3(xdd, SH), split3(xt[:, c, :], SH), spread(edl[:, c, :], SP),
                                          ALU.mult).then_inc(s_xdd, 1)

                    def combine(s):
                        c, g = steps[s]
                        hs = slice(g * HG, (g + 1) * HG)
                        y0, y1 = (split3(yt[:, i, :], HG) for i in range(2))
                        xs_ = split3(xt[:, c, g * T:(g + 1) * T], HG)
                        link(dve.tensor_tensor(y0, xs_, spread(p1("d_skip")[:, hs], SP), ALU.mult))
                        dve.wait_ge(s_y, s + 1)
                        if c:
                            link(dve.tensor_tensor(y1, split3(PS[:, 7, :], HG), spread(eac[:, c, hs], SP), ALU.mult))
                            link(dve.tensor_tensor(y0, y0, y1, ALU.add))
                        dve.tensor_tensor(xs_, y0, split3(PS[:, 6, :], HG), ALU.add).then_inc(s_yt, 1)
                        dve.wait_ge(s_yt, s + 1)
                        if c < NT - 1:
                            n = 2 * c + g
                            dve.wait_ge(s_sd, n + 1)
                            if c == 0:
                                dve.tensor_copy(St[:, g, :], PS[:, 2 + g, :]).then_inc(s_ss2, 1)
                            else:
                                sv = split3(St[:, g, :], HG)
                                link(dve.tensor_tensor(sv, sv, spread(eto[:, c, hs], SP), ALU.mult))
                                dve.tensor_tensor(St[:, g, :], St[:, g, :], PS[:, 2 + g, :], ALU.add).then_inc(s_ss2, 1)
                            dve.wait_ge(s_ss2, n + 1)

                    for s in range(8):
                        c, g = steps[s]
                        if g == 0:
                            scale_x(c)
                            if c < NT - 1:
                                state_input(c)
                        weigh(s)
                        combine(s)
                    dve.wait_ge(evacuated, je)
                    for c in range(NT):
                        for u in range(4):
                            yu = xt[:, c, u * UC:(u + 1) * UC]
                            last = dve.tensor_tensor(yu, yu, zu[u][:, c, :], ALU.mult)
                        last.then_inc(s_yz, 1)
                    dve.wait_ge(s_yz, NT)
                    dve.wait_ge(s_r2, 1)
                    link(dve.reciprocal(rst, rst))
                    for c in range(NT):
                        dve.tensor_scalar(xt[:, c, :], xt[:, c, :], rst[:, c:c + 1], None, ALU.mult).then_inc(s_yn, 1)

            s_aug = sem("fox_bias_rows_loaded")
            s_fb = sem("fox_bias_rows_ready")
            s_fv = sem("fox_vector_step")
            s_fx = sem("fox_tile_ready")
            s_ft = sem("fox_output_turned")
            s_fe = sem("fox_output_copied")
            ar = Arena("fox", 15500)
            with nc.Block() as block:
                q, k = split3(ar.take(FH * T), FH), split3(ar.take(FH * T), FH)
                v, fg = split3(ar.take(4 * T), 4), split3(ar.take(4 * T), 4)
                rinv = ar.take(FH)
                buf = (split3(ar.take(2 * T), 2), split3(ar.take(2 * T), 2), split3(ar.take(2 * T), 2),
                       ar.take(32), ar.take(32))
                att = Attention("fox", FH, q, lambda h: k[:, h, :],
                                lambda h, t: v[:, t, h * FD:(h + 1) * FD], 104, buf)
                jq, jk, jv, jg, je = J["fq"], J["fk"], J["fv"], J["fg"], J["out"]

                @block.sync
                def _(sp):
                    sp.dma_start(q[64:104, :, :], dr["aug_q"].rearrange("p (h t) -> p h t", h=FH)).then_inc(s_aug, 16)
                    sp.dma_start(k[64:104, :, :], dr["aug_k"].rearrange("p (h t) -> p h t", h=FH)).then_inc(s_aug, 16)
                    stream.send(sp, RAW, end_f + 2 * SLOTS)

                @block.gpsimd
                def _(pool):
                    stream.lower(pool, RAW, WP, end_f + SLOTS)

                @block.tensor
                def _(pe):
                    for j in range(jq, je):
                        proj.run(pe, j, tokens)
                    pe.wait_ge(evacuated, je)
                    pe.wait_ge(s_fb, 2)
                    att.tensor(pe)
                    for f in range(NT):
                        if f == 0:
                            pe.wait_ge(s_fx, NT)
                        if f >= 2:
                            pe.wait_ge(s_fe, f - 1)
                        for i in range(NT):
                            last = pe.transpose(PS[:, 2 + f % 2, i * P:(i + 1) * P], fg[:, i, f * P:(f + 1) * P], ident)
                        last.then_inc(s_ft, 1)

                @block.scalar
                def _(act):
                    for j in range(jq, je):
                        proj.after(j - 1, act)
                        act.wait_ge(projected, j + 1)
                        b = PS[:, j % 2, :]
                        if j < jv:
                            dst, h = (q, j - jq) if j < jk else (k, j - jk)
                            act.copy(dst[0:64, 2 * h, :], b[0:64, :])
                            act.copy(dst[0:64, 2 * h + 1, :], b[64:128, :]).then_inc(evacuated, 1)
                        elif j < jg:
                            u, t = divmod(j - jv, NT)
                            act.copy(v[:, t, u * UC:(u + 1) * UC], b[:, 0:UC]).then_inc(evacuated, 1)
                        else:
                            u, t = divmod(j - jg, NT)
                            act.activation(fg[:, t, u * UC:(u + 1) * UC], b[:, 0:UC], ACT.Silu).then_inc(evacuated, 1)
                    proj.after(je - 1, act)
                    att.scalar(act)
                    for f in range(NT):
                        act.wait_ge(s_ft, f + 1)
                        act.copy(M[:, 12 + f, :], PS[:, 2 + f % 2, :]).then_inc(s_fe, 1)

                @block.vector
                def _(dve):
                    link = chain(dve, s_fv)
                    dve.wait_ge(s_aug, 32)
                    dve.tensor_scalar(q[96:104, :, :], repeat(F8[0:FH, :], FH), FD ** 0.5, None,
                                      ALU.mult).then_inc(s_fb, 1)
                    dve.tensor_copy(k[64:72, :, :], repeat(F8[0:FH, :], FH)).then_inc(s_fb, 1)

                    def finish(i):
                        dve.wait_ge(att.weighted, FH * (i + 1))
                        dve.wait_ge(att.prob, FH * (i + 1))
                        link(dve.reciprocal(rinv, att.rs[:, FH * i:FH * (i + 1)]))
                        g = split3(fg[:, i, :], FH)
                        link(dve.tensor_tensor(g, g, spread(rinv, FD), ALU.mult))
                        dve.tensor_tensor(g, g, split3(PS[:, i % 2, :], FH), ALU.mult).then_inc(att.taken, 1)
                        dve.wait_ge(att.taken, i + 1)

                    att.vector(dve, finish)
                    dve.sem_inc(s_fx, NT)

            s_mh, s_ml = sem("mixed_rounded"), sem("mixed_split")
            ss = ShiftAndScale("ada", lambda u: ada_of(NADA + u))
            ar = Arena("output", 1)
            xs16 = xs_all[:, :].rearrange("p (k t) -> p k t", k=16)
            low16 = ar.parts("mixed_low", 16 * T).rearrange("p (k t) -> p k t", k=16)
            with nc.Block() as block:
                @block.sync
                def _(sp):
                    sp.wait_ge(s_ml, 16)
                    for m in range(4):
                        ss.load(sp, (2 * m, 2 * m + 1))
                        stream.send(sp, RAW, end_f + 2 * SLOTS + m + 1)

                @block.gpsimd
                def _(pool):
                    stream.lower(pool, RAW, WP, len(stream.units))

                @block.tensor
                def _(pe):
                    for j in range(J["out"], J["out"] + KD):
                        proj.run(pe, j, lambda a, k: (low16 if a else xs16)[:, k, :],
                                 s_ml if j == J["out"] else None)
                        if j > J["out"]:
                            ss.tensor(pe, j - J["out"] - 1)
                    ss.tensor(pe, NEARLY - 1)

                @block.scalar
                def _(act):
                    for k in range(16):
                        act.copy(xs16[:, k, :], M[:, k, :]).then_inc(s_mh, 1)
                    for m in range(KD):
                        proj.after(J["out"] + m, act)

                @block.vector
                def _(dve):
                    for k in range(16):
                        dve.wait_ge(s_mh, k + 1)
                        dve.tensor_tensor(low16[:, k, :], M[:, k, :], xs16[:, k, :].bitcast(F32),
                                          ALU.subtract).then_inc(s_ml, 1)
                    for m in range(KD):
                        j = J["out"] + m
                        dve.wait_ge(projected, j + 1)
                        dve.scalar_tensor_tensor(X[:, m, :], PS[:, j % 2, :], mod[:, 16 + m:17 + m], X[:, m, :],
                                                 ALU.mult, ALU.add).then_inc(evacuated, 1)
                    ss.vector(dve)

        layers(first_layer)
        phase[0].close()
        first.close()
        rstd_all = sb("rstd", T)

        class Ahead:

            def __init__(self, name, source):
                self.source = source
                self.loaded, self.high, self.low = (sem(f"{name}_{x}") for x in ("loaded", "rounded", "split"))

            def sync(self, sp):
                sp.dma_start(RAW[:, 0, :], self.source).then_inc(self.loaded, 16)

            def scalar(self, act):
                act.wait_ge(self.loaded, 16)
                act.copy(WP[:, 0, 0, :], RAW[:, 0, :]).then_inc(self.high, 1)

            def gpsimd(self, pool):
                pool.wait_ge(self.high, 1)
                pool.tensor_tensor(WP[:, 0, 1, :], RAW[:, 0, :], WP[:, 0, 0, :].bitcast(F32),
                                   ALU.subtract).then_inc(self.low, 1)

        begin_phase()
        s_g, s_sq, s_ss, s_rms, s_rc, s_xn, s_xh, s_xl = (sem(f"final_{x}") for x in (
            "gain_loaded", "squared", "square_sum", "rms", "reciprocal", "normed", "rounded", "split"))
        ahead = Ahead("first_ffn_unit", dr["w_gu"][0])
        ar = Arena("between", KD * T + T + KD)
        with nc.Block() as block:
            sq = split3(ar.take(KD * T), KD)
            rms = ar.take(T)
            gain = ar.take(KD)

            @block.sync
            def _(sp):
                sp.dma_start(gain, dr["final_g"]).then_inc(s_g, 16)
                sp.dma_start(spec[:, 0:C2N], dr["c2"]).then_inc(s_g, 16)
                ahead.sync(sp)

            @block.gpsimd
            def _(pool):
                ahead.gpsimd(pool)

            @block.tensor
            def _(pe):
                column_sum(pe, 0, [sq[:, k, :] for k in range(KD)], s_sq).then_inc(s_ss, 1)

            @block.scalar
            def _(act):
                for k in range(KD):
                    act.activation(sq[:, k, :], X[:, k, :], ACT.Square).then_inc(s_sq, 1)
                act.wait_ge(s_ss, 1)
                act.activation(rms, PS[:, 0, :], ACT.Sqrt, bias=EPS, scale=1.0 / D).then_inc(s_rms, 1)
                ahead.scalar(act)
                for k in range(KD):
                    act.wait_ge(s_xn, k + 1)
                    act.copy(XS[:, 0, k, :], X[:, k, :]).then_inc(s_xh, 1)

            @block.vector
            def _(dve):
                dve.wait_ge(s_rms, 1)
                dve.reciprocal(rms, rms).then_inc(s_rc, 1)
                dve.wait_ge(s_rc, 1)
                dve.wait_ge(s_g, 32)
                for k in range(KD + 1):
                    if k < KD:
                        dve.scalar_tensor_tensor(X[:, k, :], X[:, k, :], gain[:, k:k + 1], rms,
                                                 ALU.mult, ALU.mult).then_inc(s_xn, 1)
                    if k:
                        dve.wait_ge(s_xh, k)
                        dve.tensor_tensor(XS[:, 1, k - 1, :], X[:, k - 1, :], XS[:, 0, k - 1, :].bitcast(F32),
                                          ALU.subtract).then_inc(s_xl, 1)

        end_phase()

        class LayerNorm:

            def __init__(self, name, sq, acc, ready, base, gain, bias):
                self.sq, self.acc, self.rstd, self.ready, self.base = sq, acc, rstd_all[:, :], ready, base
                self.gain, self.bias = gain, bias
                (self.tiles, self.sum, self.centred, self.squared, self.added, self.std, self.inv, self.scaled,
                 self.done, self.high, self.low) = (sem(f"{name}_{x}") for x in (
                     "tiles_added", "sum", "centred", "squared", "square_added", "deviation", "inverse", "scaled", "normed",
                     "rounded", "split"))

            def tensor(self, pe):
                column_sum(pe, 6, [self.acc], self.tiles, KD).then_inc(self.sum, 1)
                for k in range(KD):
                    pe.wait_ge(self.squared, k + 1)
                    pe.matmul(PS[:, 7, :], ones, self.sq[:, k % 2, :], start=(k == 0),
                              stop=(k == KD - 1)).then_inc(self.added, 1)

            def scalar(self, act):
                for k in range(KD):
                    act.wait_ge(self.centred, k + 1)
                    if k >= 2:
                        act.wait_ge(self.added, k - 1)
                    act.activation(self.sq[:, k % 2, :], X[:, k, :], ACT.Square).then_inc(self.squared, 1)
                act.wait_ge(self.added, KD)
                act.activation(self.rstd, PS[:, 7, :], ACT.Sqrt, bias=LN_EPS, scale=1.0 / D).then_inc(self.std, 1)

            def scalar_finish(self, act):
                for k in range(KD):
                    act.wait_ge(self.scaled, k + 1)
                    act.activation(X[:, k, :], X[:, k, :], ACT.Identity,
                                   bias=self.bias[:, k:k + 1]).then_inc(self.done, 1)
                    act.wait_ge(self.done, k + 1)
                    act.copy(XS[:, 0, k, :], X[:, k, :]).then_inc(self.high, 1)

            def begin(self, dve):
                dve.memset(self.acc, 0.0).then_inc(self.tiles, 1)

            def accumulate(self, dve, x, m):
                dve.wait_ge(self.ready, m + (self.base + 1))
                dve.wait_ge(self.tiles, m + 1)
                dve.tensor_tensor(self.acc, self.acc, x, ALU.add).then_inc(self.tiles, 1)

            def vector(self, dve):
                dve.wait_ge(self.sum, 1)
                for k in range(KD):
                    dve.scalar_tensor_tensor(X[:, k, :], PS[:, 6, :], -1.0 / D, X[:, k, :],
                                             ALU.mult, ALU.add).then_inc(self.centred, 1)
                dve.wait_ge(self.std, 1)
                dve.reciprocal(self.rstd, self.rstd).then_inc(self.inv, 1)
                dve.wait_ge(self.inv, 1)
                dve.wait_ge(self.squared, KD)

            def vector_finish(self, dve):
                for k in range(KD + 1):
                    if k < KD:
                        dve.scalar_tensor_tensor(X[:, k, :], X[:, k, :], self.gain[:, k:k + 1], self.rstd,
                                                 ALU.mult, ALU.mult).then_inc(self.scaled, 1)
                    if k:
                        dve.wait_ge(self.high, k)
                        dve.tensor_tensor(XS[:, 1, k - 1, :], X[:, k - 1, :], XS[:, 0, k - 1, :].bitcast(F32),
                                          ALU.subtract).then_inc(self.low, 1)

        def feed_forward(l, half, s_par, after, before=None):
            nm = lambda x: sem(f"ffn{half}_{x}")
            s_ld = [nm("weights_loaded_0"), nm("weights_loaded_1")]
            (s_hi, s_lo, s_g, s_u, s_si, s_p, s_hh, s_hl, s_hf, s_r) = (nm(x) for x in (
                "weights_rounded", "weights_split", "gate_product", "unit_multiplied", "gate_activated",
                "hidden_ready", "hidden_rounded", "hidden_split", "down_halved", "residual_added"))
            KH = KF // 2
            DN = KH * P
            ar = Arena(f"ffn{half}", 4 * T)
            hid = ar.parts(f"hidden_parts{half}", 2 * KF * T).rearrange("p (a k t) -> p a k t", a=2, k=KF)
            gs, pt = split3(ar.take(2 * T), 2), split3(ar.take(2 * T), 2)
            hf = gs
            ln_i = 0 if half == 0 else 2
            ln = LayerNorm(f"ffn{half}_norm", gs, pt[:, 0, :], s_r, 2,
                           p2("ln_g")[:, ln_i * 8:ln_i * 8 + 8], p2("ln_b")[:, ln_i * 8:ln_i * 8 + 8])
            gu = lambda u: dr["w_gu"][bass.ds(l * (2 * KF) + (u + half * KF), 1)].rearrange("a p n -> (a p) n")
            dn = dr["w_d"][bass.ds(l, 1)]
            flat = lambda t: t.rearrange("p a t -> p (a t)")
            with nc.Block() as block:
                @block.sync
                def _(sp):
                    if half == 0:
                        sp.dma_start(par[:, 0:P2N], dr["par2"][bass.ds(l, 1)].rearrange("a p n -> (a p) n")).then_inc(s_par, 16)
                    sp.sem_inc(s_lo, 3)
                    sp.sem_inc(s_ld[0], 16)
                    sp.dma_start(RAW[:, 1, :], gu(1)).then_inc(s_ld[1], 16)
                    with sp.Fori(1, KH) as i:
                        for b in range(2):
                            sp.wait_ge(s_lo, i * 2 + (b + 1))
                            sp.dma_start(RAW[:, b, :], gu(i * 2 + b)).then_inc(s_ld[b], 16)
                    with sp.Fori(0, KD) as m:
                        for b in range(2):
                            sp.wait_ge(s_lo, m * 2 + (KF + b + 1))
                            sp.dma_start(RAW[:, b, 0:DN], dn[:, half, bass.ds(m, 1), :, b * DN:(b + 1) * DN]
                                         .rearrange("a c p n -> (a c p) n")).then_inc(s_ld[b], 16)
                    sp.wait_ge(s_lo, KF + 2 * KD + 2)
                    after.sync(sp)

                @block.gpsimd
                def _(pool):
                    def lower(b, n, count):
                        pool.wait_ge(s_hi, count)
                        pool.tensor_tensor(WP[:, b, 1, 0:n], RAW[:, b, 0:n], WP[:, b, 0, 0:n].bitcast(F32),
                                           ALU.subtract).then_inc(s_lo, 1)

                    lower(1, UNIT, 2)
                    with pool.Fori(1, KH) as i:
                        for b in range(2):
                            lower(b, UNIT, i * 2 + (b + 1))
                    with pool.Fori(0, KD) as m:
                        for b in range(2):
                            lower(b, DN, m * 2 + (KF + b + 1))
                    after.gpsimd(pool)

                @block.tensor
                def _(pe):
                    passes = ((0, 0), (0, 1), (1, 0))
                    with pe.Fori(0, KH) as i:
                        for b in range(2):
                            pe.wait_ge(s_lo, i * 2 + (b + 3))
                            pe.wait_ge(s_p, i * 2 + (b + 1))
                            for g, s in ((0, s_g), (1, s_u)):
                                for k in range(KD):
                                    if before and g == 0:
                                        pe.wait_ge(before.low, k + 1)
                                    for n, (w, x) in enumerate(passes):
                                        c = (g * KD + k) * P
                                        last = pe.matmul(PS[:, 2 * b + g, :], WP[:, b, w, c:c + P], XS[:, x, k, :],
                                                         start=(k == 0 and n == 0), stop=(k == KD - 1 and n == 2))
                                last.then_inc(s, 1)
                    pe.wait_ge(s_hl, KF + 2)
                    with pe.Fori(0, KD // 2) as i:
                        for mm in range(2):
                            for b in range(2):
                                pe.wait_ge(s_lo, i * 4 + (KF + 2 * mm + b + 3))
                                if b == 0:
                                    pe.wait_ge(s_hf, i * 2 + (mm + 1))
                                for k in range(KH):
                                    for n, (w, x) in enumerate(passes):
                                        last = pe.matmul(PS[:, 4 + mm, :], WP[:, b, w, k * P:(k + 1) * P],
                                                         hid[:, x, b * KH + k, :], start=(b == k == n == 0),
                                                         stop=(b == 1 and k == KH - 1 and n == 2))
                                last.then_inc(s_u, 1)
                    ln.tensor(pe)

                @block.scalar
                def _(act):
                    act.sem_inc(s_hf, 2)
                    if before:
                        before.scalar_finish(act)
                    with act.Fori(0, KH) as i:
                        for b in range(2):
                            act.wait_ge(s_g, i * 2 + (b + 1))
                            act.wait_ge(s_p, i * 2 + (b + 1))
                            act.activation(gs[:, b, :], PS[:, 2 * b, :], ACT.Silu).then_inc(s_si, 1)
                            act.wait_ge(s_p, i * 2 + (b + 3))
                            act.copy(flat(hid[:, 0, bass.ds(i * 2 + b, 1), :]), pt[:, b, :]).then_inc(s_hh, 1)
                    with act.Fori(0, KD // 2) as i:
                        for mm in range(2):
                            act.wait_ge(s_u, i * 4 + (KF + 2 * mm + 4))
                            act.wait_ge(s_r, i * 2 + (mm + 1))
                            act.activation(hf[:, mm, :], PS[:, 4 + mm, :], ACT.Copy, scale=0.5).then_inc(s_hf, 1)
                    act.wait_ge(s_u, KF + 2 * KD + 2)
                    after.scalar(act)
                    act.wait_ge(s_r, KD + 2)
                    ln.scalar(act)
                    if half == 1:
                        ln.scalar_finish(act)

                @block.vector
                def _(dve):
                    def high(b, n, count, used):
                        dve.wait_ge(s_ld[b], count)
                        dve.wait_ge(s_u, used)
                        dve.tensor_copy(WP[:, b, 0, 0:n], RAW[:, b, 0:n]).then_inc(s_hi, 1)

                    def residual(i, mm):
                        dve.wait_ge(s_hf, i * 2 + (mm + 3))
                        x = X[:, bass.ds(i * 2 + mm, 1), :].rearrange("p a t -> p (a t)")
                        dve.scalar_tensor_tensor(x, x, ALPHA, hf[:, mm, :], ALU.mult, ALU.add).then_inc(s_r, 1)
                        ln.accumulate(dve, x, i * 2 + mm)

                    dve.sem_inc(s_p, 2)
                    dve.sem_inc(s_r, 2)
                    dve.sem_inc(s_u, 2)
                    dve.sem_inc(s_hl, 2)
                    dve.sem_inc(s_hi, 1)
                    high(1, UNIT, 16, 2)
                    if before:
                        before.vector_finish(dve)
                    with dve.Fori(0, KH) as i:
                        for b in range(2):
                            dve.wait_ge(s_si, i * 2 + (b + 1))
                            dve.wait_ge(s_u, i * 2 + (b + 3))
                            dve.wait_ge(s_hl, i * 2 + (b + 1))
                            dve.tensor_tensor(pt[:, b, :], PS[:, 2 * b + 1, :], gs[:, b, :], ALU.mult).then_inc(s_p, 1)
                            high(b, UNIT, i * 16 + 32, i * 2 + (b + 3))
                            dve.wait_ge(s_hh, i * 2 + (b + 1))
                            n = bass.ds(i * 2 + b, 1)
                            dve.tensor_tensor(flat(hid[:, 1, n, :]), pt[:, b, :], flat(hid[:, 0, n, :]).bitcast(F32),
                                              ALU.subtract).then_inc(s_hl, 1)
                    dve.wait_ge(s_hl, KF + 2)
                    ln.begin(dve)
                    with dve.Fori(0, KD // 2 - 1) as i:
                        for mm in range(2):
                            for b in range(2):
                                high(b, DN, i * 32 + 16 * (KH + mm + 2), i * 4 + (KF + 2 * mm + b + 3))
                            residual(i, mm)
                    i = KD // 2 - 1
                    for mm in range(2):
                        for b in range(2 if mm == 0 else 0):
                            high(b, DN, i * 32 + 16 * (KH + mm + 2), i * 4 + (KF + 2 * mm + b + 3))
                        residual(i, mm)
                    ln.vector(dve)
                    if half == 0:
                        dve.wait_ge(s_par, 16)
                    else:
                        ln.vector_finish(dve)
            return ln

        def mixer_streams(l):
            stream = Stream([sem(f"mix_weights_loaded_{i}") for i in range(SLOTS)], sem("mix_weights_rounded"),
                            sem("mix_weights_lowered"))
            projected, evacuated = sem("mix_projected"), sem("mix_evacuated")
            proj = Project(stream, projected, evacuated)

            drl = lambda name, *ix: of_layer(name, l, *ix)

            two = [(0, P), (P, P)]
            wu = lambda i: drl("w_in2", i)
            J = {}
            J["kc"] = proj.feature_major(wu(2), UC, two)
            J["ga"] = proj.feature_major(drl("w_ga"), P, [(0, P)])
            J["g"] = proj.feature_major(wu(5), UC, two)
            J["gv"] = proj.token_major(wu(8), UC)
            end_c = len(stream.units)
            J["u"] = proj.feature_major(wu(4), UC, two)
            J["gr"] = proj.feature_major(wu(6), UC, two)
            end_1 = len(stream.units)
            J["gl"] = proj.feature_major(drl("w_gl"), P, [(0, P)])
            J["nq"] = [proj.feature_major(wu(i), UC, two) for i in (0, 1)][0]
            J["k"] = proj.feature_major(wu(3), UC, two)
            J["v"] = proj.token_major(wu(7), UC)
            end_2 = len(stream.units)
            J["out"] = [proj.feature_major(drl("w_out2", i), UC, two) for i in range(4)][0]
            return stream, projected, evacuated, proj, J, end_c, end_1, end_2

        class MixerAhead:

            def __init__(self, stream):
                self.stream = stream

            def sync(self, sp):
                self.stream.send(sp, RAW, SLOTS)

            def scalar(self, act):
                self.stream.round(act, act.copy, RAW, WP, SLOTS)

            def gpsimd(self, pool):
                self.stream.lower(pool, RAW, WP, SLOTS)

        def mix_tokens(l, streams, after, before):
            stream, projected, evacuated, proj, J, end_c, end_1, end_2 = streams
            drl = lambda name, *ix: of_layer(name, l, *ix)
            phase[0].close()
            mixing = ExitStack()
            mixed = sb("mixed", 8 * T, stack=mixing)
            M = split3(mixed[:, :], 8)
            carry = sb("mixer_carry", 512 + 64 + 576 + 3 * T + 4 * T + 2 * 528, stack=mixing)
            at = [0]

            def keep(n):
                at[0] += n
                return carry[:, at[0] - n:at[0]]

            vbd = split3(keep(512), 2)
            kc_ = keep(64)
            kc = split3(kc_[0:64], 2)
            sw = keep(128 + 64 + 256 + 128)
            gaT, gq, gk = keep(T), keep(T), keep(T)
            gv = split3(keep(4 * T)[0:64], NGC)
            up = split3(keep(2 * 528), 2)

            nb = lambda n: sem("gla_" + n)
            s_mw = nb("small_weights_loaded")
            s_z, s_lg, s_x, s_mg, s_ex, s_w1, s_ln = (nb(x) for x in (
                "buffers_zeroed", "gate_logits", "gate_biased", "gate_magnitude", "gate_exp", "gate_one_plus",
                "gate_log"))
            s_v, s_b, s_e, s_qt, s_bd, s_kt, s_kk, s_kkc = (nb(x) for x in (
                "vector_step", "log_decay", "decays_ready", "q_ready", "q_spread", "k_ready", "k_turned",
                "k_turned_copied"))
            s_at, s_am, s_ds, s_st, s_o, s_oc = (nb(x) for x in (
                "scores", "scores_masked", "state_products", "state_ready", "output", "output_copied"))
            s_s2, s_r, s_n, s_t = (nb(x) for x in ("square_sums", "rms", "normed", "turned"))
            s_pp, s_pd, s_pm, s_pw = (sem("pool_" + x) for x in ("step", "pooled", "product", "scaled"))
            s_pe, s_c1, s_cg, s_c2, s_cc = (sem("cmp_" + x) for x in (
                "position_added", "first_product", "activated", "second_product", "copied"))
            s_fin = nb("tile_done")
            s_zc = sem("cmp_buffers_zeroed")
            jc, ja, jg, jv, ju, jr, je = (J[x] for x in ("kc", "ga", "g", "gv", "u", "gr", "gl"))
            def evacuate(act, j):
                proj.after(j - 1, act)
                act.wait_ge(projected, j + 1)
                bk = PS[:, j % 2, :]
                if j < ja:
                    act.copy(zr[0:64, j - jc, 0, :], bk[0:64, :])
                    ins = act.copy(zr[0:64, j - jc, 1, :], bk[64:128, :])
                elif j < jg:
                    ins = act.copy(gaT[0:16, :], bk[0:16, :])
                elif j < jv:
                    ins = act.copy(gq if j == jg else gk, bk)
                elif j < ju:
                    t = j - jv
                    act.copy(gv[:, 2 * t, :], bk[0:64, 0:256])
                    ins = act.copy(gv[:, 2 * t + 1, :], bk[64:128, 0:256])
                elif j < jr:
                    ins = act.copy(up[:, j - ju, 16:528], bk)
                else:
                    ins = act.activation(M[:, 6 + j - jr, :], bk, ACT.Silu)
                ins.then_inc(evacuated, 1)

            ar = Arena("compress", 4096 + 2048 + 4096 + 128)
            zr = ar.take(2048).rearrange("p (v g t) -> p v g t", v=2, g=2)
            with nc.Block() as block:
                w1 = ar.take(4096).rearrange("p (v l e) -> p v l e", v=2, l=CB)
                zp = ar.take(4096).rearrange("p (v a g t) -> p v a g t", v=2, a=2, g=2)
                act_g = ar.take(128).rearrange("p (v g n) -> p v g n", v=2, g=2)

                @block.sync
                def _(sp):
                    sp.dma_start(w1[0:64].rearrange("p v l e -> p (v l e)"), drl("w_c1")).then_inc(s_mw, 16)
                    sp.dma_start(sw, drl("w_small")).then_inc(s_mw, 16)
                    stream.send(sp, RAW, end_c + 2 * SLOTS)

                @block.gpsimd
                def _(pool):
                    pool.memset(vbd, 0.0).then_inc(s_zc, 1)
                    pool.memset(kc_[0:64], 0.0).then_inc(s_zc, 1)
                    stream.lower(pool, RAW, WP, end_c + SLOTS)

                @block.tensor
                def _(pe):
                    for j in range(0, jv):
                        proj.run(pe, j, tokens, before.low if j == 0 else None)
                    pe.wait_ge(s_mw, 32)
                    pe.wait_ge(s_pe, 4)
                    for v in range(2):
                        for l_ in range(CB):
                            a, r = divmod(l_, CS)
                            rhs = zp[0:64, v, a].rearrange("p g (n l) -> p g n l", l=CS)[:, :, a:a + NCMP, r]
                            last = pe.matmul(PS[0:64, 2 + v, 0:2 * NCMP], w1[0:64, v, l_, :], rhs,
                                             start=(l_ == 0), stop=(l_ == CB - 1))
                        last.then_inc(s_c1, 1)
                    for j in range(jv, ju):
                        proj.run(pe, j, tokens)
                    pe.wait_ge(s_cg, 2)
                    pe.matmul(PS[0:64, 4, 0:2 * NCMP], sw[0:64, 0:64],
                              act_g[0:64, 0].rearrange("p g n -> p (g n)")[:, 0:2 * NCMP],
                              start=True, stop=True).then_inc(s_c2, 1)
                    for g in range(NG):
                        last = pe.matmul(PS[0:NCMP, 5, g * HD:(g + 1) * HD],
                                         act_g[0:64, 1].rearrange("p g n -> p (g n)")[:, g * NCMP:(g + 1) * NCMP],
                                         sw[0:64, 64:128], start=True, stop=True)
                    last.then_inc(s_c2, 1)

                @block.scalar
                def _(act):
                    before.scalar_finish(act)
                    for j in range(0, jv):
                        evacuate(act, j)
                    for v in range(2):
                        act.wait_ge(s_c1, v + 1)
                        act.activation(act_g[0:64, v].rearrange("p g n -> p (g n)")[:, 0:2 * NCMP],
                                       PS[0:64, 2 + v, 0:2 * NCMP], ACT.Gelu_apprx_tanh).then_inc(s_cg, 1)
                    for j in range(jv, ju):
                        evacuate(act, j)
                    proj.after(ju - 1, act)
                    act.wait_ge(s_zc, 2)
                    act.wait_ge(s_c2, 1)
                    act.copy(kc[:, :, 0:NCMP], PS[0:64, 4, 0:2 * NCMP].rearrange("p (g n) -> p g n", g=2)).then_inc(s_cc, 1)
                    act.wait_ge(s_c2, 2)
                    for g in range(NG):
                        for r in range(4):
                            act.copy(vbd[32 * r:32 * r + NCMP, g, r * HD:(r + 1) * HD],
                                     PS[0:NCMP, 5, g * HD:(g + 1) * HD]).then_inc(s_cc, 1)

                @block.vector
                def _(dve):
                    before.vector_finish(dve)
                    dve.wait_ge(s_mw, 32)
                    dve.wait_ge(evacuated, ja)
                    for v in range(2):
                        for a in range(2):
                            z3 = lambda t: t.rearrange("p g (n l) -> p (g n) l", l=CS)
                            dve.tensor_tensor(z3(zp[0:64, v, a]), z3(zr[0:64, v]),
                                              repeat(sw[0:64, 128 + 32 * v + CS * a:128 + 32 * v + CS * (a + 1)], 64),
                                              ALU.add).then_inc(s_pe, 1)

            ar = Arena("gla", 13128)
            with nc.Block() as block:
                b, e1, e2, kt, kd, xg = (ar.take(T) for _ in range(6))
                qbd_ = ar.take(2048)
                qbd = qbd_.rearrange("p (c h i) -> p c h i", c=NGC, h=GH)
                AT = split3(ar.take(512), 2)
                Sb = ar.take(256)
                kdt = split3(ar.take(NGC * P), NGC)
                pa, pb = ar.take(528), ar.take(528)
                pooled = split3(ar.take(2 * T), 2)
                dcy = ar.take(NGC)
                ss = ar.take(32)
                mag, one, lgt, qt = (ar.take(T) for _ in range(4))
                oa = split3(ar.take(4 * T)[0:64], NGC)
                osq = split3(qbd_[0:64], NGC)

                @block.sync
                def _(sp):
                    stream.send(sp, RAW, end_1 + 2 * SLOTS)

                @block.gpsimd
                def _(pool):
                    pool.memset(qbd, 0.0).then_inc(s_z, 1)
                    pool.memset(AT, 0.0).then_inc(s_z, 1)
                    pool.memset(Sb, 0.0).then_inc(s_z, 1)
                    pool.memset(up[:, :, 0:16], 0.0).then_inc(s_z, 1)
                    pool.memset(pa[:, 0:16], 0.0).then_inc(s_z, 1)
                    pool.memset(pb[:, 0:16], 0.0).then_inc(s_z, 1)
                    stream.lower(pool, RAW, WP, end_1)
                    link = chain(pool, s_pp)
                    pool.wait_ge(s_z, 6)
                    for t in range(2):
                        pool.wait_ge(evacuated, ju + t + 1)
                        src, w, bufs = up[:, t, :], 1, [pa, pb]
                        for n in range(2 + 2 * t):
                            dst = bufs[n % 2]
                            link(pool.tensor_tensor(dst[:, 16:528], src[:, 16:528], src[:, 16 - w:528 - w], ALU.add))
                            src, w = dst, 2 * w
                            half = {(0, 0): 0, (0, 1): 1, (1, 2): 0, (1, 3): 1}.get((t, n))
                            if half is not None:
                                r = slice(64 * half, 64 * half + 64)
                                inv = spec[r, C2["invcnt"][0] + t * T:C2["invcnt"][0] + (t + 1) * T]
                                link(pool.tensor_tensor(pooled[r, t, :], dst[r, 16:528], inv, ALU.mult))
                        pool.tensor_tensor(pooled[:, t, :], pooled[:, t, :], up[:, t, 16:528],
                                           ALU.subtract).then_inc(s_pd, 1)
                    stream.lower(pool, RAW, WP, end_1 + SLOTS)

                @block.tensor
                def _(pe):
                    pe.matmul(PS[:, 4, :], sw[0:16, 448:576], gaT[0:16, :], start=True, stop=True).then_inc(s_lg, 1)
                    for j in range(ju, je):
                        proj.run(pe, j, tokens)
                    pe.wait_ge(s_kt, 2)
                    pe.wait_ge(evacuated, je)
                    pe.wait_ge(s_x, 1)
                    for c in range(NGC):
                        last = pe.transpose(PS[0:64, 4 + c // 4, (c % 4) * P:(c % 4 + 1) * P],
                                            kd[:, c * GC:(c + 1) * GC], ident)
                        if c % 4 == 3:
                            last.then_inc(s_kk, 1)
                    pe.wait_ge(s_kkc, 2)
                    pe.wait_ge(s_bd, 4)
                    pe.wait_ge(s_qt, 1)

                    def scores(c):
                        if c >= 2:
                            pe.wait_ge(s_am, c - 1)
                        pe.matmul(PS[0:64, 4 + c % 2, 0:256], kt[:, c * GC:(c + 1) * GC],
                                  qbd[:, c, :, :], start=True, stop=True).then_inc(s_at, 1)

                    scores(0)
                    for c in range(NGC):
                        if c + 1 < NGC:
                            scores(c + 1)
                        if c >= 2:
                            pe.wait_ge(s_oc, c - 1)
                        if c < NGC - 1:
                            if c >= 2:
                                pe.wait_ge(s_st, c - 1)
                            pe.matmul(PS[:, c % 2, 0:256], kdt[0:64, c, :], gv[:, c, :],
                                      start=True, stop=True).then_inc(s_ds, 1)
                        if c:
                            pe.wait_ge(s_st, c)
                            pe.matmul(PS[0:64, 6 + c % 2, 0:256], qt[:, c * GC:(c + 1) * GC], Sb,
                                      start=True, stop=False, skip_group_check=True)
                        pe.wait_ge(s_am, c + 1)
                        for h in range(GH):
                            last = pe.matmul(PS[0:64, 6 + c % 2, h * GV:(h + 1) * GV],
                                             AT[0:64, c % 2, h * GC:(h + 1) * GC], gv[:, c, h * GV:(h + 1) * GV],
                                             start=(c == 0), stop=True, skip_group_check=True)
                        last.then_inc(s_o, 1)
                    for t in range(2):
                        pe.wait_ge(s_pd, t + 1)
                        pe.wait_ge(s_am, NGC)
                        pe.matmul(PS[:, 4 + t, :], sw[:, 192 + t * P:192 + (t + 1) * P], pooled[:, t, :],
                                  start=True, stop=True).then_inc(s_pm, 1)
                    pe.wait_ge(s_n, 1)
                    for t in range(2):
                        pe.wait_ge(s_oc, NGC)
                        for c in range(NGC):
                            last = pe.transpose(PS[:, 6 + t, c * GC:(c + 1) * GC], oa[:, c, t * P:(t + 1) * P],
                                                ident[0:64, 0:64])
                        last.then_inc(s_t, 1)

                @block.scalar
                def _(act):
                    act.wait_ge(s_lg, 1)
                    act.activation(xg, PS[:, 4, :], ACT.Identity, bias=p2("gla_ba")).then_inc(s_x, 1)
                    act.wait_ge(s_mg, 1)
                    act.activation(e1, mag, ACT.Exp, scale=-1.0).then_inc(s_ex, 1)
                    act.wait_ge(s_w1, 1)
                    act.activation(lgt, one, ACT.Ln).then_inc(s_ln, 1)
                    for j in range(ju, ju + 2):
                        evacuate(act, j)
                    act.wait_ge(s_b, 1)
                    act.activation(e1, b, ACT.Exp).then_inc(s_e, 1)
                    act.activation(e2, b, ACT.Exp, scale=-1.0).then_inc(s_e, 1)
                    act.activation(dcy, b.rearrange("p (c i) -> p c i", c=NGC)[:, :, GC - 1], ACT.Exp).then_inc(s_e, 1)
                    act.wait_ge(s_b, 2)
                    act.activation(mag, mag, ACT.Exp).then_inc(s_e, 1)
                    for j in range(ju + 2, je):
                        evacuate(act, j)
                    proj.after(je - 1, act)
                    act.wait_ge(s_z, 1)
                    act.wait_ge(s_qt, 1)
                    for h in range(GH):
                        r = slice(GK * h, GK * (h + 1))
                        act.copy(qbd[r, :, h, :], split3(qt[r, :], NGC)).then_inc(s_bd, 1)
                    for n in range(2):
                        act.wait_ge(s_kk, n + 1)
                        act.copy(kdt[0:64, 4 * n:4 * n + 4, :], split3(PS[0:64, 4 + n, :], 4)).then_inc(s_kkc, 1)
                    for c in range(NGC):
                        act.wait_ge(s_o, c + 1)
                        act.copy(oa[:, c, :], PS[0:64, 6 + c % 2, 0:256]).then_inc(s_oc, 1)
                    for t in range(2):
                        act.wait_ge(s_pm, t + 1)
                        act.activation(M[:, 4 + t, :], PS[:, 4 + t, :], ACT.Copy,
                                       scale=p2("pool_s")[:, t:t + 1]).then_inc(s_pw, 1)
                    act.wait_ge(s_s2, 1)
                    act.activation(ss[0:64, :], ss[0:64, :], ACT.Sqrt, bias=EPS, scale=1.0 / GV).then_inc(s_r, 1)

                @block.vector
                def _(dve):
                    link = chain(dve, s_v)
                    dve.wait_ge(s_x, 1)
                    dve.scalar_tensor_tensor(mag, xg, -1.0, xg, ALU.mult, ALU.max).then_inc(s_mg, 1)
                    dve.wait_ge(s_ex, 1)
                    dve.tensor_scalar(one, e1, 1.0, None, ALU.add).then_inc(s_w1, 1)
                    dve.wait_ge(s_w1, 1)
                    link(dve.scalar_tensor_tensor(mag, one, 1.0, e1, ALU.subtract, ALU.subtract))
                    dve.wait_ge(s_ln, 1)
                    link(dve.reciprocal(one, one))
                    link(dve.tensor_tensor(mag, mag, one, ALU.mult))
                    link(dve.tensor_tensor(lgt, lgt, mag, ALU.subtract))
                    link(dve.scalar_tensor_tensor(xg, xg, 0.0, lgt, ALU.min, ALU.subtract))
                    link(dve.tensor_scalar(xg, xg, 1.0 / 16.0, None, ALU.mult))
                    dve.tensor_tensor_scan(b, const("reset", C2, spec), xg, 0.0, ALU.mult, ALU.add).then_inc(s_b, 1)
                    dve.wait_ge(s_b, 1)
                    b3 = b.rearrange("p (c i) -> p c i", c=NGC)
                    dve.tensor_tensor(split3(mag, NGC), spread(b3[:, :, GC - 1], GC), b3, ALU.subtract).then_inc(s_b, 1)
                    dve.wait_ge(s_e, 1)
                    dve.scalar_tensor_tensor(qt, gq, GK ** -0.5, e1, ALU.mult, ALU.mult).then_inc(s_qt, 1)
                    dve.wait_ge(s_e, 2)
                    dve.tensor_tensor(kt, gk, e2, ALU.mult).then_inc(s_kt, 1)
                    dve.wait_ge(s_e, 4)
                    dve.tensor_tensor(kd, gk, mag, ALU.mult).then_inc(s_kt, 1)
                    gm = const("gmask", C2, spec)[0:64, :].bitcast(mybir.dt.uint32)
                    dve.wait_ge(s_z, 3)

                    def mask(c):
                        dve.wait_ge(s_at, c + 1)
                        if c >= 2:
                            dve.wait_ge(s_o, c - 1)
                        dve.copy_predicated(AT[0:64, c % 2, :], gm, PS[0:64, 4 + c % 2, 0:256]).then_inc(s_am, 1)

                    mask(0)
                    for c in range(NGC):
                        if c + 1 < NGC:
                            mask(c + 1)
                            dve.wait_ge(s_ds, c + 1)
                            if c:
                                dve.wait_ge(s_o, c + 1)
                                dve.wait_ge(s_st, c)
                            for h in range(GH):
                                r = slice(GK * h, GK * (h + 1))
                                cs = slice(GV * h, GV * (h + 1))
                                last = dve.scalar_tensor_tensor(Sb[r, cs], Sb[r, cs], dcy[r, c:c + 1],
                                                                PS[r, c % 2, cs], ALU.mult, ALU.add)
                            last.then_inc(s_st, 1)
                    dve.wait_ge(s_oc, NGC)
                    dve.wait_ge(s_am, NGC)
                    dve.wait_ge(s_at, NGC)
                    link(dve.tensor_tensor(osq, oa, oa, ALU.mult))
                    dve.tensor_reduce(ss[0:64, :], osq.rearrange("p c (h v) -> p (c h) v", h=GH), AX.X,
                                      ALU.add).then_inc(s_s2, 1)
                    dve.wait_ge(s_r, 1)
                    link(dve.reciprocal(ss[0:64, :], ss[0:64, :]))
                    o3 = oa.rearrange("p c (h v) -> p (c h) v", h=GH)
                    dve.tensor_tensor(o3, o3, spread(ss[0:64, :], GV), ALU.mult).then_inc(s_n, 1)
                    for t in range(2):
                        dve.wait_ge(s_t, t + 1)
                        dve.scalar_tensor_tensor(M[:, 6 + t, :], PS[:, 6 + t, :], p2("gla_g")[:, t:t + 1],
                                                 M[:, 6 + t, :], ALU.mult, ALU.mult).then_inc(s_fin, 1)

            s_cs, s_cd, s_ce, s_cn, s_cv, s_ct, s_ctc, s_co, s_cf = (sem("cmpatt_" + x) for x in (
                "scored", "shifted", "exp", "normed", "vector_step", "turned", "turned_copied", "weighted", "added"))
            s_os, s_ot, s_oe = (sem("nsa_" + x) for x in ("output_done", "output_turned", "output_copied"))
            s_gt, s_gc = (sem("branch_gates_" + x) for x in ("turned", "turned_copied"))
            ar = Arena("nsa", 15072)
            with nc.Block() as block:
                q = split3(ar.take(NH * T), NH)
                otok = split3(ar.take(4 * T), 4)
                kk = ar.take(4 * T).rearrange("p (w g t) -> p w g t", w=2, g=2)
                v = split3(ar.take(4 * 256), 4)
                gl = split3(ar.take(96), 4)
                buf = (split3(ar.take(2 * T), 2), split3(ar.take(2 * T), 2), split3(ar.take(2 * T), 2),
                       ar.take(32), ar.take(32))
                pc = split3(ar.take(4 * 256), 4)
                pct = split3(ar.take(4 * 256), 4)
                mx, den, coef = ar.take(8), ar.take(8), ar.take(8)
                tmp = ar.take(T)
                glT = tmp[0:24, :]
                att = [Attention(n, NH, q, (lambda w: lambda h: kk[:, w, h // 4, :])(w),
                                 (lambda w: lambda h, t: v[:, t, w * P + (h // 4) * HD:w * P + (h // 4 + 1) * HD])(w),
                                 64, buf) for w, n in enumerate(("selected", "window"))]
                jl, jq, jk, jv, je = J["gl"], J["nq"], J["k"], J["v"], J["out"]

                @block.sync
                def _(sp):
                    stream.send(sp, RAW, end_2 + 2 * SLOTS)

                @block.gpsimd
                def _(pool):
                    stream.lower(pool, RAW, WP, end_2 + SLOTS)

                @block.tensor
                def _(pe):
                    for j in range(jl, jk):
                        proj.run(pe, j, tokens)
                        if j == jq:
                            pe.wait_ge(evacuated, jq)
                            for i in range(NT):
                                last = pe.transpose(PS[:, 7, i * 24:(i + 1) * 24], glT[:, i * P:(i + 1) * P],
                                                    ident[0:24, 0:24])
                            last.then_inc(s_gt, 1)
                    pe.wait_ge(evacuated, jk)
                    for i in range(NT):
                        if i >= 2:
                            pe.wait_ge(s_cd, i - 1)
                        for h in range(NH):
                            last = pe.matmul(PS[:, 4 + i % 2, h * 32:(h + 1) * 32], q[0:64, h, i * P:(i + 1) * P],
                                             kc[:, h // 4, :], start=True, stop=True)
                        last.then_inc(s_cs, 1)
                    for j in range(jk, je):
                        proj.run(pe, j, tokens)
                        if j >= jv:
                            i = j - jv
                            pe.wait_ge(s_cn, i + 1)
                            if i == 1:
                                pe.wait_ge(s_gc, 1)
                            if i >= 2:
                                pe.wait_ge(s_ctc, i - 1)
                            for g in range(NG):
                                last = pe.transpose(PS[:, 6 + i % 2, g * P:(g + 1) * P],
                                                    pc[:, i, g * P:(g + 1) * P], ident)
                            last.then_inc(s_ct, 1)
                    for i in range(NT):
                        pe.wait_ge(s_ctc, i + 1)
                        if i >= 2:
                            pe.wait_ge(s_cf, i - 1)
                        for g in range(NG):
                            last = pe.matmul(PS[:, 2 + i % 2, g * 256:(g + 1) * 256], pct[:, i, g * P:(g + 1) * P],
                                             vbd[:, g, :], start=True, stop=True)
                        last.then_inc(s_co, 1)
                    pe.wait_ge(evacuated, je)
                    pe.wait_ge(s_cd, NT)
                    for a in att:
                        a.tensor(pe)
                    for f in range(NT):
                        if f == 0:
                            pe.wait_ge(s_os, 1)
                            pe.wait_ge(s_cf, NT)
                        if f >= 2:
                            pe.wait_ge(s_oe, f - 1)
                        for i in range(NT):
                            last = pe.transpose(PS[:, 2 + f % 2, i * P:(i + 1) * P], otok[:, i, f * P:(f + 1) * P], ident)
                        last.then_inc(s_ot, 1)

                @block.scalar
                def _(act):
                    def evacuate_heads(j):
                        proj.after(j - 1, act)
                        act.wait_ge(projected, j + 1)
                        bk = PS[:, j % 2, :]
                        if j < jq:
                            ins = act.activation(glT, bk[0:24, :], ACT.Sigmoid)
                        elif j < jv:
                            d = (lambda h: q[0:64, 2 * (j - jq) + h, :]) if j < jk else (lambda h: kk[0:64, j - jk, h, :])
                            act.copy(d(0), bk[0:64, :])
                            ins = act.copy(d(1), bk[64:128, :])
                        else:
                            ins = act.copy(v[:, j - jv, :], bk[:, 0:256])
                        ins.then_inc(evacuated, 1)

                    for j in range(jl, jk):
                        evacuate_heads(j)
                    for i in range(NT):
                        act.wait_ge(s_cd, i + 1)
                        act.activation(pc[:, i, :], pc[:, i, :], ACT.Exp, scale=HD ** -0.5).then_inc(s_ce, 1)
                    for j in range(jk, je):
                        evacuate_heads(j)
                        if j >= jv:
                            i = j - jv
                            act.wait_ge(s_ct, i + 1)
                            act.copy(pct[:, i, :], PS[:, 6 + i % 2, 0:256]).then_inc(s_ctc, 1)
                    proj.after(je - 1, act)
                    for a in att:
                        a.scalar(act)
                    for f in range(NT):
                        act.wait_ge(s_ot, f + 1)
                        act.copy(M[:, f, :], PS[:, 2 + f % 2, :]).then_inc(s_oe, 1)

                @block.vector
                def _(dve):
                    link = chain(dve, s_cv)
                    gates = gl.rearrange("p i (h w) -> p i h w", w=3)
                    dve.wait_ge(s_gt, 1)
                    dve.tensor_copy(gl, split3(PS[:, 7, 0:96], 4)).then_inc(s_gc, 1)
                    add = split3(const("cmpadd", C2, spec), 4)
                    keep = split3(const("cmpmul", C2, spec), 4)
                    for i in range(NT):
                        dve.wait_ge(s_cs, i + 1)
                        p3 = split3(pc[:, i, :], NH)
                        link(dve.tensor_tensor(p3, split3(PS[:, 4 + i % 2, 0:256], NH), repeat(add[:, i, :], NH), ALU.add))
                        link(dve.tensor_reduce(mx, p3, AX.X, ALU.max))
                        dve.tensor_tensor(p3, p3, spread(mx, 32), ALU.subtract).then_inc(s_cd, 1)
                        dve.wait_ge(s_cd, i + 1)
                    for i in range(NT):
                        dve.wait_ge(s_ce, i + 1)
                        p3 = split3(pc[:, i, :], NH)
                        link(dve.tensor_tensor(p3, p3, repeat(keep[:, i, :], NH), ALU.mult))
                        link(dve.tensor_reduce(den, p3, AX.X, ALU.add))
                        link(dve.tensor_scalar(den, den, 1e-30, None, ALU.max))
                        link(dve.reciprocal(den, den))
                        dve.tensor_tensor(p3, p3, spread(den, 32), ALU.mult).then_inc(s_cn, 1)
                        dve.wait_ge(s_cn, i + 1)
                    for i in range(NT):
                        dve.wait_ge(s_co, i + 1)
                        dve.wait_ge(s_gc, 1)
                        dve.tensor_tensor(split3(otok[:, i, :], NH), split3(PS[:, 2 + i % 2, :], NH),
                                          spread(gates[:, i, :, 0], HD), ALU.mult).then_inc(s_cf, 1)

                    def finish_of(w):
                        a = att[w]

                        def finish(i):
                            dve.wait_ge(a.weighted, NH * (i + 1))
                            dve.wait_ge(a.prob, NH * (i + 1))
                            link(dve.reciprocal(coef, a.rs[:, NH * i:NH * (i + 1)]))
                            link(dve.tensor_tensor(coef, coef, gates[:, i, :, w + 1], ALU.mult))
                            dve.tensor_tensor(split3(tmp, NH), split3(PS[:, i % 2, :], NH), spread(coef, HD),
                                              ALU.mult).then_inc(a.taken, 1)
                            dve.wait_ge(a.taken, i + 1)
                            link(dve.tensor_tensor(otok[:, i, :], otok[:, i, :], tmp, ALU.add))
                        return finish

                    dve.wait_ge(s_cf, NT)
                    for w in range(2):
                        att[w].vector(dve, finish_of(w))
                    dve.sem_inc(s_os, 1)

            s_mh, s_ml = sem("mix_rounded"), sem("mix_split")
            ar = Arena("mix_output", 3 * T)
            with nc.Block() as block:
                sq, acc = split3(ar.take(2 * T), 2), ar.take(T)
                ln = LayerNorm("mix_norm", sq, acc, evacuated, J["out"], p2("ln_g")[:, 8:16], p2("ln_b")[:, 8:16])

                @block.sync
                def _(sp):
                    stream.send(sp, RAW, len(stream.units))
                    sp.wait_ge(stream.low, len(stream.units))
                    after.sync(sp)

                @block.gpsimd
                def _(pool):
                    stream.lower(pool, RAW, WP, len(stream.units))
                    after.gpsimd(pool)

                @block.tensor
                def _(pe):
                    for j in range(J["out"], J["out"] + KD):
                        proj.run(pe, j, tokens, s_ml if j == J["out"] else None)
                    ln.tensor(pe)

                @block.scalar
                def _(act):
                    for k in range(KD):
                        act.copy(XS[:, 0, k, :], M[:, k, :]).then_inc(s_mh, 1)
                    for j in range(J["out"], J["out"] + KD):
                        proj.after(j, act)
                    act.wait_ge(projected, J["out"] + KD)
                    after.scalar(act)
                    ln.scalar(act)

                @block.vector
                def _(dve):
                    for k in range(KD):
                        dve.wait_ge(s_mh, k + 1)
                        dve.tensor_tensor(XS[:, 1, k, :], M[:, k, :], XS[:, 0, k, :].bitcast(F32),
                                          ALU.subtract).then_inc(s_ml, 1)
                    ln.begin(dve)
                    for m in range(KD):
                        j = J["out"] + m
                        dve.wait_ge(projected, j + 1)
                        dve.scalar_tensor_tensor(X[:, m, :], X[:, m, :], ALPHA, PS[:, j % 2, :],
                                                 ALU.mult, ALU.add).then_inc(evacuated, 1)
                        ln.accumulate(dve, X[:, m, :], m)
                    dve.wait_ge(evacuated, J["out"] + KD)
                    ln.vector(dve)
            phase[0].close()
            mixing.close()
            return ln

        def second_layer(l):
            s_par = sem("parameters2_loaded")
            first_of = lambda u: dr["w_gu"][bass.ds(l * (2 * KF) + u, 1)].rearrange("a p n -> (a p) n")
            streams = mixer_streams(l)
            norm = feed_forward(l, 0, s_par, MixerAhead(streams[0]))
            norm = mix_tokens(l, streams, Ahead("ffn1_first_unit", first_of(KF)), norm)
            feed_forward(l, 1, s_par, Ahead("ffn0_first_unit", first_of(2 * KF)), norm)

        layers(second_layer)
        phase[0].close()

        s_out = sem("output_stored")
        with nc.Block() as block:
            @block.sync
            def _(sp):
                sp.dma_start(out, x_all[:, :]).then_inc(s_out, 16)
                sp.wait_ge(s_out, 16)


def constants():
    f = np.float32
    i = np.arange(P)
    c0 = np.zeros((P, C0N), f)
    c0[:, 0:128] = np.eye(P)
    c0[:, 128:256] = 1.0
    c0[:, 256:384] = i[:, None] <= i[None, :]
    c0[:, 768:896] = np.where(i[None, :] > i[:, None], -BIG, 0.0)
    c0[:, 896] = (10000.0 ** (-(i % 64) / 64.0)).astype(f)
    c0[:, 897] = np.where(i < 64, -1.0, 1.0)
    c1 = np.zeros((P, C1N), f)
    lg = np.log(1.0 - 2.0 ** (-5.0 - np.arange(RH)))
    diff = i[None, :] - i[:, None]
    for h in range(RH):
        c1[:, h * P:(h + 1) * P] = np.where(diff >= 0, np.exp(lg[h] * np.maximum(diff, 0)), 0.0) * P ** -0.5
        c1[:, 512 + h * P:512 + (h + 1) * P] = np.exp(lg[h] * (i + 1.0))[None, :]
        c1[:, 1024 + h] = np.exp(lg[h] * (P - 1.0 - i)) * P ** -0.5
    c2 = np.zeros((P, C2N), f)
    t = np.arange(T)
    c2[:, 0:512] = (t % GC != 0)
    for n, w in enumerate((2, 4, 8, 16)):
        a, r = divmod(n, 2)
        c2[64 * r:64 * r + 64, 512 + a * T:512 + (a + 1) * T] = 1.0 / np.minimum(w, t + 1)
    for q in range(NT):
        ok = (np.arange(32)[None, :] * CS + CB - 1 <= (q * P + i)[:, None]) & (np.arange(32) < NCMP)[None, :]
        c2[:, 1536 + 32 * q:1568 + 32 * q] = np.where(ok, 0.0, -BIG)
        c2[:, 1664 + 32 * q:1696 + 32 * q] = ok
    c2[:, 1792:2048] = np.tile((np.arange(GC)[None, :] >= i[:, None]), (1, 4))
    sel = np.zeros((SH, SH * P), f)
    for h in range(SH):
        sel[h, h * P:(h + 1) * P] = 1.0
    aug_q, aug_k = np.zeros((40, FH, T), f), np.zeros((40, FH, T), f)
    for h in range(FH):
        aug_q[h, h] = -(FD ** 0.5)
        aug_k[32 + h, h] = 1.0
    return dict(c0=c0, c1=c1, c2=c2, sel=sel, aug_q=aug_q.reshape(40, -1), aug_k=aug_k.reshape(40, -1))


def layout(a):
    def units(w, cols, n):
        L, K, _ = w.shape
        w = w[:, :, cols].reshape(L, K // P, P, len(cols) // n, n)
        return np.ascontiguousarray(w.transpose(0, 3, 2, 1, 4)).reshape(L, len(cols) // n, P, -1)

    def padded(w, cols):
        w = np.concatenate([w[:, :, cols], np.zeros((DEPTH, D, P - len(cols)), np.float32)], axis=2)
        return units(w, np.arange(P), P)[:, 0]

    def column(v):
        return np.moveaxis(v.reshape(v.shape[:-1] + (-1, P)), -1, -2)

    def rows(v):
        return np.broadcast_to(v[:, None, :], (DEPTH, P, v.shape[-1]))

    r = lambda o, n: np.arange(o, o + n)
    off = np.cumsum([0, 512, 512, 512, 512, 1536, 16, 1024, 512, 512, 512, 512, 8])
    rq, rk, rv, rg, xbc, dt, z, fq, fk, fv, fg, fr = off[:12]
    cols = np.concatenate([r(rq, 512), r(rk, 512), r(rg, 512), r(rv, 512), r(xbc + 1024, 512), r(xbc, 1024),
                           r(z, 1024), r(fq, 512), r(fk, 512), r(fv, 512), r(fg, 512)])
    ada = units(a["w_ada"], r(0, 3072), UC).reshape(DEPTH * 12, P, UNIT)
    d = dict(w_ada=np.concatenate([ada, np.zeros((8, P, UNIT), np.float32)]), w_in=units(a["w_in"], cols, UC),
             w_dtf=padded(a["w_in"], np.concatenate([r(dt, 16), r(fr, 8)])),
             w_out=units(a["w_out"], r(0, D), P))
    conv = np.concatenate([column(a["conv_w"][:, k]) for k in range(CONV_K)], axis=2)
    d["par1"] = np.concatenate([column(a["norm_g"]), column(a["b_ada"]), conv, column(a["conv_b"]),
                                column(a["ssd_norm_g"]), rows(a["dt_bias"]), rows(a["b_forget"]),
                                rows(a["a_log"]), rows(a["d_skip"])], axis=2)
    d["final_g"] = column(a["final_g"])
    d["c"] = column(a["c"])[0]
    d["pos"] = np.broadcast_to(a["positions"], (P, T))
    d["x"] = a["x"][0].T.reshape(KD, P, T).transpose(1, 0, 2).reshape(P, KD * T)
    off = np.cumsum([0, 512, 128, 128, 128, 128, 128, 128, 24, 256, 128, 128, 256, 16, 256])
    nq, kc, vc, ks, vs, kw, vw, gl, u, gq, gk, gv, ga, gr = off[:14]
    cols = np.concatenate([r(nq, 512), r(kc, 256), r(ks, 128), r(kw, 128), r(u, 256), r(gq, 256), r(gr, 256),
                           r(vs, 128), r(vw, 128), r(gv, 256)])
    w = a["w_in_2"]
    d["w_in2"] = units(w, cols, UC)
    d["w_ga"] = padded(w, r(ga, 16))
    d["w_gl"] = padded(w, r(gl, 24))
    d["w_out2"] = units(a["w_out_2"], r(0, D), UC)
    wg, wu = (a[n].reshape(2 * DEPTH, D, FF) for n in ("ffn_wg_2", "ffn_wu_2"))
    gu = np.stack([units(wg, r(0, FF), P), units(wu, r(0, FF), P)], axis=3)
    d["w_gu"] = np.concatenate([gu.reshape(2 * DEPTH * KF, P, 2 * D), np.zeros((1, P, 2 * D), np.float32)])
    d["w_d"] = units(a["ffn_wd_2"].reshape(2 * DEPTH, FF, D), r(0, D), P).reshape(DEPTH, 2, KD, P, FF)
    d["w_c1"] = a["cmp_w1_2"].reshape(DEPTH, 2, CB, HD, HD).transpose(0, 3, 1, 2, 4).reshape(DEPTH, HD, -1)
    s = np.zeros((DEPTH, P, 576), np.float32)
    s[:, 0:64, 0:128] = a["cmp_w2_2"].transpose(0, 2, 1, 3).reshape(DEPTH, 64, 128)
    s[:, 0:64, 128:192] = a["cmp_pe_2"].transpose(0, 3, 1, 2).reshape(DEPTH, 64, 64)
    for n in range(4):
        t, q = divmod(n, 2)
        s[:, 64 * q:64 * q + 64, 192 + P * t + 64 * q:192 + P * t + 64 * q + 64] = a["pool_w_2"][:, n]
    s[:, 0:16, 448:576] = a["gla_wa2_2"]
    d["w_small"] = s
    ln_g, ln_b = (column(a[n]).transpose(0, 2, 1, 3).reshape(DEPTH, P, 24) for n in ("ln_g_2", "ln_b_2"))
    d["par2"] = np.concatenate([ln_g, ln_b, column(a["pool_scale_2"]), column(a["gla_ba_2"]),
                                column(a["gla_norm_g_2"])], axis=2)
    return {k: np.ascontiguousarray(v) for k, v in d.items()}


def kernel(**inputs):
    import concourse.bacc as bacc
    from concourse.bass_utils import run_bass_kernel_spmd

    arrays = layout({k: np.asarray(v) for k, v in inputs.items()})
    arrays.update(constants())
    nc = bacc.Bacc("TRN2", target_bir_lowering=False, num_devices=1)
    dr = {k: nc.dram_tensor(f"in_{k}", v.shape, mybir.dt.from_np(v.dtype), kind="ExternalInput").ap()
          for k, v in arrays.items()}
    out = nc.dram_tensor("out", (P, KD * T), F32, kind="ExternalOutput").ap()
    build(nc, dr, out)
    r = run_bass_kernel_spmd(nc, [{f"in_{k}": v for k, v in arrays.items()}], core_ids=[0])
    o = r.results[0]["out"].reshape(P, KD, T).transpose(2, 1, 0).reshape(1, T, D)
    return np.ascontiguousarray(o)
```
